# Optimizing a Trainium2 kernel written in Bass

```python
import jax
import jax.numpy as jnp
from jax import lax
import numpy as np

D_MODEL = 1024
BATCH = 1
SEQ = 128
DEPTH = 2
DEC_BATCH = 1
DEC_SEQ = 128
PAST_LEN = 128

GRID_W = 64
NORM_EPS = 1e-6

MLA_HEADS = 4
MLA_NOPE = 128
MLA_ROPE = 64
MLA_V = 128
Q_LORA = 384
KV_LORA = 256
ROPE_BASE = 10000.0
MLA_SCALE = (MLA_NOPE + MLA_ROPE) ** -0.5
Q_BLOCK = 128

GDN_HEADS = 4
GDN_DK = 64
GDN_DV = 64
GDN_CONV = 3
GDN_CHUNK = 64

RWKV_HEADS = 4
RWKV_N = 64
RWKV_W_LORA = 64
RWKV_A_LORA = 64
RWKV_G_LORA = 128
RWKV_GN_EPS = 64e-5

N_EXPERTS = 64
TOP_K = 8
N_GROUPS = 8
TOPK_GROUPS = 4
D_EXPERT = 256
D_SHARED = 256
ROUTE_SCALE = 2.5
MOE_BLOCK = 128

MLA_W = MLA_HEADS * MLA_V
GDN_QK = GDN_HEADS * GDN_DK
GDN_W = GDN_HEADS * GDN_DV
RWKV_W = RWKV_HEADS * RWKV_N
MIX_W = MLA_W + GDN_W + RWKV_W
GDN_CONV_CH = 2 * GDN_QK + GDN_W
P_MLA = Q_LORA + KV_LORA + MLA_ROPE
P_GDN = GDN_CONV_CH + GDN_W + 4 * GDN_HEADS
P_RWKV = 3 * RWKV_W + 2 * RWKV_W_LORA + 2 * RWKV_A_LORA + RWKV_G_LORA
P_IN = P_MLA + P_GDN + P_RWKV

kernel_name = 'hybrid_mla_gdn_rwkv7_moe_diffusion_step'

def rmsnorm(x, g):
    xf = x.astype(jnp.float32)
    y = xf * lax.rsqrt(jnp.mean(xf * xf, axis=-1, keepdims=True) + NORM_EPS)
    return (y * g.astype(jnp.float32)).astype(x.dtype)

def l2norm(x):
    xf = x.astype(jnp.float32)
    return xf * lax.rsqrt(jnp.sum(xf * xf, axis=-1, keepdims=True) + 1e-6)

def adaln(cvec, w, b):
    m = jnp.einsum('bd,de->be', jax.nn.silu(cvec), w) + b
    return jnp.split(m[:, None, :], 6, axis=-1)

def swiglu(x, w_gu, w_down):
    gt, up = jnp.split(x @ w_gu, 2, axis=-1)
    return (jax.nn.silu(gt) * up) @ w_down

def rope_2d_tables(n):
    rows = n // GRID_W
    row = jnp.repeat(jnp.arange(rows, dtype=jnp.float32), GRID_W)
    col = jnp.tile(jnp.arange(GRID_W, dtype=jnp.float32), rows)
    axis_dim = MLA_ROPE // 2
    inv = jnp.power(ROPE_BASE, -jnp.arange(0, axis_dim, 2, dtype=jnp.float32) / axis_dim)
    ang_r = row[:, None] * inv
    ang_c = col[:, None] * inv
    return (jnp.cos(ang_r), jnp.sin(ang_r), jnp.cos(ang_c), jnp.sin(ang_c))

def _rotate(x, cos, sin):
    h = x.shape[-1] // 2
    x1, x2 = x[..., :h], x[..., h:]
    return jnp.concatenate([x1 * cos - x2 * sin, x1 * sin + x2 * cos], axis=-1)

def rope_2d(x, tables):
    cr, sr, cc, sc = (t.astype(x.dtype) for t in tables)
    h = x.shape[-1] // 2
    return jnp.concatenate([_rotate(x[..., :h], cr, sr), _rotate(x[..., h:], cc, sc)], axis=-1)

def mla_expand(ckv, w_ukv):
    B, T, _ = ckv.shape
    kv = jnp.einsum('btc,cf->btf', ckv, w_ukv).reshape(B, T, MLA_HEADS, MLA_NOPE + MLA_V)
    return kv[..., :MLA_NOPE], kv[..., MLA_NOPE:]

def mla_attend(q_nope, q_pe, k_nope, k_pe, v):
    B, Tq, H, _ = q_nope.shape
    nb = Tq // Q_BLOCK

    def blocks(t):
        return jnp.moveaxis(t.reshape((B, nb, Q_BLOCK) + t.shape[2:]), 1, 0)

    def one_block(qs):
        qn, qp = qs
        s = jnp.einsum('bqhd,bkhd->bhqk', qn, k_nope) + jnp.einsum('bqhr,bkr->bhqk', qp, k_pe)
        p = jax.nn.softmax(s.astype(jnp.float32) * MLA_SCALE, axis=-1).astype(v.dtype)
        return jnp.einsum('bhqk,bkhd->bqhd', p, v)

    o = lax.map(one_block, (blocks(q_nope), blocks(q_pe)))
    return jnp.moveaxis(o, 0, 1).reshape(B, Tq, H * MLA_V)

def short_conv(z, w):
    T = z.shape[1]
    pad = GDN_CONV // 2
    zp = jnp.pad(z, ((0, 0), (pad, pad), (0, 0)))
    out = zp[:, 0:T] * w[0]
    for j in range(1, GDN_CONV):
        out = out + zp[:, j:j + T] * w[j]
    return out

def token_shift(z, mu_prev, mu_next):
    zp = jnp.pad(z, ((0, 0), (1, 0), (0, 0)))[:, :-1]
    zn = jnp.pad(z, ((0, 0), (0, 1), (0, 0)))[:, 1:]
    return z + mu_prev * (zp - z) + mu_next * (zn - z)

def chunk_gated_delta(q, k, v, g, beta, s0):
    B, T, H, K = q.shape
    V = v.shape[-1]
    C = GDN_CHUNK
    N = T // C
    f32 = jnp.float32

    def blocks(x):
        x = x.astype(f32).reshape((B, N, C, H) + x.shape[3:])
        return jnp.moveaxis(x, (1, 3), (0, 2))

    qc, kc, vc, gc, bc = blocks(q), blocks(k), blocks(v), blocks(g), blocks(beta)
    gcum = jnp.cumsum(gc, axis=-1)
    diff = gcum[..., :, None] - gcum[..., None, :]
    causal = jnp.tril(jnp.ones((C, C), bool))
    decay = jnp.where(causal, jnp.exp(jnp.where(causal, diff, 0.0)), 0.0)
    strict = jnp.tril(jnp.ones((C, C), f32), -1)
    kb = kc * bc[..., None]
    a_mat = jnp.einsum('nbhik,nbhjk->nbhij', kb, kc) * decay * strict
    rhs = jnp.concatenate([vc * bc[..., None], kb * jnp.exp(gcum)[..., None]], axis=-1)
    sol = lax.linalg.triangular_solve(a_mat + jnp.eye(C, dtype=f32), rhs, left_side=True,
                                      lower=True, unit_diagonal=True)
    u, w = sol[..., :V], sol[..., V:]
    qk = jnp.einsum('nbhik,nbhjk->nbhij', qc, kc) * decay
    g_last = gcum[..., -1]

    def step(S, xs):
        q_n, k_n, u_n, w_n, qk_n, gc_n, gl_n = xs
        v_new = u_n - jnp.einsum('bhck,bhkv->bhcv', w_n, S)
        o = (jnp.einsum('bhck,bhkv->bhcv', q_n * jnp.exp(gc_n)[..., None], S)
             + jnp.einsum('bhij,bhjv->bhiv', qk_n, v_new))
        k_dec = k_n * jnp.exp(gl_n[..., None] - gc_n)[..., None]
        S = S * jnp.exp(gl_n)[..., None, None] + jnp.einsum('bhck,bhcv->bhkv', k_dec, v_new)
        return S, o

    S, o = lax.scan(step, s0.astype(f32), (qc, kc, u, w, qk, gcum, g_last))
    o = jnp.moveaxis(o, (0, 2), (1, 3)).reshape(B, T, H, V)
    return o, S

def gdn_mixer(zg, lp, s0):
    B, T, _ = zg.shape
    f32 = jnp.float32
    qkv = jax.nn.silu(short_conv(zg[..., :GDN_CONV_CH], lp['gdn_conv']))
    q = l2norm(qkv[..., :GDN_QK].reshape(B, T, GDN_HEADS, GDN_DK)) * (GDN_DK ** -0.5)
    k = l2norm(qkv[..., GDN_QK:2 * GDN_QK].reshape(B, T, GDN_HEADS, GDN_DK))
    v = qkv[..., 2 * GDN_QK:].reshape(B, T, GDN_HEADS, GDN_DV).astype(f32)
    gate = zg[..., GDN_CONV_CH:GDN_CONV_CH + GDN_W].reshape(B, T, GDN_HEADS, GDN_DV)
    off = GDN_CONV_CH + GDN_W
    a = zg[..., off:off + 2 * GDN_HEADS].reshape(B, T, 2, GDN_HEADS).astype(f32)
    b = zg[..., off + 2 * GDN_HEADS:].reshape(B, T, 2, GDN_HEADS).astype(f32)
    g = -jnp.exp(lp['gdn_a_log'].astype(f32)) * jax.nn.softplus(a + lp['gdn_dt_bias'].astype(f32))
    beta = jax.nn.sigmoid(b)
    fl = lambda t: jnp.flip(t, axis=1)
    o_f, s_f = chunk_gated_delta(q, k, v, g[:, :, 0], beta[:, :, 0], s0[:, 0])
    o_b, s_b = chunk_gated_delta(fl(q), fl(k), fl(v), fl(g[:, :, 1]), fl(beta[:, :, 1]), s0[:, 1])
    o = (o_f + fl(o_b)).astype(zg.dtype)
    o = rmsnorm(o, lp['gdn_norm']) * jax.nn.silu(gate)
    return o.reshape(B, T, GDN_W), jnp.stack([s_f, s_b], axis=1)

def rwkv_direction(r, w, k, v, kk, a, s0):
    def step(S, xs):
        r_t, w_t, k_t, v_t, kk_t, a_t = xs
        sa = jnp.einsum('bhvk,bhk->bhv', S, -kk_t)
        S = (S * w_t[:, :, None, :] + sa[..., None] * (kk_t * a_t)[:, :, None, :]
             + v_t[..., None] * k_t[:, :, None, :])
        return S, jnp.einsum('bhvk,bhk->bhv', S, r_t)

    tm = lambda t: jnp.moveaxis(t, 1, 0)
    S, o = lax.scan(step, s0.astype(jnp.float32), (tm(r), tm(w), tm(k), tm(v), tm(kk), tm(a)))
    return jnp.moveaxis(o, 0, 1), S

def rwkv_mixer(zr, lp, s0):
    B, T, _ = zr.shape
    f32 = jnp.float32
    zr = token_shift(zr, lp['rwkv_mu_prev'], lp['rwkv_mu_next'])
    heads = lambda t: t.reshape(B, T, RWKV_HEADS, RWKV_N)
    fl = lambda t: jnp.flip(t, axis=1)
    r = heads(zr[..., :RWKV_W]).astype(f32)
    k = zr[..., RWKV_W:2 * RWKV_W].astype(f32)
    v = heads(zr[..., 2 * RWKV_W:3 * RWKV_W]).astype(f32)
    o1 = 3 * RWKV_W
    o2 = o1 + 2 * RWKV_W_LORA
    o3 = o2 + 2 * RWKV_A_LORA
    wd = zr[..., o1:o2].reshape(B, T, 2, RWKV_W_LORA)
    ad = zr[..., o2:o3].reshape(B, T, 2, RWKV_A_LORA)
    gd = zr[..., o3:]
    w_pre = lp['rwkv_w0'] + jnp.einsum('btdr,drc->btdc', jnp.tanh(wd), lp['rwkv_w2'])
    w_log = -jax.nn.softplus(-w_pre.astype(f32)) - 0.5
    decay = jnp.exp(-jnp.exp(w_log))
    a = jax.nn.sigmoid((lp['rwkv_a0'] + jnp.einsum('btdr,drc->btdc', ad, lp['rwkv_a2'])).astype(f32))
    gate = jnp.einsum('btr,rc->btc', jax.nn.sigmoid(gd), lp['rwkv_g2']).astype(f32)
    kk = l2norm(heads(k * lp['rwkv_k_k'].astype(f32)))
    k_a = lp['rwkv_k_a'].astype(f32)
    r_k = lp['rwkv_r_k'].astype(f32)

    def direction(d):
        a_flat = a[:, :, d]
        k_d = heads(k * (1.0 + (a_flat - 1.0) * k_a))
        a_d = heads(a_flat)
        w_d = heads(decay[:, :, d])
        bonus = jnp.sum(r * k_d * r_k, axis=-1, keepdims=True) * v
        seqs = (r, w_d, k_d, v, kk, a_d)
        if d == 1:
            seqs = tuple(fl(t) for t in seqs)
        o_d, s_d = rwkv_direction(*seqs, s0[:, d])
        if d == 1:
            o_d = fl(o_d)
        return o_d, bonus, s_d

    o_f, bonus_f, s_f = direction(0)
    o_b, bonus_b, s_b = direction(1)
    o = o_f + o_b
    mu = jnp.mean(o, axis=-1, keepdims=True)
    var = jnp.mean((o - mu) ** 2, axis=-1, keepdims=True)
    o = ((o - mu) * lax.rsqrt(var + RWKV_GN_EPS) * lp['rwkv_gn_w'].astype(f32).reshape(RWKV_HEADS, RWKV_N)
         + lp['rwkv_gn_b'].astype(f32).reshape(RWKV_HEADS, RWKV_N))
    out = (o + bonus_f + bonus_b) * heads(gate)
    return out.reshape(B, T, RWKV_W).astype(zr.dtype), jnp.stack([s_f, s_b], axis=1)

def token_mixers(h, lp, cache):
    B, T, _ = h.shape
    z = jnp.einsum('btd,dp->btp', h, lp['w_in'])
    zm, zg, zr = z[..., :P_MLA], z[..., P_MLA:P_MLA + P_GDN], z[..., P_MLA + P_GDN:]
    cq = rmsnorm(zm[..., :Q_LORA], lp['mla_q_norm'])
    q = jnp.einsum('btc,cf->btf', cq, lp['mla_w_uq']).reshape(B, T, MLA_HEADS, MLA_NOPE + MLA_ROPE)
    q_nope, q_pe = q[..., :MLA_NOPE], q[..., MLA_NOPE:]
    ckv = rmsnorm(zm[..., Q_LORA:Q_LORA + KV_LORA], lp['mla_kv_norm'])
    k_pe = zm[..., Q_LORA + KV_LORA:]
    k_nope, v = mla_expand(ckv, lp['mla_w_ukv'])
    if cache is None:
        s0_gdn = jnp.zeros((B, 2, GDN_HEADS, GDN_DK, GDN_DV), jnp.float32)
        s0_rwkv = jnp.zeros((B, 2, RWKV_HEADS, RWKV_N, RWKV_N), jnp.float32)
        k_pe_all = k_pe
    else:
        ckv_ctx, kpe_ctx, s0_gdn, s0_rwkv = cache
        tabs = rope_2d_tables(T)
        q_pe = rope_2d(q_pe, tuple(t[:, None, :] for t in tabs))
        kn_ctx, v_ctx = mla_expand(ckv_ctx, lp['mla_w_ukv'])
        k_nope = jnp.concatenate([kn_ctx, k_nope], axis=1)
        v = jnp.concatenate([v_ctx, v], axis=1)
        k_pe_all = jnp.concatenate([kpe_ctx, rope_2d(k_pe, tabs)], axis=1)
    o_mla = mla_attend(q_nope, q_pe, k_nope, k_pe_all, v)
    o_gdn, s_gdn = gdn_mixer(zg, lp, s0_gdn)
    o_rwkv, s_rwkv = rwkv_mixer(zr, lp, s0_rwkv)
    mixed = jnp.concatenate([o_mla, o_gdn, o_rwkv], axis=-1)
    out = jnp.einsum('btm,md->btd', mixed, lp['w_out'])
    return out, (ckv, k_pe, s_gdn, s_rwkv)

def routed_experts(x, eidx, ew, w_gu, w_down):
    n, D = x.shape
    m = n * TOP_K
    flat_e = eidx.reshape(m)
    order = jnp.argsort(flat_e)
    e_sorted = flat_e[order]
    tok = (order // TOP_K).astype(jnp.int32)
    counts = jnp.bincount(flat_e, length=N_EXPERTS)
    padded = (counts + MOE_BLOCK - 1) // MOE_BLOCK * MOE_BLOCK
    pad_end = jnp.cumsum(padded)
    pad_start = pad_end - padded
    start = jnp.cumsum(counts) - counts
    dest = pad_start[e_sorted] + jnp.arange(m) - start[e_sorted]
    n_blocks = m // MOE_BLOCK + N_EXPERTS
    rows = n_blocks * MOE_BLOCK
    row_tok = jnp.zeros((rows,), jnp.int32).at[dest].set(tok)
    row_w = jnp.zeros((rows,), x.dtype).at[dest].set(ew.reshape(m)[order].astype(x.dtype))
    block_e = jnp.minimum(jnp.searchsorted(pad_end, jnp.arange(n_blocks) * MOE_BLOCK, side='right'),
                          N_EXPERTS - 1)

    def expert_block(args):
        tok_b, e = args
        return swiglu(x[tok_b], w_gu[e], w_down[e])

    y = lax.map(expert_block, (row_tok.reshape(n_blocks, MOE_BLOCK), block_e)).reshape(rows, D)
    return jnp.zeros_like(x).at[row_tok].add(y * row_w[:, None])

def moe_ffn(h, lp):
    B, T, D = h.shape
    x = h.reshape(B * T, D)
    n = x.shape[0]
    scores = jax.nn.sigmoid(jnp.einsum('nd,de->ne', x, lp['moe_router']).astype(jnp.float32))
    sel = scores + lp['moe_bias'].astype(jnp.float32)
    grp = jnp.sum(lax.top_k(sel.reshape(n, N_GROUPS, N_EXPERTS // N_GROUPS), 2)[0], axis=-1)
    _, gidx = lax.top_k(grp, TOPK_GROUPS)
    gmask = jnp.sum(jax.nn.one_hot(gidx, N_GROUPS, dtype=jnp.float32), axis=1) > 0
    emask = jnp.repeat(gmask, N_EXPERTS // N_GROUPS, axis=1)
    _, eidx = lax.top_k(jnp.where(emask, sel, -jnp.inf), TOP_K)
    ew = jnp.take_along_axis(scores, eidx, axis=1)
    ew = ew / jnp.sum(ew, axis=-1, keepdims=True) * ROUTE_SCALE
    routed = routed_experts(x, eidx, ew, lp['moe_w_gu'], lp['moe_w_down'])
    shared = swiglu(x, lp['shared_w_gu'], lp['shared_w_down'])
    return (routed + shared).reshape(B, T, D)

def trunk_layer(x, mods, lp, cache):
    sh1, sc1, g1, sh2, sc2, g2 = mods
    h = rmsnorm(x, lp['norm1']) * (1.0 + sc1) + sh1
    mix, ctx_tensors = token_mixers(h, lp, cache)
    x = x + g1 * mix
    h = rmsnorm(x, lp['norm2']) * (1.0 + sc2) + sh2
    x = x + g2 * moe_ffn(h, lp)
    return x, ctx_tensors

def setup_inputs(seed: int = 0) -> dict:
    key = jax.random.key(seed)
    ks = jax.random.split(key, 48)
    ctr = [0]

    def nxt():
        k = ks[ctr[0]]
        ctr[0] += 1
        return k

    def nrm(shape, scale):
        return jax.random.normal(nxt(), shape, jnp.float32) * scale

    def unif(shape, lo, hi):
        return jax.random.uniform(nxt(), shape, jnp.float32, lo, hi)

    def gain(shape):
        return 1.0 + nrm(shape, 0.02)

    D = D_MODEL
    return {
        'x_prompt': nrm((BATCH, SEQ, D), 1.0),
        'x_sample': nrm((DEC_BATCH, DEC_SEQ, D), 1.0),
        'cache_mla_ckv': nrm((DEC_BATCH, DEPTH, PAST_LEN, KV_LORA), 1.0),
        'cache_mla_kpe': nrm((DEC_BATCH, DEPTH, PAST_LEN, MLA_ROPE), 1.0),
        'state_gdn': nrm((DEC_BATCH, DEPTH, 2, GDN_HEADS, GDN_DK, GDN_DV), 0.3),
        'state_rwkv': nrm((DEC_BATCH, DEPTH, 2, RWKV_HEADS, RWKV_N, RWKV_N), 0.3),
        'c': nrm((DEC_BATCH, D), 1.0),
        'c_ctx': nrm((D,), 1.0),
        'ada_w': nrm((DEPTH, D, 6 * D), 0.5 * D ** -0.5),
        'ada_b': nrm((DEPTH, 6 * D), 0.02),
        'norm1': gain((DEPTH, D)),
        'w_in': nrm((DEPTH, D, P_IN), D ** -0.5),
        'mla_q_norm': gain((DEPTH, Q_LORA)),
        'mla_w_uq': nrm((DEPTH, Q_LORA, MLA_HEADS * (MLA_NOPE + MLA_ROPE)), Q_LORA ** -0.5),
        'mla_kv_norm': gain((DEPTH, KV_LORA)),
        'mla_w_ukv': nrm((DEPTH, KV_LORA, MLA_HEADS * (MLA_NOPE + MLA_V)), KV_LORA ** -0.5),
        'gdn_conv': nrm((DEPTH, GDN_CONV, GDN_CONV_CH), GDN_CONV ** -0.5),
        'gdn_a_log': jnp.log(unif((DEPTH, 2, GDN_HEADS), 1.0, 16.0)),
        'gdn_dt_bias': unif((DEPTH, 2, GDN_HEADS), -4.5, -2.5),
        'gdn_norm': gain((DEPTH, GDN_DV)),
        'rwkv_mu_prev': unif((DEPTH, P_RWKV), 0.0, 0.5),
        'rwkv_mu_next': unif((DEPTH, P_RWKV), 0.0, 0.5),
        'rwkv_w0': unif((DEPTH, 2, RWKV_W), -6.0, 1.0),
        'rwkv_w2': nrm((DEPTH, 2, RWKV_W_LORA, RWKV_W), RWKV_W_LORA ** -0.5),
        'rwkv_a0': nrm((DEPTH, 2, RWKV_W), 0.5),
        'rwkv_a2': nrm((DEPTH, 2, RWKV_A_LORA, RWKV_W), RWKV_A_LORA ** -0.5),
        'rwkv_g2': nrm((DEPTH, RWKV_G_LORA, RWKV_W), RWKV_G_LORA ** -0.5),
        'rwkv_k_k': 0.85 + nrm((DEPTH, RWKV_W), 0.02),
        'rwkv_k_a': gain((DEPTH, RWKV_W)),
        'rwkv_r_k': nrm((DEPTH, RWKV_HEADS, RWKV_N), 0.1),
        'rwkv_gn_w': gain((DEPTH, RWKV_W)),
        'rwkv_gn_b': nrm((DEPTH, RWKV_W), 0.02),
        'w_out': nrm((DEPTH, MIX_W, D), MIX_W ** -0.5),
        'norm2': gain((DEPTH, D)),
        'moe_router': nrm((DEPTH, D, N_EXPERTS), D ** -0.5),
        'moe_bias': nrm((DEPTH, N_EXPERTS), 0.01),
        'moe_w_gu': nrm((DEPTH, N_EXPERTS, D, 2 * D_EXPERT), D ** -0.5),
        'moe_w_down': nrm((DEPTH, N_EXPERTS, D_EXPERT, D), D_EXPERT ** -0.5),
        'shared_w_gu': nrm((DEPTH, D, 2 * D_SHARED), D ** -0.5),
        'shared_w_down': nrm((DEPTH, D_SHARED, D), D_SHARED ** -0.5),
        'norm_f': gain((D,)),
    }

def reference(x_prompt, x_sample, cache_mla_ckv, cache_mla_kpe, state_gdn, state_rwkv, c, c_ctx,
              ada_w, ada_b, norm1, w_in, mla_q_norm, mla_w_uq, mla_kv_norm, mla_w_ukv,
              gdn_conv, gdn_a_log, gdn_dt_bias, gdn_norm,
              rwkv_mu_prev, rwkv_mu_next, rwkv_w0, rwkv_w2, rwkv_a0, rwkv_a2, rwkv_g2,
              rwkv_k_k, rwkv_k_a, rwkv_r_k, rwkv_gn_w, rwkv_gn_b,
              w_out, norm2, moe_router, moe_bias, moe_w_gu, moe_w_down, shared_w_gu, shared_w_down,
              norm_f):
    def layer_params(l):
        return {
            'norm1': norm1[l], 'w_in': w_in[l],
            'mla_q_norm': mla_q_norm[l], 'mla_w_uq': mla_w_uq[l],
            'mla_kv_norm': mla_kv_norm[l], 'mla_w_ukv': mla_w_ukv[l],
            'gdn_conv': gdn_conv[l], 'gdn_a_log': gdn_a_log[l], 'gdn_dt_bias': gdn_dt_bias[l],
            'gdn_norm': gdn_norm[l],
            'rwkv_mu_prev': rwkv_mu_prev[l], 'rwkv_mu_next': rwkv_mu_next[l],
            'rwkv_w0': rwkv_w0[l], 'rwkv_w2': rwkv_w2[l], 'rwkv_a0': rwkv_a0[l], 'rwkv_a2': rwkv_a2[l],
            'rwkv_g2': rwkv_g2[l], 'rwkv_k_k': rwkv_k_k[l], 'rwkv_k_a': rwkv_k_a[l],
            'rwkv_r_k': rwkv_r_k[l], 'rwkv_gn_w': rwkv_gn_w[l], 'rwkv_gn_b': rwkv_gn_b[l],
            'w_out': w_out[l], 'norm2': norm2[l],
            'moe_router': moe_router[l], 'moe_bias': moe_bias[l],
            'moe_w_gu': moe_w_gu[l], 'moe_w_down': moe_w_down[l],
            'shared_w_gu': shared_w_gu[l], 'shared_w_down': shared_w_down[l],
        }

    xp = x_prompt
    ckv_list, kpe_list, sg_list, sr_list = [], [], [], []
    for l in range(DEPTH):
        lp = layer_params(l)
        mods = adaln(c_ctx[None, :], ada_w[l], ada_b[l])
        xp, (ckv_l, kpe_l, sg_l, sr_l) = trunk_layer(xp, mods, lp, None)
        ckv_list.append(ckv_l)
        kpe_list.append(kpe_l)
        sg_list.append(sg_l)
        sr_list.append(sr_l)
    y_prompt = rmsnorm(xp, norm_f)

    xs = x_sample
    for l in range(DEPTH):
        lp = layer_params(l)
        mods = adaln(c, ada_w[l], ada_b[l])
        cache = (cache_mla_ckv[:, l], cache_mla_kpe[:, l], state_gdn[:, l], state_rwkv[:, l])
        xs, _ = trunk_layer(xs, mods, lp, cache)
    y_sample = rmsnorm(xs, norm_f)

    new_cache_mla_ckv = jnp.stack(ckv_list, axis=1)
    new_cache_mla_kpe = jnp.stack(kpe_list, axis=1)
    new_state_gdn = jnp.stack(sg_list, axis=1)
    new_state_rwkv = jnp.stack(sr_list, axis=1)
    return (y_prompt, y_sample, new_cache_mla_ckv, new_cache_mla_kpe, new_state_gdn, new_state_rwkv)


_drawn_inputs = setup_inputs


def setup_inputs(seed=0):
    import zlib

    import numpy as np

    out = dict(_drawn_inputs(seed))
    spreads = {}
    factors = {'mla_q_norm': 4.824,
     'mla_kv_norm': 2.953,
     'gdn_norm': 3.456,
     'rwkv_gn_w': 2.879,
     'rwkv_gn_b': 2.723,
     'cache_mla_kpe': 2.749}
    for name, (base, spread) in spreads.items():
        noise = np.random.default_rng([zlib.crc32(name.encode()), seed]).standard_normal(out[name].shape)
        drawn = base * np.exp(spread * noise) if base else spread * noise
        out[name] = jnp.asarray(drawn.astype(out[name].dtype))
    for name, factor in factors.items():
        out[name] = (out[name] * factor).astype(out[name].dtype)
    return out
```

```python
from contextlib import ExitStack

import numpy as np

import concourse.bass as bass
from concourse import mybir

F32 = mybir.dt.float32
ALU = mybir.AluOpType
ACT = mybir.ActivationFunctionType
AX = mybir.AxisListType.X

T = 128
D = 1024
KD = D // 128
LAYERS = 2
EPS = 1e-6

HEADS = 4
NOPE, ROPE, VDIM = 128, 64, 128
QL, KVL = 384, 256
MLA_SCALE = (NOPE + ROPE) ** -0.5
GRID_W = 64
ROPE_BASE = 10000.0

N = 64
GN_EPS = 64e-5
P_MLA = QL + KVL + ROPE
Z_G = P_MLA
Z_GATE = Z_G + 3 * HEADS * N
Z_AB = Z_GATE + HEADS * N
Z_R = Z_AB + 4 * HEADS
Z_K, Z_V = Z_R + 256, Z_R + 512
Z_WD, Z_AD, Z_GD = Z_R + 768, Z_R + 896, Z_R + 1024
P_IN = Z_R + 1152
ZC = 6
ZW = [512] * 5 + [P_IN - 2560]

EXPERTS = 64
FF = 256
ROUTE_SCALE = 2.5
BIG = 1e30

LEVELS = 7
CONV = 384
SHIFTED = [Z_G + CONV * c for c in range(2)] + [Z_R + CONV * c for c in range(3)]

CONSTS = {}
CW = 0
for _n, _w in [("ident", 128), ("ones", 128), ("tri0", 128), ("tri1", 128), ("strict0", 128), ("strict1", 128),
               ("cen0", 128), ("cen1", 128), ("prev", 128), ("next", 128), ("half0", 1), ("half1", 1),
               ("cos", 64), ("sin", 64), ("before", 64)] + \
              [(f"level{k}_{d}", 128) for k in range(LEVELS) for d in range(2)]:
    CONSTS[_n] = (CW, _w)
    CW += _w


def constants():
    p, f = np.arange(T)[:, None], np.arange(T)[None, :]
    c = {"ident": p == f, "ones": np.ones((T, T)), "tri0": p <= f, "tri1": p >= f, "strict0": p < f,
         "strict1": p > f, "cen0": (p <= f) * 1.0 - (p < T // 2), "cen1": (p >= f) * 1.0 - (p >= T // 2),
         "prev": p == f - 1, "next": p == f + 1, "half0": p < T // 2, "half1": p >= T // 2}
    half = ROPE // 2
    inv = ROPE_BASE ** (-np.arange(0, half, 2) / half)
    ang = np.stack([(p // GRID_W) * inv[None], (p % GRID_W) * inv[None]], 1)
    c["cos"] = np.stack([np.cos(ang)] * 2, 2).reshape(T, ROPE)
    c["sin"] = np.stack([-np.sin(ang), np.sin(ang)], 2).reshape(T, ROPE)
    i, j = np.arange(8)[:, None], np.arange(8)[None, :]
    c["before"] = np.broadcast_to((j < i).reshape(1, 64), (T, 64))
    for k in range(LEVELS):
        L = 1 << k
        m = (p // (2 * L) == f // (2 * L)) & (p // L % 2 == 0) & (f // L % 2 == 1)
        c[f"level{k}_0"], c[f"level{k}_1"] = m, m.T
    return np.concatenate([np.asarray(c[n], np.float32).reshape(T, -1) for n in CONSTS], 1)


PAIRS = [("gdn", 0), ("gdn", 1), ("rwkv", 0), ("rwkv", 1)]


def plan():
    t = []
    t += [(("mods", n), "V") for n in range(12)]
    t += [(("modT",), "V")]
    t += [(("gate", w, g, n), "A") for w in range(2) for g in range(2) for n in range(2)]
    t += [(("h1", g, n), "V") for g in range(2) for n in range(2)]
    t += [(("z", c, g), "A") for c in range(ZC) for g in range(2)]
    t += [((s, g, c), "V") for g in range(2) for c in range(5) for s in ("zp", "zn")]
    t += [(("decay",), "V")]
    t += [(("cqT", g), "A") for g in range(2)] + [(("ckvT", b), "A") for b in range(3)]
    t += [(("qT", k), "A") for k in range(2)] + [(("qpe", g), "V") for g in range(2)]
    t += [(("qpeT", g), "A") for g in range(2)]
    t += [(("kT", h), "A") for h in range(HEADS)] + [(("v", b), "V") for b in range(3)]
    for g in range(2):
        for h in range(HEADS):
            t += [(("score", g, h), "A"), (("pT", g, h), "V"), (("mla", g, h), "V")]
    for kind, g in PAIRS:
        p = (kind, g)
        if kind == "gdn":
            t += [(("qkT", g, s), "A") for s in range(2)] + [(("row", g, d), "V") for d in range(2)]
            t += [(("kk", g), "V"), (("qk", g), "V")]
            t += [(("kS", g), "V"), (("qS", g), "V")] * g
        else:
            t += [(("wdT", g), "A"), (("gdT", g), "A"), (("wpre", g), "V"), (("apre", g), "V"), (("rgate", g), "A")]
            t += [(("cum", g), "A")] + [(("suf", g), "A")] * (1 - g)
            t += [((s, g, d), "A") for d in range(2) for s in ("KTt", "RT", "BT", "KhT")]
            t += [((s, g, d, hp), "V") for d in range(2) for hp in range(2) for s in ("PB", "PK")]
            t += [(("cc", g), "A"), (("S0T", g), "V"), (("RS", g), "A")] * g
            t += [(("R", g), "A")]
        t += [(("T1", p, d), "A") for d in range(2)]
        for k in range(1, LEVELS):
            t += [(("X", p, k, d), "A") for d in range(2)]
            for d in range(2):
                t += [(("Y", p, k, d), "V")] * (k < LEVELS - 1) + [(("YT", p, k, d), "V")]
        t += [(("W", p), "V"), (("O", p), "V")] + [(("S", p), "V")] * (1 - g)
    t += [(("mixT", g, n), "A") for g in range(2) for n in range(2)]
    t += [(("out", n, g), "V") for n in range(2) for g in range(2)]
    t += [(("h2", g, n), "V") for g in range(2) for n in range(2)]
    t += [(("route", g), "V") for g in range(2)]
    return t


class Tiles:

    def __init__(self):
        self.order = [n for n, _ in plan()]
        self.who = dict(plan())
        self.index = {n: i for i, n in enumerate(self.order)}
        assert len(self.index) == len(self.order)
        self.total = len(self.order)
        self.rank, self.per = {}, {"V": 0, "A": 0}
        for n in self.order:
            self.per[self.who[n]] += 1
            self.rank[n] = self.per[self.who[n]]

    def filled(self, l, name):
        return l * self.total + (self.index[name] + 1)

    def emptied(self, l, name):
        return l * self.per[self.who[name]] + self.rank[name]


PIECES = [("ada", n) for n in range(12)] + [("w_in", c) for c in range(ZC)] + ["uq", "ukv"] + \
         [("w_out", n) for n in range(2)] + ["router", "shared"]
SLOTS = 4
assert len(PIECES) % SLOTS == 0 and EXPERTS % SLOTS == 0
RING_USES = len(PIECES) + EXPERTS
ITEMS = 2 * (EXPERTS + 1)
LAST_TILE = [("mods", n) for n in range(12)] + [("z", c, 1) for c in range(ZC)] + [("qpe", 1), ("v", 2)] + \
            [("out", n, 1) for n in range(2)] + [("route", 1)]
GU0, DOWN0 = 2 * SLOTS, 3


def build(nc, a, consts, outs):
    tiles = Tiles()
    y_prompt, y_sample, new_ckv, new_kpe, new_gdn, new_rwkv = outs
    with ExitStack() as ctx:
        def sb(name, n, parts=128):
            return ctx.enter_context(nc.sbuf_tensor(name, [parts, n], F32))

        def sem(name):
            return ctx.enter_context(nc.semaphore(name))

        ring = [sb(f"ring{s}", 4096) for s in range(SLOTS)]
        W1 = sb("W1", 8192)
        PR = sb("PR", 7168)
        C = sb("consts", CW)
        X = sb("x", 2 * D)
        HT = sb("hT", KD * 2 * T)
        Z = sb("z", 6144)
        GB = sb("gateB", 4096)
        SP = sb("small_params", 3088)
        SM = sb("small", 608)
        P = ctx.enter_context(nc.psum_tensor("P", [128, 8, 512], F32))

        def cst(name, parts=128):
            o, w = CONSTS[name]
            return C[0:parts, o:o + w]

        def many(ap, *dims):
            p, n = ap.shape
            return ap.rearrange("p (a n) -> p a n", a=1).to_broadcast([p, dims[0], n])

        def wide(ap, n):
            p, k = ap.shape
            return ap.rearrange("p (k a) -> p k a", a=1).to_broadcast([p, k, n])

        def v3(ap, k):
            return ap.rearrange("p (k n) -> p k n", k=k)

        ident = cst("ident")
        x = v3(X[:, :], 2)
        hT = v3(HT[:, :], KD)
        z = v3(Z[:, 0:2 * P_IN], 2)
        mods = Z[0:2, :]
        gateB = GB[:, :].rearrange("p (w g n) -> p w g n", w=2, g=2)

        o = 0
        small = {}
        for name, w in [("q_norm", QL), ("kv_norm", KVL), ("gdn_norm", N), ("w0", 512), ("a0", 512), ("k_k", 256),
                        ("k_a", 256), ("r_k", 256), ("gn_w", 256), ("gn_b", 256), ("bias", 64), ("a_log", 8),
                        ("dt", 8)]:
            small[name] = SP[:, o:o + w]
            o += w
        small_src = {"q_norm": a["mla_q_norm"], "kv_norm": a["mla_kv_norm"], "gdn_norm": a["gdn_norm"],
                     "w0": a["rwkv_w0"].rearrange("l d c -> l (d c)"), "a0": a["rwkv_a0"].rearrange("l d c -> l (d c)"),
                     "k_k": a["rwkv_k_k"], "k_a": a["rwkv_k_a"], "r_k": a["rwkv_r_k"].rearrange("l h n -> l (h n)"),
                     "gn_w": a["rwkv_gn_w"], "gn_b": a["rwkv_gn_b"], "bias": a["moe_bias"],
                     "a_log": a["gdn_a_log"].rearrange("l d h -> l (d h)"),
                     "dt": a["gdn_dt_bias"].rearrange("l d h -> l (d h)")}

        o = 0
        sm = {}
        for name, w in [("ss", 8), ("rs", 8), ("cT", 16), ("modT", 64), ("nT", 16), ("nalog", 8), ("gg", 16),
                        ("beta", 16), ("t16", 16), ("gcs", 32), ("egs", 32), ("nqk", 16), ("mx", 4), ("sum", 4),
                        ("comb", 128), ("scores", 64), ("sel", 64), ("w64", 64), ("st8", 24), ("ecc", 8)]:
            sm[name] = SM[:, o:o + w]
            o += w
        modT = sm["modT"].rearrange("p (m k g) -> p m k g", m=4, k=KD)
        gg = sm["gg"].rearrange("p (d g h) -> p d g h", d=2, g=2)
        beta = sm["beta"].rearrange("p (d g h) -> p d g h", d=2, g=2)
        gc = sm["gcs"][:, 0:16].rearrange("p (d g h) -> p d g h", d=2, g=2)
        egc = sm["egs"][:, 0:16].rearrange("p (d g h) -> p d g h", d=2, g=2)
        egs = sm["egs"][:, 16:32].rearrange("p (d g h) -> p d g h", d=2, g=2)
        comb = sm["comb"].rearrange("p (g e) -> p g e", g=2)

        mix3 = v3(PR[:, 0:5760], 3)
        conv_t = [PR[:, 5760:6144], PR[:, 6144:6528]]
        nrows = PR[0:8, 6528:6528 + 256].rearrange("p (w n) -> p w n", w=2)
        crow = W1[0:2, 0:D]
        ada_b = W1[0:2, 0:6144]

        o = 0
        mla = {}
        for name, w in [("cqn", 768), ("ckvn", 768), ("kpe", 192), ("cqT", 768), ("ckvT", 768), ("kpeT", 384),
                        ("qpe", 512), ("kT", 1536), ("v", 1536)]:
            mla[name] = W1[:, o:o + w]
            o += w
        cqn, ckvn, kpe = v3(mla["cqn"], 2), v3(mla["ckvn"], 3), v3(mla["kpe"], 3)
        cqT, ckvT = v3(mla["cqT"], 3), v3(mla["ckvT"], 2)
        kpeT = mla["kpeT"][0:64, :]
        qpe, kT, vv = v3(mla["qpe"], 2), v3(mla["kT"], HEADS), v3(mla["v"], 3)
        prob = [W1[:, 0:256], W1[:, 256:512]]
        pT = [v3(W1[:, 768:1024], 2), v3(W1[:, 1024:1280], 2)]
        rt = v3(W1[:, 7232:7744], 2)
        assert o <= 7232
        qT = HT[:, 0:1024].rearrange("p (h g t) -> p h g t", h=HEADS, g=2)
        qpeT = HT[0:64, 1024:2048].rearrange("p (g h t) -> p g h t", g=2, h=HEADS)

        def u4(ap):
            return ap.rearrange("p (d h n) -> p d h n", d=2, h=HEADS)
        AT, MT, PB, PK = (u4(W1[:, 1024 * k:1024 * k + 1024]) for k in range(4))
        KRT = W1[0:64, 4096:6144].rearrange("p (d h s t) -> p d h s t", d=2, h=HEADS, s=2)
        BT = u4(W1[0:64, 6144:7168])
        KTh = u4(W1[0:64, 7168:8192])
        Tm, TT, XX = (u4(W1[:, 4096 + 1024 * k:5120 + 1024 * k]) for k in range(3))
        Lm = [u4(W1[:, 7168:8192]), u4(PR[:, 0:1024])]
        qkT = W1[0:64, 4096:5120].rearrange("p (s h t) -> p s h t", s=2, h=HEADS)
        gtri = MT
        Rt, Ktl = v3(W1[:, 0:512], 2), v3(W1[:, 512:1024], 2)
        Bh, Kh = v3(W1[:, 1024:1536], 2), v3(W1[:, 1536:2048], 2)
        E, Ei = v3(W1[:, 2048:2560], 2), v3(W1[:, 2560:3072], 2)
        Ex, Fs = v3(W1[:, 3072:3584], 2), v3(W1[:, 3584:4096], 2)
        o = 1024
        nat = {}
        for name, w in [("lw", 512), ("a", 512), ("kd", 512), ("Bf", 512), ("Kf", 512), ("R", 512), ("SA", 512),
                        ("gate", 256), ("kk", 256), ("w2", 512), ("a2", 512), ("g2", 256), ("wdT", 512),
                        ("oacc", 256)]:
            nat[name] = PR[:, o:o + w]
            o += w
        nat["gdT"] = nat["oacc"][:, 0:128]
        lw, aa, kd, Bf, Kf = (v3(nat[n], 2) for n in ("lw", "a", "kd", "Bf", "Kf"))
        R, SA = u4(nat["R"]), u4(nat["SA"])
        S0nat, S0T = u4(nat["Bf"][0:64, :]), u4(nat["Kf"][0:64, :])
        w2, a2 = v3(nat["w2"][0:64, :], 2), v3(nat["a2"][0:64, :], 2)
        wdT = v3(nat["wdT"][0:64, :], 4)
        S0g = u4(nat["w2"][0:64, :])
        kdec = u4(nat["kd"])
        sq = nat["wdT"]
        oacc = nat["oacc"]
        sout = nat["a2"][0:64, :]

        down = [v3(W1[:, 2048 * s:2048 * s + 2048], 2) for s in range(SLOTS)]
        sg = [PR[:, 256 * i:256 * i + 256] for i in range(2)]
        act_ = [PR[:, 512 + 256 * i:768 + 256 * i] for i in range(2)]
        actT = [v3(PR[:, 1024 + 256 * i:1280 + 256 * i], 2) for i in range(2)]
        xs = v3(PR[:, 2048:4096], 2)
        xs1 = v3(W1[:, 0:2048], 2)
        xo = v3(PR[:, 4096:6144], 2)
        normf = W1[:, 0:D]

        const_in = sem("const_in")
        x_in = sem("x_in")
        c_in = sem("c_in")
        ring_in = [sem(f"ring_in{s}") for s in range(SLOTS)]
        down_in = [sem(f"down_in{s}") for s in range(SLOTS)]
        down_used = sem("down_used")
        filled = sem("tile_filled")
        empty = {"V": sem("tile_emptied_v"), "A": sem("tile_emptied_a")}
        x_done = sem("x_done")
        cT_ready = sem("cT_ready")
        small_in = sem("small_in")
        adab_in = sem("adab_in")
        mix_in = sem("mix_in")
        ctx_in = sem("ctx_in")
        state_in = sem("state_in")
        lora_in = sem("lora_in")
        ss_ready = sem("sum_squares_ready")
        ss_eps = sem("mean_square_ready")
        rs_ready = sem("rstd_ready")
        xn_ready = sem("xn_ready")
        z_mid = sem("z_scaled")
        conv_done = sem("conv_done")
        silu_done = sem("z_activated")
        mix_c = sem("centre_weight_ready")
        gates_v = sem("gates_v")
        gates_a = sem("gates_a")
        cq_ready = sem("cq_ready")
        ckv_ready = sem("ckv_ready")
        qpe_ready = sem("qpe_ready")
        nmax = sem("negative_max_ready")
        prob_ready = sem("prob_ready")
        gtri_ready = sem("gtri_ready")
        dec_v = sem("decay_difference_ready")
        dec_a = sem("decay_ready")
        at_ready = sem("at_ready")
        lm_ready = sem("level_ready")
        tt_ready = sem("tt_ready")
        rhs_ready = sem("rhs_ready")
        kdec_ready = sem("kdec_ready")
        fin_v = sem("finish_v")
        fin_a = sem("finish_a")
        pair_done = sem("pair_done")
        mixed = sem("mixed_ready")
        rw_v = sem("rwkv_v")
        rw_a = sem("rwkv_a")
        rwp = sem("rwkv_operands")
        ckv_out = sem("ckv_stored")
        state_ready = sem("state_ready")
        state_out = sem("state_stored")
        logit_v = sem("logits_copied")
        logit_a = sem("scores_ready")
        gu_full = sem("gu_full")
        silu_e = sem("expert_silu")
        act_done = sem("expert_act")
        t_full = sem("act_transposed")
        t_empty = sem("actT_ready")
        y_full = sem("y_full")
        normf_in = sem("normf_in")
        y_ready = sem("y_ready")
        y_out = sem("y_out")
        narrow_turns = sem("narrow_turns")

        block = ctx.enter_context(nc.Block())

        @block.sync
        def _(sp):
            sp.dma_start(C[:, :], consts).then_inc(const_in, 16)
            for g, src in enumerate((a["x_prompt"], a["x_sample"])):
                sp.dma_start(x[:, g, :], src[0]).then_inc(x_in, 16)
            with sp.Fori(0, LAYERS) as l:
                def chunk(ap):
                    return ap.rearrange("a (k p) n -> p (a k) n", p=128)

                def gu_used(expert):
                    return l * ITEMS + (GU0 + 2 * expert + 4)

                def piece(i, k, n, src):
                    if i < SLOTS:
                        sp.wait_ge(gu_full, l * ITEMS + (GU0 + 2 * (EXPERTS - SLOTS + i) + 4 - ITEMS))
                    else:
                        sp.wait_ge(filled, tiles.filled(l, LAST_TILE[i - SLOTS]))
                    dst = v3(ring[i % SLOTS][:, 0:k * n], k)
                    sp.dma_start(dst, src).then_inc(ring_in[i % SLOTS], 16)

                i = 0
                for n in range(12):
                    piece(i, KD, 512, chunk(a["ada_w"][bass.ds(l, 1), :, 512 * n:512 * n + 512]))
                    i += 1
                for c in range(ZC):
                    piece(i, KD, ZW[c], chunk(a["w_in"][bass.ds(l, 1), :, 512 * c:512 * c + ZW[c]]))
                    i += 1
                piece(i, 3, 768, chunk(a["mla_w_uq"][bass.ds(l, 1), :, :]))
                piece(i + 1, 2, 1024, chunk(a["mla_w_ukv"][bass.ds(l, 1), :, :]))
                i += 2
                for n in range(2):
                    piece(i, KD, 512, chunk(a["w_out"][bass.ds(l, 1), :, 512 * n:512 * n + 512]))
                    i += 1
                piece(i, KD, EXPERTS, chunk(a["moe_router"][bass.ds(l, 1), :, :]))
                piece(i + 1, KD, 2 * FF, chunk(a["shared_w_gu"][bass.ds(l, 1), :, :]))
                assert i + 2 == len(PIECES)
                sp.wait_ge(mixed, l * 2 + 2)
                sp.wait_ge(state_out, l * 32 + 32)
                sp.dma_start(down[3], chunk(a["shared_w_down"][bass.ds(l, 1), :, :])).then_inc(down_in[3], 16)
                gu_all = a["moe_w_gu"].rearrange("l e k n -> (l e) k n")
                dn_all = a["moe_w_down"].rearrange("l e k n -> (l e) k n")

                def expert(e, s):
                    sp.dma_start(v3(ring[s][:, :], KD), chunk(gu_all[bass.ds(l * EXPERTS + e, 1), :, :])
                                 ).then_inc(ring_in[s], 16)
                    sp.wait_ge(down_used, l * EXPERTS + e + (DOWN0 - 2))
                    sp.dma_start(down[s], chunk(dn_all[bass.ds(l * EXPERTS + e, 1), :, :])).then_inc(down_in[s], 16)

                for s in range(SLOTS):
                    if s < SLOTS - 1:
                        sp.wait_ge(filled, tiles.filled(l, LAST_TILE[len(PIECES) - SLOTS + s]))
                    else:
                        sp.wait_ge(gu_full, gu_used(-1))
                    expert(s, s)
                with sp.Fori(1, EXPERTS // SLOTS) as eb:
                    for s in range(SLOTS):
                        sp.wait_ge(gu_full, gu_used(s - SLOTS) + eb * (2 * SLOTS))
                        expert(eb * SLOTS + s, s)
            sp.wait_ge(x_done, LAYERS + 1)
            sp.dma_start(normf, a["norm_f"].rearrange("(a n) -> a n", a=1).partition_broadcast(128)
                         ).then_inc(normf_in, 16)
            for g, dst in enumerate((y_prompt, y_sample)):
                sp.wait_ge(y_ready, g + 1)
                sp.dma_start(dst[0], xo[:, g, :]).then_inc(y_out, 16)
            sp.wait_ge(y_out, 32)
            sp.wait_ge(ckv_out, 32 * LAYERS)
            sp.wait_ge(state_out, 32 * LAYERS)

        @block.tensor
        def _(pe):
            def tile(l, name):
                settled[0] = False
                i = tiles.index[name]
                assert i == order[0], name
                order[0] += 1
                if i >= 8:
                    before = tiles.order[i - 8]
                    pe.wait_ge(empty[tiles.who[before]], tiles.emptied(l, before))
                return P[:, i % 8, :]

            def need(l, name):
                pe.wait_ge(empty[tiles.who[name]], tiles.emptied(l, name))

            def turn_narrow(out, src, unit):
                if not settled[0]:
                    pe.nop().then_inc(narrow_turns, 1)
                    settled[0] = True
                return pe.transpose(out, src, unit)

            def mm(out, lhsT, rhs, start, stop):
                return pe.matmul(out, lhsT, rhs, start=start, stop=stop)

            order, settled = [0], [False]
            pe.wait_ge(const_in, 16)
            pe.wait_ge(cT_ready, 1)
            for k in range(KD):
                last = pe.transpose(P[:, 0, 2 * k:2 * k + 2], crow[:, 128 * k:128 * k + 128], cst("ident", 2)[:, 0:2])
            last.then_inc(cT_ready, 1)
            for _ in range(DOWN0):
                pe.nop().then_inc(down_used, 1)
            for _ in range(GU0):
                pe.nop().then_inc(gu_full, 1)
            pe.wait_ge(cT_ready, 3)
            cT = v3(sm["cT"], KD)

            with pe.Fori(0, LAYERS) as l:
                order[0] = 0
                pe.wait_ge(x_done, l + 1)

                def piece(i):
                    u = i // SLOTS + 1
                    pe.wait_ge(ring_in[i % SLOTS], l * (RING_USES // SLOTS * 16) + 16 * u)
                    return ring[i % SLOTS]

                i = 0
                for n in range(12):
                    w = v3(piece(i)[:, :], KD)
                    b = tile(l, ("mods", n))
                    for k in range(KD):
                        last = mm(b[0:2, :], cT[:, k, :], w[:, k, :], k == 0, k == KD - 1)
                    last.then_inc(filled, 1)
                    i += 1
                need(l, ("mods", 11))
                pe.wait_ge(adab_in, l * 48 + 48)
                b = tile(l, ("modT",))
                for m, part in enumerate((0, 1, 3, 4)):
                    for k in range(KD):
                        c0 = part * D + 128 * k
                        turn_narrow(b[:, (m * KD + k) * 2:(m * KD + k) * 2 + 2], mods[:, c0:c0 + 128],
                                     cst("ident", 2)[:, 0:2])
                for w in range(2):
                    last = pe.transpose(b[:, 64 + 8 * w:72 + 8 * w], nrows[:, w, :], cst("ident", 8)[:, 0:8])
                last.then_inc(filled, 1)
                for w, part in enumerate((2, 5)):
                    for g in range(2):
                        for n in range(2):
                            b = tile(l, ("gate", w, g, n))
                            c0 = part * D + 512 * n
                            mm(b, cst("ident", 2)[:, g:g + 1].to_broadcast([2, T]), mods[:, c0:c0 + 512], True, True).then_inc(filled, 1)

                def to_columns(which, xn_count):
                    for g in range(2):
                        for n in range(2):
                            b = tile(l, (which, g, n))
                            if n == 0:
                                pe.wait_ge(xn_ready, l * 4 + (xn_count + g))
                            for k in range(4):
                                c0 = 512 * n + 128 * k
                                src = (xs1 if which == "h1" else xs)[:, g, c0:c0 + 128]
                                last = pe.transpose(b[:, 128 * k:128 * k + 128], src, ident)
                            last.then_inc(filled, 1)

                to_columns("h1", 1)
                need(l, ("h1", 1, 1))
                for c in range(ZC):
                    w = v3(piece(i)[:, 0:KD * ZW[c]], KD)
                    for g in range(2):
                        b = tile(l, ("z", c, g))
                        for k in range(KD):
                            last = mm(b[:, 0:ZW[c]], hT[:, k, 128 * g:128 * g + 128], w[:, k, :], k == 0, k == KD - 1)
                        last.then_inc(filled, 1)
                    i += 1
                need(l, ("z", ZC - 1, 1))
                for g in range(2):
                    for c, c0 in enumerate(SHIFTED):
                        for s, shift in (("zp", "prev"), ("zn", "next")):
                            b = tile(l, (s, g, c))
                            mm(b[:, 0:CONV], cst(shift), z[:, g, c0:c0 + CONV], True, True).then_inc(filled, 1)
                b = tile(l, ("decay",))
                pe.wait_ge(gates_v, l * 4 + 4)
                for d in range(2):
                    gd = gg[:, d, :, :]
                    mm(b[:, 8 * d:8 * d + 8], cst(f"tri{d}"), gd, True, True)
                    last = mm(b[:, 16 + 8 * d:24 + 8 * d], cst(f"strict{1 - d}"), gd, True, True)
                last.then_inc(filled, 1)

                for g in range(2):
                    b = tile(l, ("cqT", g))
                    pe.wait_ge(cq_ready, l * 2 + (g + 1))
                    for k in range(3):
                        last = pe.transpose(b[:, 128 * k:128 * k + 128], cqn[:, g, 128 * k:128 * k + 128], ident)
                    last.then_inc(filled, 1)
                for blk in range(3):
                    b = tile(l, ("ckvT", blk))
                    pe.wait_ge(ckv_ready, l * 3 + (blk + 1))
                    for k in range(2):
                        pe.transpose(b[:, 128 * k:128 * k + 128], ckvn[:, blk, 128 * k:128 * k + 128], ident)
                    turn_narrow(b[0:64, 256:384], kpe[:, blk, :], ident).then_inc(filled, 1)
                uq = v3(piece(i)[:, 0:3 * 768], 3)
                need(l, ("cqT", 1))
                for hp in range(2):
                    b = tile(l, ("qT", hp))
                    for h in (2 * hp, 2 * hp + 1):
                        for k in range(3):
                            last = mm(b[:, 256 * (h % 2):256 * (h % 2) + 256], uq[:, k, 192 * h:192 * h + 128],
                                      cqT[:, k, :], k == 0, k == 2)
                    last.then_inc(filled, 1)
                for g in range(2):
                    b = tile(l, ("qpe", g))
                    for k in range(3):
                        w = uq[:, k, :].rearrange("p (h n) -> p h n", h=HEADS)[:, :, NOPE:NOPE + ROPE]
                        last = mm(b[:, 0:256], cqT[:, k, 128 * g:128 * g + 128], w, k == 0, k == 2)
                    last.then_inc(filled, 1)
                i += 1
                for g in range(2):
                    b = tile(l, ("qpeT", g))
                    pe.wait_ge(qpe_ready, l * 2 + (g + 1))
                    for h in range(HEADS):
                        last = turn_narrow(b[0:64, 128 * h:128 * h + 128], qpe[:, g, 64 * h:64 * h + 64], ident)
                    last.then_inc(filled, 1)
                ukv = v3(piece(i)[:, 0:2048], 2)
                need(l, ("ckvT", 2))
                for h in range(HEADS):
                    b = tile(l, ("kT", h))
                    for k in range(2):
                        last = mm(b[:, 0:384], ukv[:, k, 256 * h:256 * h + 128], ckvT[:, k, :], k == 0, k == 1)
                    last.then_inc(filled, 1)
                for blk in range(3):
                    b = tile(l, ("v", blk))
                    for k in range(2):
                        w = ukv[:, k, :].rearrange("p (h n) -> p h n", h=HEADS)[:, :, NOPE:NOPE + VDIM]
                        last = mm(b, ckvT[:, k, 128 * blk:128 * blk + 128], w, k == 0, k == 1)
                    last.then_inc(filled, 1)
                i += 1
                need(l, ("qpeT", 1))
                need(l, ("v", 2))
                need(l, ("kT", 3))
                for g in range(2):
                    k0, nk = (0, 1) if g == 0 else (1, 2)
                    keys = slice(128 * k0, 128 * (k0 + nk))
                    for h in range(HEADS):
                        b = tile(l, ("score", g, h))
                        mm(b[:, 0:128 * nk], qT[:, h, g, :], kT[:, h, keys], True, False)
                        mm(b[:, 0:128 * nk], qpeT[:, g, h, :], kpeT[:, keys], False, True).then_inc(filled, 1)
                        b = tile(l, ("pT", g, h))
                        pe.wait_ge(prob_ready, l * 8 + (4 * g + h + 1))
                        for q in range(nk):
                            last = pe.transpose(b[:, 128 * q:128 * q + 128], prob[h % 2][:, 128 * q:128 * q + 128], ident)
                        last.then_inc(filled, 1)
                        b = tile(l, ("mla", g, h))
                        need(l, ("pT", g, h))
                        for q in range(nk):
                            last = mm(b[:, 0:128], pT[h % 2][:, q, :], vv[:, k0 + q, 128 * h:128 * h + 128],
                                      q == 0, q == nk - 1)
                        last.then_inc(filled, 1)

                for pi, p in enumerate(PAIRS):
                    kind, g = p
                    if kind == "gdn":
                        for s in range(2):
                            b = tile(l, ("qkT", g, s))
                            for h in range(HEADS):
                                c0 = Z_G + 256 * s + 64 * h
                                if s == 0 and h == 0:
                                    pe.wait_ge(fin_v, l * 6 + (g + 1))
                                last = turn_narrow(b[0:64, 128 * h:128 * h + 128], z[:, g, c0:c0 + 64], ident)
                            last.then_inc(filled, 1)
                        for d in range(2):
                            b = tile(l, ("row", g, d))
                            if d == 0:
                                pe.wait_ge(gtri_ready, l * 2 + (g + 1))
                            mm(b, cst("ones"), gtri[:, d, :, :].rearrange("p h n -> p (h n)"), True, True
                               ).then_inc(filled, 1)
                        b = tile(l, ("kk", g))
                        need(l, ("qkT", g, 1))
                        for h in range(HEADS):
                            last = mm(b[:, 128 * h:128 * h + 128], qkT[:, 1, h, :], qkT[:, 1, h, :], True, True)
                        last.then_inc(filled, 1)
                        b = tile(l, ("qk", g))
                        for h in range(HEADS):
                            last = mm(b[:, 128 * h:128 * h + 128], qkT[:, 1, h, :], qkT[:, 0, h, :], True, True)
                        last.then_inc(filled, 1)
                        if g:
                            pe.wait_ge(state_in, l * 32 + 16)
                            for name, s in (("kS", 1), ("qS", 0)):
                                b = tile(l, (name, g))
                                for d in range(2):
                                    for h in range(HEADS):
                                        c0 = 64 * (4 * d + h)
                                        last = mm(b[:, c0:c0 + 64], qkT[:, s, h, :], S0g[:, d, h, :], True, True)
                                last.then_inc(filled, 1)
                    else:
                        b = tile(l, ("wdT", g))
                        for q in range(4):
                            c0 = Z_WD + 64 * q
                            last = turn_narrow(b[0:64, 128 * q:128 * q + 128], z[:, g, c0:c0 + 64], ident)
                        last.then_inc(filled, 1)
                        b = tile(l, ("gdT", g))
                        pe.transpose(b[:, 0:128], z[:, g, Z_GD:Z_GD + 128], ident).then_inc(filled, 1)
                        need(l, ("gdT", g))
                        pe.wait_ge(lora_in, l * 96 + 48 * (g + 1))
                        for q, (name, w) in enumerate((("wpre", w2), ("apre", a2))):
                            b = tile(l, (name, g))
                            for d in range(2):
                                last = mm(b[:, 256 * d:256 * d + 256], wdT[:, 2 * q + d, :], w[:, d, :], True, True)
                            last.then_inc(filled, 1)
                        b = tile(l, ("rgate", g))
                        mm(b[:, 0:256], nat["gdT"], nat["g2"], True, True).then_inc(filled, 1)
                        b = tile(l, ("cum", g))
                        pe.wait_ge(rwp, l * 4 + (2 * g + 1))
                        for d in range(2):
                            last = mm(b[:, 256 * d:256 * d + 256], cst(f"cen{d}"), lw[:, d, :], True, True)
                        last.then_inc(filled, 1)
                        if g == 0:
                            b = tile(l, ("suf", g))
                            for d in range(2):
                                last = mm(b[:, 256 * d:256 * d + 256], cst(f"strict{1 - d}"), lw[:, d, :], True, True)
                            last.then_inc(filled, 1)
                        pe.wait_ge(rwp, l * 4 + (2 * g + 2))
                        for d in range(2):
                            for name, src in (("KTt", Ktl), ("RT", Rt), ("BT", Bh), ("KhT", Kh)):
                                b = tile(l, (name, g, d))
                                for h in range(HEADS):
                                    last = turn_narrow(b[0:64, 128 * h:128 * h + 128], src[:, d, 64 * h:64 * h + 64],
                                                        ident)
                                last.then_inc(filled, 1)
                        need(l, ("KhT", g, 1))
                        for d in range(2):
                            for hp in range(2):
                                for name, src in (("PB", BT), ("PK", KTh)):
                                    b = tile(l, (name, g, d, hp))
                                    for h in (2 * hp, 2 * hp + 1):
                                        last = mm(b[:, 256 * (h % 2):256 * (h % 2) + 256], src[:, d, h, :],
                                                  KRT[:, d, h, :, :].rearrange("p s t -> p (s t)"), True, True)
                                    last.then_inc(filled, 1)
                        if g:
                            b = tile(l, ("cc", g))
                            for d in range(2):
                                for h in range(HEADS):
                                    q = 4 * d + h
                                    last = mm(b[0:64, q:q + 1], lw[:, d, 64 * h:64 * h + 64], cst(f"half{d}"),
                                              True, True)
                            last.then_inc(filled, 1)
                            b = tile(l, ("S0T", g))
                            pe.wait_ge(state_in, l * 32 + 32)
                            for d in range(2):
                                for h in range(HEADS):
                                    c0 = 64 * (4 * d + h)
                                    last = turn_narrow(b[0:64, c0:c0 + 64], S0nat[:, d, h, :],
                                                        cst("ident", 64)[:, 0:64])
                            last.then_inc(filled, 1)
                            b = tile(l, ("RS", g))
                            need(l, ("S0T", g))
                            for h in range(HEADS):
                                for d in range(2):
                                    last = mm(b[:, 64 * h:64 * h + 64], KRT[:, d, h, 1, :], S0T[:, d, h, :],
                                              d == 0, d == 1)
                            last.then_inc(filled, 1)
                        b = tile(l, ("R", g))
                        need(l, ("PK", g, 1, 1))
                        for d in range(2):
                            for h in range(HEADS):
                                c0 = 64 * (4 * d + h)
                                v_h = z[:, g, Z_V + 64 * h:Z_V + 64 * h + 64]
                                if g:
                                    mm(b[:, c0:c0 + 64], KRT[:, d, h, 0, :], S0T[:, d, h, :], True, False)
                                last = mm(b[:, c0:c0 + 64], MT[:, d, h, :], v_h, not g, True)
                        last.then_inc(filled, 1)

                    for d in range(2):
                        b = tile(l, ("T1", p, d))
                        if d == 0:
                            pe.wait_ge(tt_ready, l * 4 + (pi + 1))
                        for h in range(HEADS):
                            last = pe.transpose(b[:, 128 * h:128 * h + 128], TT[:, d, h, :], ident)
                        last.then_inc(filled, 1)
                    for k in range(1, LEVELS):
                        final = k == LEVELS - 1
                        for d in range(2):
                            b = tile(l, ("X", p, k, d))
                            if d == 0:
                                pe.wait_ge(lm_ready, l * 4 * LEVELS + (pi * LEVELS + k + 1))
                            need(l, ("T1", p, d) if k == 1 else ("Y", p, k - 1, d))
                            for h in range(HEADS):
                                last = mm(b[:, 128 * h:128 * h + 128], Lm[k % 2][:, d, h, :], Tm[:, d, h, :], True, True)
                            last.then_inc(filled, 1)
                        for d in range(2):
                            if not final:
                                b = tile(l, ("Y", p, k, d))
                                need(l, ("X", p, k, d))
                                if k > 1:
                                    need(l, ("YT", p, k - 1, d))
                                for h in range(HEADS):
                                    last = mm(b[:, 128 * h:128 * h + 128], TT[:, d, h, :], XX[:, d, h, :], True, True)
                                last.then_inc(filled, 1)
                            b = tile(l, ("YT", p, k, d))
                            if final:
                                need(l, ("X", p, k, d))
                                need(l, ("YT", p, k - 1, d))
                            for h in range(HEADS):
                                last = mm(b[:, 128 * h:128 * h + 128], XX[:, d, h, :], TT[:, d, h, :], True, True)
                            last.then_inc(filled, 1)

                    b = tile(l, ("W", p))
                    need(l, ("YT", p, LEVELS - 1, 1))
                    if kind == "gdn":
                        pe.wait_ge(rhs_ready, l * 2 + (g + 1))
                    else:
                        need(l, ("R", g))
                    for d in range(2):
                        for h in range(HEADS):
                            c0 = 64 * (4 * d + h)
                            last = mm(b[:, c0:c0 + 64], TT[:, d, h, :], R[:, d, h, :], True, True)
                    last.then_inc(filled, 1)
                    b = tile(l, ("O", p))
                    need(l, ("W", p))
                    for h in range(HEADS):
                        out = b[:, 64 * h:64 * h + 64]
                        if kind == "gdn":
                            for d in range(2):
                                last = mm(out, PK[:, d, h, :], SA[:, d, h, :], d == 0, d == 1)
                        else:
                            v_h = z[:, g, Z_V + 64 * h:Z_V + 64 * h + 64]
                            for d in range(2):
                                mm(out, PB[:, d, h, :], SA[:, d, h, :], d == 0, False)
                                last = mm(out, PK[:, d, h, :], v_h, False, d == 1)
                    last.then_inc(filled, 1)
                    if g == 0:
                        b = tile(l, ("S", p))
                        if kind == "gdn":
                            pe.wait_ge(kdec_ready, l * 1 + 1)
                        for d in range(2):
                            for h in range(HEADS):
                                c0 = 64 * (4 * d + h)
                                if kind == "gdn":
                                    last = mm(b[0:64, c0:c0 + 64], kdec[:, d, h, :], SA[:, d, h, :], True, True)
                                else:
                                    hs = slice(64 * h, 64 * h + 64)
                                    mm(b[0:64, c0:c0 + 64], SA[:, d, h, :], Bf[:, d, hs], True, False)
                                    last = mm(b[0:64, c0:c0 + 64], z[:, g, Z_V + 64 * h:Z_V + 64 * h + 64],
                                              Kf[:, d, hs], False, True)
                        last.then_inc(filled, 1)

                pe.wait_ge(mixed, l * 2 + 2)
                for g in range(2):
                    for n in range(2):
                        b = tile(l, ("mixT", g, n))
                        for k in range(4):
                            c0 = [(0, 128, 256, 384), (Z_G, Z_G + 128, Z_R, Z_R + 128)][n][k]
                            last = pe.transpose(b[:, 128 * k:128 * k + 128], z[:, g, c0:c0 + 128], ident)
                        last.then_inc(filled, 1)
                need(l, ("mixT", 1, 1))
                for n in range(2):
                    w = v3(piece(i)[:, :], KD)
                    for g in range(2):
                        b = tile(l, ("out", n, g))
                        for k in range(KD):
                            last = mm(b, hT[:, k, 128 * g:128 * g + 128], w[:, k, :], k == 0, k == KD - 1)
                        last.then_inc(filled, 1)
                    i += 1

                to_columns("h2", 3)
                need(l, ("h2", 1, 1))
                w = v3(piece(i)[:, 0:KD * EXPERTS], KD)
                for g in range(2):
                    b = tile(l, ("route", g))
                    for k in range(KD):
                        last = mm(b[:, 0:EXPERTS], hT[:, k, 128 * g:128 * g + 128], w[:, k, :], k == 0, k == KD - 1)
                    last.then_inc(filled, 1)
                i += 1
                assert order[0] == tiles.total
                need(l, ("route", 1))

                def gate_up(item, g, w, k0, k1):
                    for k in range(k0, k1):
                        last = pe.matmul(P[:, 4 + g, :], hT[:, k, 128 * g:128 * g + 128], w[:, k, :],
                                         start=k == 0, stop=k == KD - 1, skip_group_check=True)
                    return last

                def turn(count, g):
                    pe.wait_ge(act_done, count)
                    for f in range(2):
                        last = pe.transpose(P[:, 6 + g, 128 * f:128 * f + 128], act_[g][:, 128 * f:128 * f + 128], ident)
                    last.then_inc(t_full, 1)

                def project(count, g, wd, first):
                    pe.wait_ge(t_empty, count)
                    for n in range(2):
                        for f in range(2):
                            last = pe.matmul(P[:, 2 * g + n, :], actT[g][:, f, :], wd[:, f, 512 * n:512 * n + 512],
                                             start=first and f == 0, stop=False, skip_group_check=True)
                    return last

                w = v3(piece(i)[:, :], KD)
                gate_up(0, 0, w, 0, KD).then_inc(gu_full, 1)
                gate_up(1, 1, w, 0, 4)
                turn(l * ITEMS + 1, 0)
                gate_up(1, 1, w, 4, KD).then_inc(gu_full, 1)
                pe.wait_ge(down_in[3], l * (17 * 16) + 16)
                project(l * ITEMS + 1, 0, down[3], True)
                zeros = cst("strict0")[:, 0:1].to_broadcast([128, T])
                for n in range(2):
                    pe.matmul(P[:, 2 + n, :], zeros, C[:, 0:512], start=True, stop=False, skip_group_check=True)
                with pe.Fori(0, EXPERTS // SLOTS) as eb:
                    for s in range(SLOTS):
                        u = len(PIECES) // SLOTS + 1
                        pe.wait_ge(ring_in[s], l * (RING_USES // SLOTS * 16) + eb * 16 + 16 * u)
                        w = v3(ring[s][:, :], KD)
                        it = l * ITEMS + eb * (2 * SLOTS) + 2 * s
                        pe.wait_ge(act_done, it + 1)
                        gate_up(0, 0, w, 0, 4)
                        turn(it + 2, 1)
                        gate_up(0, 0, w, 4, KD).then_inc(gu_full, 1)
                        project(it + 2, 1, down[(s + 3) % SLOTS], False).then_inc(down_used, 1)
                        gate_up(0, 1, w, 0, 4)
                        turn(it + 3, 0)
                        gate_up(0, 1, w, 4, KD).then_inc(gu_full, 1)
                        if s == 3:
                            pe.wait_ge(down_in[s], l * (17 * 16) + eb * 16 + 32)
                        else:
                            pe.wait_ge(down_in[s], l * (16 * 16) + eb * 16 + 16)
                        project(it + 3, 0, down[s], False)
                turn(l * ITEMS + ITEMS, 1)
                project(l * ITEMS + ITEMS, 1, down[3], False).then_inc(y_full, 1)

        @block.scalar
        def _(act):
            def row(ap, l):
                return ap[bass.ds(l, 1), :].partition_broadcast(128)

            def f(l, name):
                act.wait_ge(filled, tiles.filled(l, name))
                return P[:, tiles.index[name] % 8, :]

            def done(ins, name):
                i = tiles.index[name]
                assert tiles.who[name] == "A" and tiles.rank[name] == cnt[0] + 1, name
                cnt[0] += 1
                ins.then_inc(empty["A"], 1)

            cnt = [0]
            act.dma_start(crow[0:1, :], a["c_ctx"].rearrange("(a n) -> a n", a=1)).then_inc(c_in, 16)
            act.dma_start(crow[1:2, :], a["c"]).then_inc(c_in, 16)
            act.wait_ge(c_in, 32)
            act.activation(crow, crow, ACT.Silu).then_inc(cT_ready, 1)
            act.wait_ge(cT_ready, 2)
            act.activation(sm["cT"], P[:, 0, 0:16], ACT.Copy).then_inc(cT_ready, 1)

            with act.Fori(0, LAYERS) as l:
                cnt[0] = 0
                act.wait_ge(x_done, l + 1)
                act.wait_ge(cT_ready, 3)
                act.dma_start(ada_b, a["ada_b"][bass.ds(l, 1), :].partition_broadcast(2)).then_inc(adab_in, 16)
                for w, name in enumerate(("norm1", "norm2")):
                    act.dma_start(nrows[:, w, :], a[name][bass.ds(l, 1), :].rearrange("a (k n) -> (a k) n", k=8)
                                  ).then_inc(adab_in, 16)
                for name in small:
                    act.dma_start(small[name], row(small_src[name], l)).then_inc(small_in, 16)
                conv = a["gdn_conv"]
                for j, (tap, mu) in enumerate(((0, "rwkv_mu_prev"), (2, "rwkv_mu_next"))):
                    act.dma_start(mix3[:, j, 0:768], conv[bass.ds(l, 1), tap, :].partition_broadcast(128)
                                  ).then_inc(mix_in, 16)
                    act.dma_start(mix3[:, j, 768:1920], row(a[mu], l)).then_inc(mix_in, 16)
                act.dma_start(mix3[:, 2, 0:768], conv[bass.ds(l, 1), 1, :].partition_broadcast(128)
                              ).then_inc(mix_in, 16)

                def norm(which, n):
                    for g in range(2):
                        ins = act.activation(W1[:, 6144:7168] if which == 0 else PR[:, 0:D], x[:, g, :], ACT.Square,
                                             accum_out=sm["ss"][:, g:g + 1])
                        act.drain()
                        act.nop().then_inc(ss_ready, 1)
                    act.wait_ge(ss_eps, n)
                    act.activation(sm["rs"][:, 0:2], sm["ss"][:, 2:4], ACT.Ln)
                    act.drain()
                    act.activation(sm["rs"][:, 2:4], sm["rs"][:, 0:2], ACT.Exp, scale=-0.5).then_inc(rs_ready, 1)

                norm(0, l * 2 + 1)
                for w in range(2):
                    for g in range(2):
                        for n in range(2):
                            name = ("gate", w, g, n)
                            done(act.activation(gateB[:, w, g, 512 * n:512 * n + 512], f(l, name), ACT.Copy), name)
                for c in range(ZC):
                    for g in range(2):
                        name = ("z", c, g)
                        done(act.activation(z[:, g, 512 * c:512 * c + ZW[c]], f(l, name)[:, 0:ZW[c]], ACT.Copy), name)
                act.dma_start(ckvn[:, 1, :], a["cache_mla_ckv"][0, bass.ds(l, 1), :, :].rearrange("a t c -> (a t) c")
                              ).then_inc(ctx_in, 16)
                act.dma_start(kpe[:, 1, :], a["cache_mla_kpe"][0, bass.ds(l, 1), :, :].rearrange("a t c -> (a t) c")
                              ).then_inc(ctx_in, 16)
                for g in range(2):
                    act.activation(cqn[:, g, :], z[:, g, 0:QL], ACT.Square, accum_out=sm["ss"][:, 4 * g:4 * g + 1])
                    act.drain()
                    act.activation(ckvn[:, 2 * g, :], z[:, g, QL:QL + KVL], ACT.Square,
                                   accum_out=sm["ss"][:, 4 * g + 1:4 * g + 2])
                    act.drain()
                act.nop().then_inc(gates_a, 1)
                for g in range(2):
                    for c in range(5):
                        act.wait_ge(conv_done, l * 10 + (5 * g + c + 1))
                        c0 = SHIFTED[c]
                        if c < 2:
                            act.activation(z[:, g, c0:c0 + CONV], z[:, g, c0:c0 + CONV], ACT.Silu)
                        if c == 4:
                            act.activation(z[:, g, Z_WD:Z_WD + 128], z[:, g, Z_WD:Z_WD + 128], ACT.Tanh)
                            act.activation(z[:, g, Z_GD:Z_GD + 128], z[:, g, Z_GD:Z_GD + 128], ACT.Sigmoid)
                    act.activation(z[:, g, Z_GATE:Z_GATE + 256], z[:, g, Z_GATE:Z_GATE + 256], ACT.Silu
                                   ).then_inc(silu_done, 1)
                act.wait_ge(gates_v, l * 4 + 1)
                act.activation(beta, z[:, :, Z_AB + 8:Z_AB + 16].rearrange("p g (d h) -> p d g h", d=2), ACT.Sigmoid)
                act.activation(sm["nalog"], small["a_log"], ACT.Exp)
                act.activation(sm["t16"], sm["t16"], ACT.Exp)
                act.drain()
                act.activation(sm["t16"], sm["t16"], ACT.Ln, bias=1.0).then_inc(gates_a, 1)
                act.wait_ge(gates_v, l * 4 + 2)
                act.activation(sm["rs"][:, 0:4], sm["st8"][:, 0:4], ACT.Ln)
                act.activation(sm["nqk"], sm["nqk"], ACT.Ln)
                act.drain()
                act.activation(sm["rs"][:, 0:4], sm["rs"][:, 0:4], ACT.Exp, scale=-0.5)
                act.activation(sm["nqk"], sm["nqk"], ACT.Exp, scale=-0.5).then_inc(gates_a, 1)

                act.wait_ge(ckv_ready, l * 3 + 3)
                act.dma_start(new_ckv[0, bass.ds(l, 1), :, :].rearrange("a t c -> (a t) c"), ckvn[:, 0, :]
                              ).then_inc(ckv_out, 16)
                act.dma_start(new_kpe[0, bass.ds(l, 1), :, :].rearrange("a t c -> (a t) c"), kpe[:, 0, :]
                              ).then_inc(ckv_out, 16)
                for g in range(2):
                    name = ("cqT", g)
                    done(act.activation(cqT[:, :, 128 * g:128 * g + 128], v3(f(l, name)[:, 0:384], 3), ACT.Copy), name)
                for blk in range(3):
                    name = ("ckvT", blk)
                    b = f(l, name)
                    act.activation(ckvT[:, :, 128 * blk:128 * blk + 128], v3(b[:, 0:256], 2), ACT.Copy)
                    done(act.activation(kpeT[:, 128 * blk:128 * blk + 128], b[0:64, 256:384], ACT.Copy), name)
                for hp in range(2):
                    name = ("qT", hp)
                    done(act.activation(qT[:, 2 * hp:2 * hp + 2, :, :].rearrange("p h g t -> p (h g t)"), f(l, name),
                                        ACT.Copy), name)
                for g in range(2):
                    name = ("qpeT", g)
                    done(act.activation(qpeT[:, g, :, :].rearrange("p h t -> p (h t)"), f(l, name)[0:64, :],
                                        ACT.Copy), name)
                for h in range(HEADS):
                    name = ("kT", h)
                    done(act.activation(kT[:, h, :], f(l, name)[:, 0:384], ACT.Copy), name)
                act.wait_ge(ckv_out, l * 32 + 32)
                for g in range(2):
                    nk = 1 + g
                    for h in range(HEADS):
                        name = ("score", g, h)
                        act.wait_ge(nmax, l * 8 + (4 * g + h + 1))
                        ins = act.activation(prob[h % 2][:, 0:128 * nk], f(l, name)[:, 0:128 * nk], ACT.Exp,
                                             bias=sm["mx"][:, h:h + 1], scale=MLA_SCALE,
                                             accum_out=sm["sum"][:, h:h + 1])
                        done(ins, name)
                        act.drain()
                        act.nop().then_inc(prob_ready, 1)

                def ainv(pi, p):
                    for d in range(2):
                        name = ("T1", p, d)
                        done(act.activation(Tm[:, d, :, :].rearrange("p h n -> p (h n)"), f(l, name), ACT.Copy), name)
                    for k in range(1, LEVELS):
                        for d in range(2):
                            name = ("X", p, k, d)
                            done(act.activation(XX[:, d, :, :].rearrange("p h n -> p (h n)"), f(l, name), ACT.Copy),
                                 name)

                for pi, p in enumerate(PAIRS):
                    kind, g = p
                    if kind == "gdn":
                        for s in range(2):
                            name = ("qkT", g, s)
                            done(act.activation(qkT[:, s, :, :].rearrange("p h t -> p (h t)"), f(l, name)[0:64, :],
                                                ACT.Copy), name)
                        if g == 0:
                            act.wait_ge(gates_v, l * 4 + 4)
                            act.wait_ge(empty["V"], tiles.emptied(l, ("decay",)))
                            act.activation(sm["egs"], sm["gcs"], ACT.Exp)
                            act.drain()
                            act.nop().then_inc(dec_a, 1)
                        for d in range(2):
                            act.wait_ge(dec_v, l * 4 + (2 * g + d + 1))
                            act.activation(PB[:, d, :, :], PB[:, d, :, :], ACT.Exp, scale=-1.0).then_inc(dec_a, 1)
                        ainv(pi, p)
                        act.wait_ge(fin_v, l * 6 + (3 + g))
                        act.activation(sm["nqk"][:, 0:4], sm["nqk"][:, 0:4], ACT.Ln)
                        act.drain()
                        act.activation(sm["nqk"][:, 0:4], sm["nqk"][:, 0:4], ACT.Exp, scale=-0.5).then_inc(fin_a, 1)
                        if g == 0:
                            act.wait_ge(state_ready, l * 2 + 1)
                            act.dma_start(new_gdn[0, bass.ds(l, 1), :, :, :, :].rearrange("a d h k v -> k (a d h) v"),
                                          v3(sout, 8)).then_inc(state_out, 16)
                            act.dma_start(v3(nat["w2"][0:64, :], 8),
                                          a["state_gdn"][0, bass.ds(l, 1), :, :, :, :].rearrange("a d h k v -> k (a d h) v")
                                          ).then_inc(state_in, 16)
                    else:
                        act.wait_ge(pair_done, l * 4 + pi)
                        if g == 1:
                            act.wait_ge(state_ready, l * 2 + 2)
                            act.dma_start(new_rwkv[0, bass.ds(l, 1), :, :, :, :].rearrange("a d h k v -> k (a d h) v"),
                                          v3(sout, 8)).then_inc(state_out, 16)
                            act.wait_ge(state_out, l * 32 + 32)
                            act.dma_start(v3(nat["Bf"][0:64, :], 8),
                                          a["state_rwkv"][0, bass.ds(l, 1), :, :, :, :].rearrange("a d h k v -> k (a d h) v")
                                          ).then_inc(state_in, 16)
                        else:
                            act.wait_ge(state_out, l * 32 + 16)
                        act.dma_start(w2, a["rwkv_w2"][bass.ds(l, 1), :, :, :].rearrange("a d r c -> r (a d) c")
                                      ).then_inc(lora_in, 16)
                        act.dma_start(a2, a["rwkv_a2"][bass.ds(l, 1), :, :, :].rearrange("a d r c -> r (a d) c")
                                      ).then_inc(lora_in, 16)
                        act.dma_start(nat["g2"], a["rwkv_g2"][bass.ds(l, 1), :, :].rearrange("a r c -> (a r) c")
                                      ).then_inc(lora_in, 16)
                        name = ("wdT", g)
                        done(act.activation(nat["wdT"][0:64, :], f(l, name)[0:64, :], ACT.Copy), name)
                        name = ("gdT", g)
                        done(act.activation(nat["gdT"], f(l, name)[:, 0:128], ACT.Copy), name)
                        act.wait_ge(rw_v, l * 6 + (3 * g + 1))
                        act.activation(nat["lw"], nat["lw"], ACT.Sigmoid)
                        act.activation(nat["a"], nat["a"], ACT.Sigmoid).then_inc(rw_a, 1)
                        name = ("rgate", g)
                        done(act.activation(nat["gate"], f(l, name)[:, 0:256], ACT.Copy), name)
                        act.wait_ge(rw_v, l * 6 + (3 * g + 2))
                        act.activation(sm["nqk"][:, 0:4], sm["nqk"][:, 0:4], ACT.Ln)
                        act.drain()
                        act.activation(sm["nqk"][:, 0:4], sm["nqk"][:, 0:4], ACT.Exp, scale=-0.5)
                        name = ("cum", g)
                        b = f(l, name)
                        act.wait_ge(rw_v, l * 6 + (3 * g + 3))
                        act.activation(E[:, :, :].rearrange("p d n -> p (d n)"), b, ACT.Exp)
                        act.activation(Ex[:, :, :].rearrange("p d n -> p (d n)"),
                                       Ex[:, :, :].rearrange("p d n -> p (d n)"), ACT.Exp)
                        done(act.activation(Ei[:, :, :].rearrange("p d n -> p (d n)"), b, ACT.Exp, scale=-1.0), name)
                        if g == 0:
                            name = ("suf", g)
                            done(act.activation(Fs[:, :, :].rearrange("p d n -> p (d n)"), f(l, name), ACT.Exp), name)
                        act.drain()
                        act.nop().then_inc(rw_a, 1)
                        for d in range(2):
                            for s in ("KTt", "RT", "BT", "KhT"):
                                name = (s, g, d)
                                b = v3(f(l, name)[0:64, :], HEADS)
                                dst = {"KTt": KRT[:, d, :, 0, :], "RT": KRT[:, d, :, 1, :], "BT": BT[:, d, :, :],
                                       "KhT": KTh[:, d, :, :]}[s]
                                done(act.activation(dst, b, ACT.Copy), name)
                        if g:
                            name = ("cc", g)
                            done(act.activation(sm["ecc"][0:64, :], f(l, name)[0:64, 0:8], ACT.Exp), name)
                            name = ("RS", g)
                            done(act.activation(oacc, f(l, name)[:, 0:256], ACT.Copy), name)
                        name = ("R", g)
                        done(act.activation(nat["R"], f(l, name), ACT.Copy, scale=-1.0), name)
                        ainv(pi, p)
                        act.wait_ge(fin_v, l * 6 + (5 + g))
                        act.activation(sm["nqk"][:, 0:4], sm["nqk"][:, 0:4], ACT.Ln)
                        act.drain()
                        act.activation(sm["nqk"][:, 0:4], sm["nqk"][:, 0:4], ACT.Exp, scale=-0.5).then_inc(fin_a, 1)

                for g in range(2):
                    for n in range(2):
                        name = ("mixT", g, n)
                        done(act.activation(hT[:, 4 * n:4 * n + 4, 128 * g:128 * g + 128], v3(f(l, name), 4), ACT.Copy),
                             name)
                act.wait_ge(empty["V"], tiles.emptied(l, ("out", 1, 1)))
                norm(1, l * 2 + 2)
                for g in range(2):
                    act.wait_ge(logit_v, l * 4 + (2 * g + 1))
                    act.activation(sm["scores"], sm["scores"], ACT.Sigmoid).then_inc(logit_a, 1)
                act.wait_ge(logit_v, l * 4 + 4)

                assert cnt[0] == tiles.per["A"]

                def silu(item, g):
                    act.wait_ge(gu_full, item + GU0)
                    act.activation(sg[g], P[:, 4 + g, 0:FF], ACT.Silu).then_inc(silu_e, 1)

                def evict(item, g):
                    act.wait_ge(t_full, item)
                    act.activation(actT[g][:, :, :].rearrange("p f t -> p (f t)"), P[:, 6 + g, 0:256], ACT.Copy
                                   ).then_inc(t_empty, 1)

                silu(l * ITEMS + 1, 0)
                evict(l * ITEMS + 1, 0)
                silu(l * ITEMS + 2, 1)
                with act.Fori(0, EXPERTS) as e:
                    it = l * ITEMS + e * 2
                    evict(it + 2, 1)
                    silu(it + 3, 0)
                    evict(it + 3, 0)
                    silu(it + 4, 1)
                evict(l * ITEMS + ITEMS, 1)

            act.wait_ge(x_done, LAYERS + 1)
            for g in range(2):
                act.activation(PR[:, 0:D], x[:, g, :], ACT.Square, accum_out=sm["ss"][:, g:g + 1])
                act.drain()
                act.nop().then_inc(ss_ready, 1)
            act.wait_ge(ss_eps, 2 * LAYERS + 1)
            act.activation(sm["rs"][:, 0:2], sm["ss"][:, 2:4], ACT.Ln)
            act.drain()
            act.activation(sm["rs"][:, 2:4], sm["rs"][:, 0:2], ACT.Exp, scale=-0.5).then_inc(rs_ready, 1)

        @block.vector
        def _(dve):
            def f(l, name):
                dve.wait_ge(filled, tiles.filled(l, name))
                return P[:, tiles.index[name] % 8, :]

            def done(ins, name):
                i = tiles.index[name]
                assert tiles.who[name] == "V" and tiles.rank[name] == cnt[0] + 1, name
                cnt[0] += 1
                ins.then_inc(empty["V"], 1)

            def tt(out, p, q, op):
                return dve.tensor_tensor(out, p, q, op)

            cnt = [0]
            dve.wait_ge(x_in, 32)
            dve.wait_ge(const_in, 16)
            dve.nop().then_inc(x_done, 1)

            def norm(n):
                dve.wait_ge(ss_ready, n * 2 + 2)
                dve.tensor_scalar(sm["ss"][:, 2:4], sm["ss"][:, 0:2], 1.0 / D, EPS, ALU.mult, ALU.add
                                  ).then_inc(ss_eps, 1)
                dve.wait_ge(rs_ready, n + 1)

            with dve.Fori(0, LAYERS) as l:
                cnt[0] = 0

                def normalise(n, which):
                    norm(n)
                    for g in range(2):
                        dve.tensor_scalar((xs, xs1)[which == 0][:, g, :], x[:, g, :], sm["rs"][:, 2 + g:3 + g], None,
                                          ALU.mult).then_inc(xn_ready, 1)
                    for g in range(2):
                        for h in range(2):
                            name = (f"h{which + 1}", g, h)
                            b = f(l, name)
                            for k in range(4):
                                kk = 4 * h + k
                                last = dve.tensor_scalar(hT[:, kk, 128 * g:128 * g + 128], b[:, 128 * k:128 * k + 128],
                                                         modT[:, 2 * which + 1, kk, g:g + 1],
                                                         modT[:, 2 * which, kk, g:g + 1], ALU.mult, ALU.add)
                            done(last, name)

                dve.wait_ge(adab_in, l * 48 + 48)
                for n in range(12):
                    name = ("mods", n)
                    c0 = 512 * n
                    done(tt(mods[:, c0:c0 + 512], f(l, name)[0:2, :], ada_b[:, c0:c0 + 512], ALU.add), name)
                name = ("modT",)
                b = f(l, name)
                dve.tensor_copy(sm["modT"], b[:, 0:64])
                done(dve.tensor_copy(sm["nT"], b[:, 64:80]), name)
                dve.drain()
                for w in range(2):
                    s = modT[:, 2 * w + 1, :, :]
                    n3 = wide(sm["nT"][:, 8 * w:8 * w + 8], 2)
                    dve.tensor_scalar(s, s, 1.0, None, ALU.add)
                    dve.drain()
                    tt(s, s, n3, ALU.mult)
                    dve.drain()
                dve.wait_ge(mix_in, l * 80 + 80)
                c0 = mix3[:, 2, 768:1920]
                tt(c0, mix3[:, 0, 768:1920], mix3[:, 1, 768:1920], ALU.add)
                dve.drain()
                dve.tensor_scalar(c0, c0, -1.0, 1.0, ALU.mult, ALU.add).then_inc(mix_c, 1)
                normalise(l * 2, 0)

                for g in range(2):
                    for c, c0 in enumerate(SHIFTED):
                        m0 = CONV * c
                        bp, bn = f(l, ("zp", g, c)), f(l, ("zn", g, c))
                        done(tt(conv_t[0], bp[:, 0:CONV], mix3[:, 0, m0:m0 + CONV], ALU.mult), ("zp", g, c))
                        done(tt(conv_t[1], bn[:, 0:CONV], mix3[:, 1, m0:m0 + CONV], ALU.mult), ("zn", g, c))
                        dve.drain()
                        tt(conv_t[0], conv_t[0], conv_t[1], ALU.add)
                        dve.drain()
                        dve.wait_ge(z_mid, l * 10 + (5 * g + c + 1))
                        tt(z[:, g, c0:c0 + CONV], z[:, g, c0:c0 + CONV], conv_t[0], ALU.add).then_inc(conv_done, 1)
                        dve.drain()

                dve.wait_ge(small_in, l * (16 * 13) + 16 * 13)
                dve.wait_ge(gates_a, l * 3 + 1)
                dtb = small["dt"].rearrange("p (d a h) -> p d a h", d=2, a=1).to_broadcast([128, 2, 2, 4])
                tt(gg, z[:, :, Z_AB:Z_AB + 8].rearrange("p g (d h) -> p d g h", d=2), dtb, ALU.add)
                dve.drain()
                dve.scalar_tensor_tensor(out=sm["t16"], in0=sm["gg"], scalar=-1.0, in1=sm["gg"], op0=ALU.mult,
                                         op1=ALU.min).then_inc(gates_v, 1)
                for g in range(2):
                    dve.tensor_scalar(sm["st8"][:, 2 * g:2 * g + 1], sm["ss"][:, 4 * g:4 * g + 1], 1.0 / QL, EPS,
                                      ALU.mult, ALU.add)
                    dve.tensor_scalar(sm["st8"][:, 2 * g + 1:2 * g + 2], sm["ss"][:, 4 * g + 1:4 * g + 2], 1.0 / KVL,
                                      EPS, ALU.mult, ALU.add)
                dve.wait_ge(silu_done, l * 2 + 2)
                for g in range(2):
                    qk = z[:, g, Z_G:Z_G + 512]
                    tt(sq, qk, qk, ALU.mult)
                    dve.drain()
                    dve.tensor_reduce(sm["nqk"][:, 8 * g:8 * g + 8], v3(sq, 8), AX, ALU.add)
                    dve.drain()
                dve.tensor_scalar(sm["nqk"], sm["nqk"], EPS, None, ALU.add).then_inc(gates_v, 1)
                dve.wait_ge(gates_a, l * 3 + 2)
                dve.scalar_tensor_tensor(out=sm["gg"], in0=sm["gg"], scalar=0.0, in1=sm["t16"], op0=ALU.max,
                                         op1=ALU.add)
                dve.tensor_scalar(sm["nalog"], sm["nalog"], -1.0, None, ALU.mult)
                dve.drain()
                nal = sm["nalog"].rearrange("p (d a h) -> p d a h", d=2, a=1).to_broadcast([128, 2, 2, 4])
                tt(gg, gg, nal, ALU.mult).then_inc(gates_v, 1)
                dve.wait_ge(gates_a, l * 3 + 3)
                for g in range(2):
                    dve.scalar_tensor_tensor(out=cqn[:, g, :], in0=z[:, g, 0:QL], scalar=sm["rs"][:, 2 * g:2 * g + 1],
                                             in1=small["q_norm"], op0=ALU.mult, op1=ALU.mult).then_inc(cq_ready, 1)
                for blk, g in ((0, 0), (1, None), (2, 1)):
                    if g is None:
                        dve.wait_ge(ctx_in, l * 32 + 32)
                        dve.nop().then_inc(ckv_ready, 1)
                        continue
                    kp = z[:, g, QL + KVL:P_MLA]
                    if g == 0:
                        dve.tensor_copy(kpe[:, 0, :], kp)
                    else:
                        q4 = kp.rearrange("p (a s n) -> p a s n", a=2, s=2)
                        r4 = rt[:, 0, 0:64].rearrange("p (a s n) -> p a s n", a=2, s=2)
                        s4 = cst("sin").rearrange("p (a s n) -> p a s n", a=2, s=2)
                        for s in range(2):
                            tt(r4[:, :, s, :], q4[:, :, 1 - s, :], s4[:, :, s, :], ALU.mult)
                        tt(kpe[:, 2, :], kp, cst("cos"), ALU.mult)
                        dve.drain()
                        tt(kpe[:, 2, :], kpe[:, 2, :], rt[:, 0, 0:64], ALU.add)
                    dve.scalar_tensor_tensor(out=ckvn[:, blk, :], in0=z[:, g, QL:QL + KVL],
                                             scalar=sm["rs"][:, 2 * g + 1:2 * g + 2], in1=small["kv_norm"],
                                             op0=ALU.mult, op1=ALU.mult).then_inc(ckv_ready, 1)
                for g in range(2):
                    dve.tensor_scalar(sm["nqk"][:, 8 * g:8 * g + 4], sm["nqk"][:, 8 * g:8 * g + 4], N ** -0.5, None,
                                      ALU.mult)
                dve.drain()
                for g in range(2):
                    qk = v3(z[:, g, Z_G:Z_G + 512], 8)
                    tt(qk, qk, wide(sm["nqk"][:, 8 * g:8 * g + 8], 64), ALU.mult).then_inc(fin_v, 1)
                dve.nop().then_inc(gates_v, 1)
                name = ("decay",)
                done(dve.tensor_copy(sm["gcs"], f(l, name)[:, 0:32]), name)

                for g in range(2):
                    name = ("qpe", g)
                    b = f(l, name)
                    if g == 0:
                        ins = dve.tensor_copy(qpe[:, 0, :], b[:, 0:256])
                        done(ins, name)
                        dve.drain()
                        dve.nop().then_inc(qpe_ready, 1)
                    else:
                        dve.tensor_copy(rt[:, 1, 0:256], b[:, 0:256])
                        dve.drain()
                        src = rt[:, 1, 0:256].rearrange("p (h a s n) -> p (h a) s n", h=4, a=2, s=2)
                        dst = rt[:, 0, 0:256].rearrange("p (h a s n) -> p (h a) s n", h=4, a=2, s=2)
                        s4 = cst("sin").rearrange("p (x a s n) -> p x a s n", x=1, a=2, s=2)
                        for h in range(HEADS):
                            for s in range(2):
                                tt(dst[:, 2 * h:2 * h + 2, s, :], src[:, 2 * h:2 * h + 2, 1 - s, :],
                                   cst("sin").rearrange("p (a s n) -> p a s n", a=2, s=2)[:, :, s, :], ALU.mult)
                        tt(v3(qpe[:, 1, :], 4), v3(rt[:, 1, 0:256], 4), many(cst("cos"), 4), ALU.mult)
                        dve.drain()
                        tt(qpe[:, 1, :], qpe[:, 1, :], rt[:, 0, 0:256], ALU.add).then_inc(qpe_ready, 1)
                        done(dve.nop(), name)
                for blk in range(3):
                    name = ("v", blk)
                    done(dve.tensor_copy(vv[:, blk, :], f(l, name)), name)
                for g in range(2):
                    nk = 1 + g
                    for h in range(HEADS):
                        b = f(l, ("score", g, h))
                        dve.tensor_reduce(sm["st8"][:, h:h + 1], b[:, 0:128 * nk], AX, ALU.max)
                        dve.drain()
                        dve.tensor_scalar(sm["mx"][:, h:h + 1], sm["st8"][:, h:h + 1], -MLA_SCALE, None, ALU.mult
                                          ).then_inc(nmax, 1)
                        name = ("pT", g, h)
                        done(dve.tensor_copy(pT[h % 2][:, 0:nk, :].rearrange("p k t -> p (k t)"),
                                             f(l, name)[:, 0:128 * nk]), name)
                        dve.wait_ge(prob_ready, l * 8 + (4 * g + h + 1))
                        dve.reciprocal(sm["st8"][:, 4:5], sm["sum"][:, h:h + 1])
                        dve.drain()
                        name = ("mla", g, h)
                        done(dve.tensor_scalar(z[:, g, 128 * h:128 * h + 128], f(l, name)[:, 0:128], sm["st8"][:, 4:5],
                                               None, ALU.mult), name)
                        dve.drain()

                def solve(pi, p):
                    dve.wait_ge(lm_ready, l * 4 * LEVELS + (pi * LEVELS + 1))
                    for d in range(2):
                        last = tt(TT[:, d, :, :], many(ident, HEADS), Lm[0][:, d, :, :], ALU.subtract)
                    last.then_inc(tt_ready, 1)
                    for k in range(1, LEVELS):
                        for d in range(2):
                            if k < LEVELS - 1:
                                name = ("Y", p, k, d)
                                if d == 0:
                                    dve.drain()
                                b = v3(f(l, name), HEADS)
                                done(tt(Tm[:, d, :, :], Tm[:, d, :, :], b, ALU.subtract), name)
                            elif d == 0:
                                dve.drain()
                            name = ("YT", p, k, d)
                            b = v3(f(l, name), HEADS)
                            done(tt(TT[:, d, :, :], TT[:, d, :, :], b, ALU.subtract), name)

                for pi, p in enumerate(PAIRS):
                    kind, g = p
                    if kind == "gdn":
                        if g == 0:
                            dve.wait_ge(filled, tiles.filled(l, ("mla", 1, 3)))
                        for d in range(2):
                            for h in range(HEADS):
                                last = dve.tensor_scalar(gtri[:, d, h, :], cst(f"tri{d}"), gg[:, d, g, h:h + 1], None,
                                                         ALU.mult)
                        last.then_inc(gtri_ready, 1)
                        for d in range(2):
                            name = ("row", g, d)
                            b = f(l, name)
                            for h in range(HEADS):
                                last = dve.tensor_scalar(PB[:, d, h, :], b[:, 128 * h:128 * h + 128],
                                                         gc[:, d, g, h:h + 1], -1.0, ALU.subtract, ALU.mult)
                            done(last, name)
                            dve.drain()
                            dve.tensor_scalar(PB[:, d, :, :], PB[:, d, :, :], 0.0, None, ALU.max).then_inc(dec_v, 1)
                        for d in range(2):
                            dve.wait_ge(dec_a, l * 5 + (2 + 2 * g + d))
                            tt(PB[:, d, :, :], PB[:, d, :, :], many(cst(f"tri{d}"), HEADS), ALU.mult)
                        dve.drain()
                        b = f(l, ("kk", g))
                        for d in range(2):
                            for h in range(HEADS):
                                last = dve.scalar_tensor_tensor(out=AT[:, d, h, :], in0=b[:, 128 * h:128 * h + 128],
                                                                scalar=beta[:, d, g, h:h + 1], in1=PB[:, d, h, :],
                                                                op0=ALU.mult, op1=ALU.mult)
                        done(last, ("kk", g))
                        b = v3(f(l, ("qk", g)), HEADS)
                        for d in range(2):
                            last = tt(PK[:, d, :, :], b, PB[:, d, :, :], ALU.mult)
                        done(last, ("qk", g))
                        dve.drain()
                        dve.nop().then_inc(at_ready, 1)
                        vg = v3(z[:, g, Z_G + 512:Z_G + 768], HEADS)
                        if g == 0:
                            for d in range(2):
                                last = dve.tensor_copy(R[:, d, :, :], vg)
                            last.then_inc(rhs_ready, 1)
                            kg = v3(z[:, g, Z_G + 256:Z_G + 512], HEADS)
                            for d in range(2):
                                last = tt(kdec[:, d, :, :], kg, wide(egs[:, d, g, :], 64), ALU.mult)
                            last.then_inc(kdec_ready, 1)
                        else:
                            b = u4(f(l, ("kS", g)))
                            for d in range(2):
                                last = tt(R[:, d, :, :], b[:, d, :, :], wide(egc[:, d, g, :], 64), ALU.mult)
                            done(last, ("kS", g))
                            dve.drain()
                            for d in range(2):
                                last = tt(R[:, d, :, :], vg, R[:, d, :, :], ALU.subtract)
                            last.then_inc(rhs_ready, 1)
                            b = u4(f(l, ("qS", g)))
                            tt(v3(oacc, HEADS), b[:, 0, :, :], wide(egc[:, 0, g, :], 64), ALU.mult)
                            done(tt(v3(sq[:, 0:256], HEADS), b[:, 1, :, :], wide(egc[:, 1, g, :], 64), ALU.mult),
                                 ("qS", g))
                            dve.drain()
                            tt(oacc, oacc, sq[:, 0:256], ALU.add)
                            dve.drain()
                        solve(pi, p)
                        b = u4(f(l, ("W", p)))
                        for d in range(2):
                            last = tt(SA[:, d, :, :], b[:, d, :, :], wide(beta[:, d, g, :], 64), ALU.mult)
                        done(last, ("W", p))
                        b = f(l, ("O", p))
                        if g:
                            ins = tt(oacc, b[:, 0:256], oacc, ALU.add)
                        else:
                            ins = dve.tensor_copy(oacc, b[:, 0:256])
                        done(ins, ("O", p))
                        dve.drain()
                        tt(sq[:, 0:256], oacc, oacc, ALU.mult)
                        dve.drain()
                        dve.tensor_reduce(sm["st8"][:, 0:4], v3(sq[:, 0:256], HEADS), AX, ALU.add)
                        dve.drain()
                        dve.tensor_scalar(sm["nqk"][:, 0:4], sm["st8"][:, 0:4], 1.0 / N, EPS, ALU.mult, ALU.add
                                          ).then_inc(fin_v, 1)
                        tt(v3(sq[:, 0:256], HEADS), v3(z[:, g, Z_GATE:Z_GATE + 256], HEADS),
                           many(small["gdn_norm"], HEADS), ALU.mult)
                        dve.drain()
                        tt(oacc, oacc, sq[:, 0:256], ALU.mult)
                        dve.drain()
                        dve.wait_ge(fin_a, l * 4 + (pi + 1))
                        tt(v3(z[:, g, Z_G:Z_G + 256], HEADS), v3(oacc, HEADS), wide(sm["nqk"][:, 0:4], 64), ALU.mult)
                        if g == 0:
                            name = ("S", p)
                            done(dve.tensor_copy(sout, f(l, name)[0:64, :]), name)
                            dve.drain()
                            dve.nop().then_inc(state_ready, 1)
                        dve.drain()
                        dve.nop().then_inc(pair_done, 1)
                        continue

                    r, k_, v_ = (z[:, g, c0:c0 + 256] for c0 in (Z_R, Z_K, Z_V))

                    name = ("wpre", g)
                    done(tt(nat["lw"], f(l, name), small["w0"], ALU.add), name)
                    name = ("apre", g)
                    done(tt(nat["a"], f(l, name), small["a0"], ALU.add), name)
                    dve.drain()
                    dve.nop().then_inc(rw_v, 1)
                    kk = nat["kk"]
                    tt(kk, k_, small["k_k"], ALU.mult)
                    dve.drain()
                    tt(sq[:, 0:256], kk, kk, ALU.mult)
                    dve.drain()
                    dve.tensor_reduce(sm["st8"][:, 0:4], v3(sq[:, 0:256], HEADS), AX, ALU.add)
                    dve.drain()
                    dve.tensor_scalar(sm["nqk"][:, 0:4], sm["st8"][:, 0:4], EPS, None, ALU.add).then_inc(rw_v, 1)
                    dve.wait_ge(rw_a, l * 4 + (2 * g + 1))
                    dve.tensor_scalar(nat["lw"], nat["lw"], -float(np.exp(-0.5)), None, ALU.mult).then_inc(rwp, 1)
                    ka = many(small["k_a"], 2)
                    dve.scalar_tensor_tensor(out=kd, in0=aa, scalar=-1.0, in1=ka, op0=ALU.add, op1=ALU.mult)
                    dve.drain()
                    tt(kd, kd, many(k_, 2), ALU.mult)
                    dve.drain()
                    tt(kd, kd, many(k_, 2), ALU.add)
                    b = v3(f(l, ("cum", g)), 2)
                    tt(Ex, b, lw, ALU.subtract)
                    dve.drain()
                    dve.nop().then_inc(rw_v, 1)
                    dve.wait_ge(rw_a, l * 4 + (2 * g + 2))
                    tt(v3(kk, HEADS), v3(kk, HEADS), wide(sm["nqk"][:, 0:4], 64), ALU.mult)
                    dve.drain()
                    tt(aa, aa, many(kk, 2), ALU.mult)
                    dve.drain()
                    tt(Rt, many(r, 2), E, ALU.mult)
                    tt(Ktl, many(kk, 2), Ex, ALU.mult)
                    tt(Bh, aa, Ei, ALU.mult)
                    tt(Kh, kd, Ei, ALU.mult).then_inc(rwp, 1)
                    if g == 0:
                        tt(Bf, aa, Fs, ALU.mult)
                        tt(Kf, kd, Fs, ALU.mult)
                    tt(sq[:, 256:512], r, small["r_k"], ALU.mult)
                    tt(sq[:, 0:256], kd[:, 0, :], kd[:, 1, :], ALU.add)
                    dve.drain()
                    tt(sq[:, 0:256], sq[:, 0:256], sq[:, 256:512], ALU.mult)
                    dve.drain()
                    dve.tensor_reduce(sm["st8"][:, 8:12], v3(sq[:, 0:256], HEADS), AX, ALU.add)
                    dve.drain()
                    for d in range(2):
                        for hp in range(2):
                            for s, (low, high) in (("PB", (AT, PB)), ("PK", (MT, PK))):
                                name = (s, g, d, hp)
                                b = f(l, name).rearrange("p (h s t) -> p h s t", h=2, s=2)
                                hs = slice(2 * hp, 2 * hp + 2)
                                tt(low[:, d, hs, :], b[:, :, 0, :], many(cst(f"strict{d}"), 2), ALU.mult)
                                done(tt(high[:, d, hs, :], b[:, :, 1, :], many(cst(f"tri{d}"), 2), ALU.mult), name)
                    dve.drain()
                    dve.nop().then_inc(at_ready, 1)
                    if g:
                        name = ("S0T", g)
                        b = f(l, name)
                        dve.wait_ge(empty["A"], tiles.emptied(l, ("cc", g)))
                        done(tt(v3(nat["Kf"][0:64, :], 8), v3(b[0:64, :], 8), wide(sm["ecc"][0:64, :], 64), ALU.mult),
                             name)
                    solve(pi, p)
                    name = ("W", p)
                    done(dve.tensor_copy(nat["SA"], f(l, name)), name)
                    b = f(l, ("O", p))
                    if g:
                        ins = tt(oacc, b[:, 0:256], oacc, ALU.add)
                    else:
                        ins = dve.tensor_copy(oacc, b[:, 0:256])
                    done(ins, ("O", p))
                    dve.drain()
                    o4 = v3(oacc, HEADS)
                    dve.tensor_reduce(sm["st8"][:, 0:4], o4, AX, ALU.add)
                    dve.drain()
                    dve.tensor_scalar(sm["st8"][:, 0:4], sm["st8"][:, 0:4], 1.0 / N, None, ALU.mult)
                    dve.drain()
                    tt(o4, o4, wide(sm["st8"][:, 0:4], 64), ALU.subtract)
                    dve.drain()
                    tt(sq[:, 0:256], oacc, oacc, ALU.mult)
                    dve.drain()
                    dve.tensor_reduce(sm["st8"][:, 4:8], v3(sq[:, 0:256], HEADS), AX, ALU.add)
                    dve.drain()
                    dve.tensor_scalar(sm["nqk"][:, 0:4], sm["st8"][:, 4:8], 1.0 / N, GN_EPS, ALU.mult, ALU.add
                                      ).then_inc(fin_v, 1)
                    tt(v3(sq[:, 0:256], HEADS), v3(v_, HEADS), wide(sm["st8"][:, 8:12], 64), ALU.mult)
                    dve.drain()
                    tt(sq[:, 0:256], sq[:, 0:256], small["gn_b"], ALU.add)
                    tt(oacc, oacc, small["gn_w"], ALU.mult)
                    dve.drain()
                    dve.wait_ge(fin_a, l * 4 + (pi + 1))
                    tt(o4, o4, wide(sm["nqk"][:, 0:4], 64), ALU.mult)
                    dve.drain()
                    tt(oacc, oacc, sq[:, 0:256], ALU.add)
                    dve.drain()
                    ins = tt(r, oacc, nat["gate"], ALU.mult)
                    if g == 0:
                        name = ("S", p)
                        done(dve.tensor_copy(sout, f(l, name)[0:64, :]), name)
                        dve.drain()
                        dve.nop().then_inc(state_ready, 1)
                    dve.drain()
                    dve.nop().then_inc(mixed, 1)
                    dve.nop().then_inc(pair_done, 1)

                for n in range(2):
                    for g in range(2):
                        name = ("out", n, g)
                        cols = slice(512 * n, 512 * n + 512)
                        tt(xs[:, g, cols], f(l, name), gateB[:, 0, g, cols], ALU.mult)
                        dve.drain()
                        done(tt(x[:, g, cols], x[:, g, cols], xs[:, g, cols], ALU.add), name)
                        dve.drain()
                normalise(l * 2 + 1, 1)

                for g in range(2):
                    name = ("route", g)
                    done(dve.tensor_copy(sm["scores"], f(l, name)[:, 0:EXPERTS]), name)
                    dve.drain()
                    dve.nop().then_inc(logit_v, 1)
                    dve.wait_ge(logit_a, l * 2 + (g + 1))
                    sel, w64, st = sm["sel"], sm["w64"], sm["st8"]
                    tt(sel, sm["scores"], small["bias"], ALU.add)
                    dve.drain()
                    for q in range(8):
                        dve.max(w64[:, 8 * q:8 * q + 8], sel[:, 8 * q:8 * q + 8])
                    dve.drain()
                    top = v3(w64, 8)
                    grp = st[:, 0:8]
                    tt(grp.rearrange("p (k a) -> p k a", a=1), top[:, :, 0:1], top[:, :, 1:2], ALU.add)
                    dve.drain()
                    tt(v3(w64, 8), many(grp, 8), wide(grp, 8), ALU.is_equal)
                    tt(v3(PR[:, 0:64], 8), many(grp, 8), wide(grp, 8), ALU.is_gt)
                    dve.drain()
                    tt(w64, w64, cst("before"), ALU.mult)
                    dve.drain()
                    tt(w64, w64, PR[:, 0:64], ALU.add)
                    dve.drain()
                    dve.tensor_reduce(st[:, 8:16], v3(w64, 8), AX, ALU.add)
                    dve.drain()
                    dve.tensor_scalar(st[:, 8:16], st[:, 8:16], 4.0, -BIG, ALU.is_ge, ALU.mult)
                    dve.drain()
                    tt(v3(sel, 8), v3(sel, 8), wide(st[:, 8:16], 8), ALU.add)
                    dve.drain()
                    dve.max(st[:, 16:24], sel)
                    dve.drain()
                    dve.match_replace(out=w64, in_to_replace=st[:, 16:24], in_values=sel, imm_value=-3 * BIG)
                    dve.drain()
                    tt(w64, w64, sel, ALU.not_equal)
                    dve.drain()
                    tt(w64, w64, sm["scores"], ALU.mult)
                    dve.drain()
                    dve.tensor_reduce(st[:, 0:1], w64, AX, ALU.add)
                    dve.drain()
                    dve.reciprocal(st[:, 1:2], st[:, 0:1])
                    dve.drain()
                    dve.tensor_scalar(comb[:, g, :], w64, st[:, 1:2], ROUTE_SCALE, ALU.mult, ALU.mult
                                      ).then_inc(logit_v, 1)
                    dve.drain()

                assert cnt[0] == tiles.per["V"]

                for g in range(2):
                    dve.wait_ge(silu_e, l * ITEMS + (g + 1))
                    tt(act_[g], P[:, 4 + g, FF:2 * FF], sg[g], ALU.mult).then_inc(act_done, 1)
                with dve.Fori(0, EXPERTS) as e:
                    for g in range(2):
                        dve.wait_ge(silu_e, l * ITEMS + e * 2 + (g + 3))
                        dve.scalar_tensor_tensor(out=act_[g], in0=P[:, 4 + g, FF:2 * FF],
                                                 scalar=comb[:, g, bass.ds(e, 1)], in1=sg[g], op0=ALU.mult,
                                                 op1=ALU.mult).then_inc(act_done, 1)
                dve.wait_ge(y_full, l + 1)
                for g in range(2):
                    for n in range(2):
                        cols = slice(512 * n, 512 * n + 512)
                        tt(xs[:, g, cols], P[:, 2 * g + n, :], gateB[:, 1, g, cols], ALU.mult)
                        dve.drain()
                        last = tt(x[:, g, cols], x[:, g, cols], xs[:, g, cols], ALU.add)
                last.then_inc(x_done, 1)
                dve.drain()

            norm(2 * LAYERS)
            dve.wait_ge(normf_in, 16)
            for g in range(2):
                dve.scalar_tensor_tensor(out=xo[:, g, :], in0=x[:, g, :], scalar=sm["rs"][:, 2 + g:3 + g], in1=normf,
                                         op0=ALU.mult, op1=ALU.mult).then_inc(y_ready, 1)

        @block.gpsimd
        def _(pool):
            pool.wait_ge(const_in, 16)
            with pool.Fori(0, LAYERS) as l:
                pool.wait_ge(mix_c, l + 1)
                for g in range(2):
                    for c, c0 in enumerate(SHIFTED):
                        pool.wait_ge(filled, tiles.filled(l, ("zn", g, c)))
                        zc = z[:, g, c0:c0 + CONV]
                        pool.tensor_tensor(zc, zc, mix3[:, 2, CONV * c:CONV * c + CONV], ALU.mult).then_inc(z_mid, 1)
                for pi, p in enumerate(PAIRS):
                    for k in range(LEVELS):
                        if k == 0:
                            pool.wait_ge(at_ready, l * 4 + (pi + 1))
                            pool.wait_ge(filled, tiles.filled(l, ("kk", p[1]) if p[0] == "gdn" else ("R", p[1])))
                        elif k == 1:
                            pass
                        elif k == 2:
                            pool.wait_ge(tt_ready, l * 4 + (pi + 1))
                        else:
                            pool.wait_ge(filled, tiles.filled(l, ("X", p, k - 2, 1)))
                        for d in range(2):
                            last = pool.tensor_tensor(Lm[k % 2][:, d, :, :], AT[:, d, :, :],
                                                      many(cst(f"level{k}_{d}"), HEADS), ALU.mult)
                        last.then_inc(lm_ready, 1)


_INS = ["x_prompt", "x_sample", "cache_mla_ckv", "cache_mla_kpe", "state_gdn", "state_rwkv", "c", "c_ctx", "ada_w",
        "ada_b", "norm1", "w_in", "mla_q_norm", "mla_w_uq", "mla_kv_norm", "mla_w_ukv", "gdn_conv", "gdn_a_log",
        "gdn_dt_bias", "gdn_norm", "rwkv_mu_prev", "rwkv_mu_next", "rwkv_w0", "rwkv_w2", "rwkv_a0", "rwkv_a2",
        "rwkv_g2", "rwkv_k_k", "rwkv_k_a", "rwkv_r_k", "rwkv_gn_w", "rwkv_gn_b", "w_out", "norm2", "moe_router",
        "moe_bias", "moe_w_gu", "moe_w_down", "shared_w_gu", "shared_w_down", "norm_f"]
_OUTS = [(1, T, D), (1, T, D), (1, LAYERS, T, KVL), (1, LAYERS, T, ROPE), (1, LAYERS, 2, HEADS, N, N),
         (1, LAYERS, 2, HEADS, N, N)]


def kernel(**inputs):
    import concourse.bacc as _bacc
    from concourse.bass_utils import run_bass_kernel_spmd as _run

    nc = _bacc.Bacc("TRN2", target_bir_lowering=False, num_devices=1)
    arrays, args = {}, {}
    for name in _INS:
        arr = np.ascontiguousarray(inputs[name])
        arrays[f"in_{name}"] = arr
        args[name] = nc.dram_tensor(f"in_{name}", arr.shape, mybir.dt.from_np(arr.dtype), kind="ExternalInput").ap()
    table = constants()
    arrays["shape_constants"] = table
    consts = nc.dram_tensor("shape_constants", table.shape, F32, kind="ExternalInput").ap()
    outs = [nc.dram_tensor(f"out_{i}", s, F32, kind="ExternalOutput").ap() for i, s in enumerate(_OUTS)]
    build(nc, args, consts, outs)
    r = _run(nc, [arrays], core_ids=[0])
    return tuple(r.results[0][f"out_{i}"] for i in range(len(_OUTS)))
```

```python
from contextlib import ExitStack

import numpy as np

import concourse.bass as bass
from concourse import mybir

F32 = mybir.dt.float32
I32 = mybir.dt.int32
BF16 = mybir.dt.bfloat16
U32 = mybir.dt.uint32
ALU = mybir.AluOpType
ACT = mybir.ActivationFunctionType
AX = mybir.AxisListType.X

T = 128
D = 1024
KD = D // 128
LAYERS = 2
EPS = 1e-6

HEADS = 4
NOPE, ROPE, VDIM = 128, 64, 128
QL, KVL = 384, 256
MLA_SCALE = (NOPE + ROPE) ** -0.5
GRID_W = 64
ROPE_BASE = 10000.0

N = 64
GN_EPS = 64e-5
P_MLA = QL + KVL + ROPE
Z_G = P_MLA
Z_GATE = Z_G + 3 * HEADS * N
Z_AB = Z_GATE + HEADS * N
Z_R = Z_AB + 4 * HEADS
Z_K, Z_V = Z_R + 256, Z_R + 512
Z_WD, Z_AD, Z_GD = Z_R + 768, Z_R + 896, Z_R + 1024
P_IN = Z_R + 1152
ZC = 6
ZW = [512] * 5 + [P_IN - 2560]

EXPERTS = 64
FF = 256
ROUTE_SCALE = 2.5
TOP_K = 8
BIG = 1e30
CAP = 96
PASSES = -(-2 * T // CAP)
NOWHERE = 8192.0

LEVELS = 7
CONV = 384
SHIFTED = [Z_G + CONV * c for c in range(2)] + [Z_R + CONV * c for c in range(3)]

CONSTS = {}
CW = 0
for _n, _w in [("ident", 128), ("ones", 128), ("tri0", 128), ("tri1", 128), ("strict0", 128), ("strict1", 128),
               ("cen0", 128), ("cen1", 128), ("prev", 128), ("next", 128), ("half0", 1), ("half1", 1),
               ("cos", 64), ("sin", 64), ("before", 64), ("iota", 128), ("token", 4), ("first_row", 64)] + \
              [(f"level{k}_{d}", 128) for k in range(LEVELS) for d in range(2)]:
    CONSTS[_n] = (CW, _w)
    CW += _w


def constants():
    p, f = np.arange(T)[:, None], np.arange(T)[None, :]
    c = {"ident": p == f, "ones": np.ones((T, T)), "tri0": p <= f, "tri1": p >= f, "strict0": p < f,
         "strict1": p > f, "cen0": (p <= f) * 1.0 - (p < T // 2), "cen1": (p >= f) * 1.0 - (p >= T // 2),
         "prev": p == f - 1, "next": p == f + 1, "half0": p < T // 2, "half1": p >= T // 2}
    half = ROPE // 2
    inv = ROPE_BASE ** (-np.arange(0, half, 2) / half)
    ang = np.stack([(p // GRID_W) * inv[None], (p % GRID_W) * inv[None]], 1)
    c["cos"] = np.stack([np.cos(ang)] * 2, 2).reshape(T, ROPE)
    c["sin"] = np.stack([-np.sin(ang), np.sin(ang)], 2).reshape(T, ROPE)
    i, j = np.arange(8)[:, None], np.arange(8)[None, :]
    c["iota"] = f + 0 * p
    c["token"] = np.concatenate([p + 1, 0 * p, p + 1, 0 * p + T], 1)
    c["first_row"] = CAP * np.arange(EXPERTS)[None, :] + 1 + 0 * p
    c["before"] = np.broadcast_to((j < i).reshape(1, 64), (T, 64))
    for k in range(LEVELS):
        L = 1 << k
        m = (p // (2 * L) == f // (2 * L)) & (p // L % 2 == 0) & (f // L % 2 == 1)
        c[f"level{k}_0"], c[f"level{k}_1"] = m, m.T
    return np.concatenate([np.asarray(c[n], np.float32).reshape(T, -1) for n in CONSTS], 1)


PAIRS = [("gdn", 0), ("gdn", 1), ("rwkv", 0), ("rwkv", 1)]


def plan():
    t = []
    t += [(("mods", n), "V") for n in range(12)]
    t += [(("modT",), "V")]
    t += [(("gate", w, g, n), "A") for w in range(2) for g in range(2) for n in range(2)]
    t += [(("h1", g, n), "V") for g in range(2) for n in range(2)]
    t += [(("z", c, g), "A") for c in range(ZC) for g in range(2)]
    t += [((s, g, c), "V") for g in range(2) for c in range(5) for s in ("zp", "zn")]
    t += [(("decay",), "V")]
    t += [(("cqT", g), "A") for g in range(2)] + [(("ckvT", b), "A") for b in range(3)]
    t += [(("qT", k), "A") for k in range(2)] + [(("qpe", g), "V") for g in range(2)]
    t += [(("qpeT", g), "A") for g in range(2)]
    t += [(("kT", h), "A") for h in range(HEADS)] + [(("v", b), "V") for b in range(3)]
    for g in range(2):
        for h in range(HEADS):
            t += [(("score", g, h), "A"), (("pT", g, h), "V"), (("mla", g, h), "V")]
    for kind, g in PAIRS:
        p = (kind, g)
        if kind == "gdn":
            t += [(("qkT", g, s), "A") for s in range(2)] + [(("row", g, d), "V") for d in range(2)]
            t += [(("kk", g), "V"), (("qk", g), "V")]
            t += [(("kS", g), "V"), (("qS", g), "V")] * g
        else:
            t += [(("wdT", g), "A"), (("gdT", g), "A"), (("wpre", g), "V"), (("apre", g), "V"), (("rgate", g), "A")]
            t += [(("cum", g), "A")] + [(("suf", g), "A")] * (1 - g)
            t += [((s, g, d), "A") for d in range(2) for s in ("KTt", "RT", "BT", "KhT")]
            t += [((s, g, d, hp), "V") for d in range(2) for hp in range(2) for s in ("PB", "PK")]
            t += [(("cc", g), "A"), (("S0T", g), "V"), (("RS", g), "A")] * g
            t += [(("R", g), "A")]
        t += [(("T1", p, d), "A") for d in range(2)]
        for k in range(1, LEVELS):
            t += [(("X", p, k, d), "A") for d in range(2)]
            for d in range(2):
                t += [(("Y", p, k, d), "V")] * (k < LEVELS - 1) + [(("YT", p, k, d), "V")]
        t += [(("W", p), "V"), (("O", p), "V")] + [(("S", p), "V")] * (1 - g)
    t += [(("mixT", g, n), "A") for g in range(2) for n in range(2)]
    t += [(("out", n, g), "V") for n in range(2) for g in range(2)]
    t += [(("h2", g, n), "V") for g in range(2) for n in range(2)]
    t += [(("route", g), "V") for g in range(2)]
    t += [(("rows", g, n), "A") for g in range(2) for n in range(2)]
    t += [(("pos",), "V")]
    return t


class Tiles:

    def __init__(self):
        self.order = [n for n, _ in plan()]
        self.who = dict(plan())
        self.index = {n: i for i, n in enumerate(self.order)}
        assert len(self.index) == len(self.order)
        self.total = len(self.order)
        self.rank, self.per = {}, {"V": 0, "A": 0}
        for n in self.order:
            self.per[self.who[n]] += 1
            self.rank[n] = self.per[self.who[n]]

    def filled(self, l, name):
        return l * self.total + (self.index[name] + 1)

    def emptied(self, l, name):
        return l * self.per[self.who[name]] + self.rank[name]


PIECES = [("ada", n) for n in range(12)] + [("w_in", c) for c in range(ZC)] + ["uq", "ukv"] + \
         [("w_out", n) for n in range(2)] + ["router", "shared"]
SLOTS = 4
assert len(PIECES) % SLOTS == 0 and EXPERTS % SLOTS == 0
LAST_TILE = [("mods", n) for n in range(12)] + [("z", c, 1) for c in range(ZC)] + [("qpe", 1), ("v", 2)] + \
            [("out", n, 1) for n in range(2)] + [("route", 1)]
RING_LAYER = 16 * (len(PIECES) + PASSES * EXPERTS) // SLOTS
DOWN_PASS = 16 * EXPERTS // SLOTS
G0, A0, Y0 = SLOTS, 2, 1


def build(nc, a, consts, outs):
    tiles = Tiles()
    y_prompt, y_sample, new_ckv, new_kpe, new_gdn, new_rwkv = outs
    with ExitStack() as ctx:
        def sb(name, n, parts=128):
            return ctx.enter_context(nc.sbuf_tensor(name, [parts, n], F32))

        def sem(name):
            return ctx.enter_context(nc.semaphore(name))

        ring = [sb(f"ring{s}", 4096) for s in range(SLOTS)]
        W1 = sb("W1", 8192)
        PR = sb("PR", 7168)
        C = sb("consts", CW)
        X = sb("x", 2 * D)
        HT = sb("hT", KD * 2 * T)
        Z = sb("z", 6144)
        GB = sb("gateB", 4096)
        SP = sb("small_params", 3088)
        SM = sb("small", 612)
        IDT = ctx.enter_context(nc.sbuf_tensor("index_table", [128, EXPERTS], U32))
        RIX = ctx.enter_context(nc.sbuf_tensor("result_index", [128, 2 * TOP_K], U32))
        gidx = [ctx.enter_context(nc.sbuf_tensor(f"gather_index{i}", [128, 1], U32)) for i in range(2)]
        onehot = [ctx.enter_context(nc.sbuf_tensor(f"onehot{i}", [128, 8 * CAP], BF16))[:, :].rearrange(
            "p (e c) -> p e c", e=8) for i in range(2)]
        token = ctx.enter_context(nc.sbuf_tensor("token", [128, 4], BF16))[:, :].rearrange("p (g c) -> p g c", g=2)
        most = ctx.enter_context(nc.sbuf_tensor("most_tokens", [128, 2], I32))
        idt = IDT[:, :].rearrange("p (e c) -> p e c", c=1)
        h_rows = nc.dram_tensor("h_rows", [2 * T, D], F32).ap()
        y_rows = nc.dram_tensor("y_rows", [EXPERTS * CAP, D], F32).ap()
        P = ctx.enter_context(nc.psum_tensor("P", [128, 8, 512], F32))

        def cst(name, parts=128):
            o, w = CONSTS[name]
            return C[0:parts, o:o + w]

        def many(ap, *dims):
            p, n = ap.shape
            return ap.rearrange("p (a n) -> p a n", a=1).to_broadcast([p, dims[0], n])

        def wide(ap, n):
            p, k = ap.shape
            return ap.rearrange("p (k a) -> p k a", a=1).to_broadcast([p, k, n])

        def v3(ap, k):
            return ap.rearrange("p (k n) -> p k n", k=k)

        ident = cst("ident")
        x = v3(X[:, :], 2)
        hT = v3(HT[:, :], KD)
        z = v3(Z[:, 0:2 * P_IN], 2)
        mods = Z[0:2, :]
        gateB = GB[:, :].rearrange("p (w g n) -> p w g n", w=2, g=2)

        o = 0
        small = {}
        for name, w in [("q_norm", QL), ("kv_norm", KVL), ("gdn_norm", N), ("w0", 512), ("a0", 512), ("k_k", 256),
                        ("k_a", 256), ("r_k", 256), ("gn_w", 256), ("gn_b", 256), ("bias", 64), ("a_log", 8),
                        ("dt", 8)]:
            small[name] = SP[:, o:o + w]
            o += w
        small_src = {"q_norm": a["mla_q_norm"], "kv_norm": a["mla_kv_norm"], "gdn_norm": a["gdn_norm"],
                     "w0": a["rwkv_w0"].rearrange("l d c -> l (d c)"), "a0": a["rwkv_a0"].rearrange("l d c -> l (d c)"),
                     "k_k": a["rwkv_k_k"], "k_a": a["rwkv_k_a"], "r_k": a["rwkv_r_k"].rearrange("l h n -> l (h n)"),
                     "gn_w": a["rwkv_gn_w"], "gn_b": a["rwkv_gn_b"], "bias": a["moe_bias"],
                     "a_log": a["gdn_a_log"].rearrange("l d h -> l (d h)"),
                     "dt": a["gdn_dt_bias"].rearrange("l d h -> l (d h)")}

        o = 0
        sm = {}
        for name, w in [("ss", 8), ("rs", 8), ("cT", 16), ("modT", 64), ("nT", 16), ("nalog", 8), ("gg", 16),
                        ("beta", 16), ("t16", 16), ("gcs", 32), ("egs", 32), ("nqk", 16), ("mx", 4), ("sum", 4),
                        ("comb", 128), ("scores", 64), ("sel", 64), ("w64", 64), ("st8", 24), ("ecc", 8), ("ran", 1)]:
            sm[name] = SM[:, o:o + w]
            o += w
        modT = sm["modT"].rearrange("p (m k g) -> p m k g", m=4, k=KD)
        gg = sm["gg"].rearrange("p (d g h) -> p d g h", d=2, g=2)
        beta = sm["beta"].rearrange("p (d g h) -> p d g h", d=2, g=2)
        gc = sm["gcs"][:, 0:16].rearrange("p (d g h) -> p d g h", d=2, g=2)
        egc = sm["egs"][:, 0:16].rearrange("p (d g h) -> p d g h", d=2, g=2)
        egs = sm["egs"][:, 16:32].rearrange("p (d g h) -> p d g h", d=2, g=2)
        comb = sm["comb"].rearrange("p (g e) -> p g e", g=2)

        mix3 = v3(PR[:, 0:5760], 3)
        conv_t = [PR[:, 5760:6144], PR[:, 6144:6528]]
        nrows = PR[0:8, 6528:6528 + 256].rearrange("p (w n) -> p w n", w=2)
        crow = W1[0:2, 0:D]
        ada_b = W1[0:2, 0:6144]

        o = 0
        mla = {}
        for name, w in [("cqn", 768), ("ckvn", 768), ("kpe", 192), ("cqT", 768), ("ckvT", 768), ("kpeT", 384),
                        ("qpe", 512), ("kT", 1536), ("v", 1536)]:
            mla[name] = W1[:, o:o + w]
            o += w
        cqn, ckvn, kpe = v3(mla["cqn"], 2), v3(mla["ckvn"], 3), v3(mla["kpe"], 3)
        cqT, ckvT = v3(mla["cqT"], 3), v3(mla["ckvT"], 2)
        kpeT = mla["kpeT"][0:64, :]
        qpe, kT, vv = v3(mla["qpe"], 2), v3(mla["kT"], HEADS), v3(mla["v"], 3)
        prob = [W1[:, 0:256], W1[:, 256:512]]
        pT = [v3(W1[:, 768:1024], 2), v3(W1[:, 1024:1280], 2)]
        rt = v3(W1[:, 7232:7744], 2)
        assert o <= 7232
        qT = HT[:, 0:1024].rearrange("p (h g t) -> p h g t", h=HEADS, g=2)
        qpeT = HT[0:64, 1024:2048].rearrange("p (g h t) -> p g h t", g=2, h=HEADS)

        def u4(ap):
            return ap.rearrange("p (d h n) -> p d h n", d=2, h=HEADS)
        AT, MT, PB, PK = (u4(W1[:, 1024 * k:1024 * k + 1024]) for k in range(4))
        KRT = W1[0:64, 4096:6144].rearrange("p (d h s t) -> p d h s t", d=2, h=HEADS, s=2)
        BT = u4(W1[0:64, 6144:7168])
        KTh = u4(W1[0:64, 7168:8192])
        Tm, TT, XX = (u4(W1[:, 4096 + 1024 * k:5120 + 1024 * k]) for k in range(3))
        Lm = [u4(W1[:, 7168:8192]), u4(PR[:, 0:1024])]
        qkT = W1[0:64, 4096:5120].rearrange("p (s h t) -> p s h t", s=2, h=HEADS)
        gtri = MT
        Rt, Ktl = v3(W1[:, 0:512], 2), v3(W1[:, 512:1024], 2)
        Bh, Kh = v3(W1[:, 1024:1536], 2), v3(W1[:, 1536:2048], 2)
        E, Ei = v3(W1[:, 2048:2560], 2), v3(W1[:, 2560:3072], 2)
        Ex, Fs = v3(W1[:, 3072:3584], 2), v3(W1[:, 3584:4096], 2)
        o = 1024
        nat = {}
        for name, w in [("lw", 512), ("a", 512), ("kd", 512), ("Bf", 512), ("Kf", 512), ("R", 512), ("SA", 512),
                        ("gate", 256), ("kk", 256), ("w2", 512), ("a2", 512), ("g2", 256), ("wdT", 512),
                        ("oacc", 256)]:
            nat[name] = PR[:, o:o + w]
            o += w
        nat["gdT"] = nat["oacc"][:, 0:128]
        lw, aa, kd, Bf, Kf = (v3(nat[n], 2) for n in ("lw", "a", "kd", "Bf", "Kf"))
        R, SA = u4(nat["R"]), u4(nat["SA"])
        S0nat, S0T = u4(nat["Bf"][0:64, :]), u4(nat["Kf"][0:64, :])
        w2, a2 = v3(nat["w2"][0:64, :], 2), v3(nat["a2"][0:64, :], 2)
        wdT = v3(nat["wdT"][0:64, :], 4)
        S0g = u4(nat["w2"][0:64, :])
        kdec = u4(nat["kd"])
        sq = nat["wdT"]
        oacc = nat["oacc"]
        sout = nat["a2"][0:64, :]

        down = [v3(W1[:, 2048 * s:2048 * s + 2048], 2) for s in range(SLOTS)]
        xg = [PR[:, 1024 * i:1024 * i + 1024] for i in range(2)]
        xgT = [v3(PR[:, 2048 + 1024 * i:3072 + 1024 * i], KD) for i in range(2)]
        yo = [PR[:, 4096 + 1024 * i:5120 + 1024 * i] for i in range(2)]
        sg = [PR[:, 6144 + 256 * i:6400 + 256 * i] for i in range(2)]
        act_ = [PR[:, 6656 + 256 * i:6912 + 256 * i] for i in range(2)]
        rows = v3(PR[:, 4096:6144], 2)
        acc = PR[:, 0:2048]
        o = 0
        moe = {}
        for name, w in [("chosen", 128), ("pos", 128), ("ra", 128),
                        ("rb", 128), ("iw", 128), ("cnt", 64), ("row", 128), ("cw", 128), ("in", 128), ("rix", 16),
                        ("rw", 16), ("none", 16), ("actT0", 256), ("actT1", 256)]:
            moe[name] = Z[:, o:o + w]
            o += w
        actT = [v3(moe[f"actT{i}"], 2) for i in range(2)]
        xeT, aeT = [t[:, :, 0:CAP] for t in xgT], [t[:, :, 0:CAP] for t in actT]
        chosen, pos = v3(moe["chosen"], 2), v3(moe["pos"], 2)
        iw = moe["iw"].rearrange("p (e c) -> p e c", c=2)
        xs = v3(PR[:, 2048:4096], 2)
        xs1 = v3(W1[:, 0:2048], 2)
        xo = v3(PR[:, 4096:6144], 2)
        normf = W1[:, 0:D]

        const_in = sem("const_in")
        x_in = sem("x_in")
        c_in = sem("c_in")
        ring_in = [sem(f"ring_in{s}") for s in range(SLOTS)]
        down_in = [sem(f"down_in{s}") for s in range(SLOTS)]
        filled = sem("tile_filled")
        empty = {"V": sem("tile_emptied_v"), "A": sem("tile_emptied_a")}
        x_done = sem("x_done")
        cT_ready = sem("cT_ready")
        small_in = sem("small_in")
        adab_in = sem("adab_in")
        mix_in = sem("mix_in")
        ctx_in = sem("ctx_in")
        state_in = sem("state_in")
        lora_in = sem("lora_in")
        ss_ready = sem("sum_squares_ready")
        ss_eps = sem("mean_square_ready")
        rs_ready = sem("rstd_ready")
        xn_ready = sem("xn_ready")
        z_mid = sem("z_scaled")
        conv_done = sem("conv_done")
        silu_done = sem("z_activated")
        mix_c = sem("centre_weight_ready")
        gates_v = sem("gates_v")
        gates_a = sem("gates_a")
        cq_ready = sem("cq_ready")
        ckv_ready = sem("ckv_ready")
        qpe_ready = sem("qpe_ready")
        nmax = sem("negative_max_ready")
        prob_ready = sem("prob_ready")
        gtri_ready = sem("gtri_ready")
        dec_v = sem("decay_difference_ready")
        dec_a = sem("decay_ready")
        at_ready = sem("at_ready")
        lm_ready = sem("level_ready")
        tt_ready = sem("tt_ready")
        rhs_ready = sem("rhs_ready")
        kdec_ready = sem("kdec_ready")
        fin_v = sem("finish_v")
        fin_a = sem("finish_a")
        pair_done = sem("pair_done")
        mixed = sem("mixed_ready")
        rw_v = sem("rwkv_v")
        rw_a = sem("rwkv_a")
        rwp = sem("rwkv_operands")
        ckv_out = sem("ckv_stored")
        state_ready = sem("state_ready")
        state_out = sem("state_stored")
        logit_v = sem("logits_copied")
        logit_a = sem("scores_ready")
        rows_out = sem("rows_stored")
        chosen_ready = sem("chosen_ready")
        most_ready = sem("most_ready")
        sh_full = sem("shared_gu_full")
        sh_silu = sem("shared_silu")
        sh_act = sem("shared_act")
        sh_turn = sem("shared_act_turned")
        sh_ready = sem("shared_actT_ready")
        sh_y = sem("shared_y_full")
        x_shared = sem("x_shared")
        sel_ready = sem("onehot_ready")
        sel_used = sem("onehot_used")
        idx_ready = sem("index_ready")
        gx_in = [sem(f"gathered{i}") for i in range(2)]
        xT_full = sem("xT_full")
        xT = {"A": sem("xT_ready_a"), "V": sem("xT_ready_v")}
        g_full = sem("gu_full")
        silu_e = sem("expert_silu")
        act_done = sem("expert_act")
        t_full = sem("act_turned")
        t_ready = sem("actT_ready")
        y_full = sem("y_full")
        y_out_e = {"A": sem("y_emptied_a"), "V": sem("y_emptied_v")}
        stored = [sem(f"y_stored{i}") for i in range(2)]
        pass_stored = sem("pass_stored")
        rix_ready = sem("result_index_ready")
        own_step = sem("own_step")
        sum_in = [sem(f"sum_in{i}") for i in range(4)]
        sum_used = sem("sum_used")
        normf_in = sem("normf_in")
        y_ready = sem("y_ready")
        y_out = sem("y_out")
        narrow_turns = sem("narrow_turns")

        block = ctx.enter_context(nc.Block())

        @block.sync
        def _(sp):
            sp.dma_start(C[:, :], consts).then_inc(const_in, 16)
            for g, src in enumerate((a["x_prompt"], a["x_sample"])):
                sp.dma_start(x[:, g, :], src[0]).then_inc(x_in, 16)
            with sp.Fori(0, LAYERS) as l:
                def chunk(ap):
                    return ap.rearrange("a (k p) n -> p (a k) n", p=128)

                def piece(i, k, n, src):
                    if i < SLOTS:
                        sp.wait_ge(g_full, l * (PASSES * EXPERTS) + (G0 - SLOTS + i + 1))
                    else:
                        sp.wait_ge(filled, tiles.filled(l, LAST_TILE[i - SLOTS]))
                    dst = v3(ring[i % SLOTS][:, 0:k * n], k)
                    sp.dma_start(dst, src).then_inc(ring_in[i % SLOTS], 16)

                i = 0
                for n in range(12):
                    piece(i, KD, 512, chunk(a["ada_w"][bass.ds(l, 1), :, 512 * n:512 * n + 512]))
                    i += 1
                for c in range(ZC):
                    piece(i, KD, ZW[c], chunk(a["w_in"][bass.ds(l, 1), :, 512 * c:512 * c + ZW[c]]))
                    i += 1
                piece(i, 3, 768, chunk(a["mla_w_uq"][bass.ds(l, 1), :, :]))
                piece(i + 1, 2, 1024, chunk(a["mla_w_ukv"][bass.ds(l, 1), :, :]))
                i += 2
                for n in range(2):
                    piece(i, KD, 512, chunk(a["w_out"][bass.ds(l, 1), :, 512 * n:512 * n + 512]))
                    i += 1
                piece(i, KD, EXPERTS, chunk(a["moe_router"][bass.ds(l, 1), :, :]))
                piece(i + 1, KD, 2 * FF, chunk(a["shared_w_gu"][bass.ds(l, 1), :, :]))
                assert i + 2 == len(PIECES)
                sp.wait_ge(mixed, l * 2 + 2)
                sp.wait_ge(state_out, l * 32 + 32)
                sp.dma_start(down[3], chunk(a["shared_w_down"][bass.ds(l, 1), :, :])).then_inc(down_in[3], 16)
                gu_all = a["moe_w_gu"].rearrange("l e k n -> (l e) k n")
                dn_all = a["moe_w_down"].rearrange("l e k n -> (l e) k n")

                sp.wait_ge(filled, tiles.filled(l, LAST_TILE[-1]))
                sp.nop().then_inc(own_step, 1)
                sp.wait_ge(sh_full, l * 2 + 2)
                sp.nop().then_inc(own_step, 1)
                sp.wait_ge(most_ready, l + 1)
                sp.nop().then_inc(own_step, 1)
                most_here = sp.value_load(most[0:1, 0:1], min_val=0, max_val=2 * T)
                ran = sp.value_load(most[0:1, 1:2], min_val=0, max_val=LAYERS * PASSES)
                with sp.Fori(0, PASSES) as b:
                    with sp.If(b * CAP < most_here):
                        base = (l * PASSES + b) * EXPERTS
                        sp.wait_ge(sum_used, (ran + b) * TOP_K + 1)
                        sp.nop().then_inc(own_step, 1)

                        def block(eb, first=False):
                            for s in range(SLOTS):
                                e = eb * SLOTS + s
                                sp.wait_ge(g_full, base + e + (G0 + 1 - SLOTS))
                                sp.nop().then_inc(own_step, 1)
                                sp.dma_start(v3(ring[s][:, :], KD), chunk(gu_all[bass.ds(l * EXPERTS + e, 1), :, :])
                                             ).then_inc(ring_in[s], 16)
                                if first and s == 3:
                                    sp.wait_ge(sh_y, l + 1)
                                sp.wait_ge(y_full, base + e + (G0 + 1 - SLOTS))
                                sp.nop().then_inc(own_step, 1)
                                sp.dma_start(down[s], chunk(dn_all[bass.ds(l * EXPERTS + e, 1), :, :])
                                             ).then_inc(down_in[s], 16)

                        block(0, True)
                        with sp.Fori(1, EXPERTS // SLOTS) as eb:
                            block(eb)
                    with sp.Else():
                        sp.wait_ge(y_full, (l * PASSES + b) * EXPERTS + G0)
                        sp.nop().then_inc(own_step, 1)
                        for s in range(SLOTS):
                            sp.nop().then_inc(ring_in[s], 16 * EXPERTS // SLOTS)
                            sp.nop().then_inc(down_in[s], 16 * EXPERTS // SLOTS)
            sp.wait_ge(x_done, LAYERS + 1)
            sp.dma_start(normf, a["norm_f"].rearrange("(a n) -> a n", a=1).partition_broadcast(128)
                         ).then_inc(normf_in, 16)
            for g, dst in enumerate((y_prompt, y_sample)):
                sp.wait_ge(y_ready, g + 1)
                sp.dma_start(dst[0], xo[:, g, :]).then_inc(y_out, 16)
            sp.wait_ge(y_out, 32)
            sp.wait_ge(ckv_out, 32 * LAYERS)
            sp.wait_ge(state_out, 32 * LAYERS)

        @block.tensor
        def _(pe):
            def tile(l, name):
                settled[0] = False
                i = tiles.index[name]
                assert i == order[0], name
                order[0] += 1
                if i >= 8:
                    before = tiles.order[i - 8]
                    pe.wait_ge(empty[tiles.who[before]], tiles.emptied(l, before))
                return P[:, i % 8, :]

            def need(l, name):
                pe.wait_ge(empty[tiles.who[name]], tiles.emptied(l, name))

            def turn_narrow(out, src, unit):
                if not settled[0]:
                    pe.nop().then_inc(narrow_turns, 1)
                    settled[0] = True
                return pe.transpose(out, src, unit)

            def mm(out, lhsT, rhs, start, stop):
                return pe.matmul(out, lhsT, rhs, start=start, stop=stop)

            order, settled = [0], [False]
            pe.wait_ge(const_in, 16)
            pe.wait_ge(cT_ready, 1)
            for k in range(KD):
                last = pe.transpose(P[:, 0, 2 * k:2 * k + 2], crow[:, 128 * k:128 * k + 128], cst("ident", 2)[:, 0:2])
            last.then_inc(cT_ready, 1)
            pe.nop().then_inc(g_full, G0)
            pe.nop().then_inc(y_full, G0)
            pe.nop().then_inc(sel_used, 2)
            pe.wait_ge(cT_ready, 3)
            cT = v3(sm["cT"], KD)

            with pe.Fori(0, LAYERS) as l:
                order[0] = 0
                def piece(i):
                    u = i // SLOTS + 1
                    pe.wait_ge(ring_in[i % SLOTS], l * RING_LAYER + 16 * u)
                    return ring[i % SLOTS]

                i = 0
                for n in range(12):
                    w = v3(piece(i)[:, :], KD)
                    b = tile(l, ("mods", n))
                    for k in range(KD):
                        last = mm(b[0:2, :], cT[:, k, :], w[:, k, :], k == 0, k == KD - 1)
                    last.then_inc(filled, 1)
                    i += 1
                need(l, ("mods", 11))
                pe.wait_ge(adab_in, l * 48 + 48)
                b = tile(l, ("modT",))
                for m, part in enumerate((0, 1, 3, 4)):
                    for k in range(KD):
                        c0 = part * D + 128 * k
                        turn_narrow(b[:, (m * KD + k) * 2:(m * KD + k) * 2 + 2], mods[:, c0:c0 + 128],
                                     cst("ident", 2)[:, 0:2])
                for w in range(2):
                    last = pe.transpose(b[:, 64 + 8 * w:72 + 8 * w], nrows[:, w, :], cst("ident", 8)[:, 0:8])
                last.then_inc(filled, 1)
                for w, part in enumerate((2, 5)):
                    for g in range(2):
                        for n in range(2):
                            b = tile(l, ("gate", w, g, n))
                            c0 = part * D + 512 * n
                            mm(b, cst("ident", 2)[:, g:g + 1].to_broadcast([2, T]), mods[:, c0:c0 + 512], True, True).then_inc(filled, 1)

                def to_columns(which, xn_count):
                    for g in range(2):
                        for n in range(2):
                            b = tile(l, (which, g, n))
                            if n == 0:
                                pe.wait_ge(xn_ready, l * 4 + (xn_count + g))
                            for k in range(4):
                                c0 = 512 * n + 128 * k
                                src = (xs1 if which == "h1" else xs)[:, g, c0:c0 + 128]
                                last = pe.transpose(b[:, 128 * k:128 * k + 128], src, ident)
                            last.then_inc(filled, 1)

                to_columns("h1", 1)
                need(l, ("h1", 1, 1))
                for c in range(ZC):
                    w = v3(piece(i)[:, 0:KD * ZW[c]], KD)
                    for g in range(2):
                        b = tile(l, ("z", c, g))
                        for k in range(KD):
                            last = mm(b[:, 0:ZW[c]], hT[:, k, 128 * g:128 * g + 128], w[:, k, :], k == 0, k == KD - 1)
                        last.then_inc(filled, 1)
                    i += 1
                need(l, ("z", ZC - 1, 1))
                for g in range(2):
                    for c, c0 in enumerate(SHIFTED):
                        for s, shift in (("zp", "prev"), ("zn", "next")):
                            b = tile(l, (s, g, c))
                            mm(b[:, 0:CONV], cst(shift), z[:, g, c0:c0 + CONV], True, True).then_inc(filled, 1)
                b = tile(l, ("decay",))
                pe.wait_ge(gates_v, l * 4 + 4)
                for d in range(2):
                    gd = gg[:, d, :, :]
                    mm(b[:, 8 * d:8 * d + 8], cst(f"tri{d}"), gd, True, True)
                    last = mm(b[:, 16 + 8 * d:24 + 8 * d], cst(f"strict{1 - d}"), gd, True, True)
                last.then_inc(filled, 1)

                for g in range(2):
                    b = tile(l, ("cqT", g))
                    pe.wait_ge(cq_ready, l * 2 + (g + 1))
                    for k in range(3):
                        last = pe.transpose(b[:, 128 * k:128 * k + 128], cqn[:, g, 128 * k:128 * k + 128], ident)
                    last.then_inc(filled, 1)
                for blk in range(3):
                    b = tile(l, ("ckvT", blk))
                    pe.wait_ge(ckv_ready, l * 3 + (blk + 1))
                    for k in range(2):
                        pe.transpose(b[:, 128 * k:128 * k + 128], ckvn[:, blk, 128 * k:128 * k + 128], ident)
                    turn_narrow(b[0:64, 256:384], kpe[:, blk, :], ident).then_inc(filled, 1)
                uq = v3(piece(i)[:, 0:3 * 768], 3)
                need(l, ("cqT", 1))
                for hp in range(2):
                    b = tile(l, ("qT", hp))
                    for h in (2 * hp, 2 * hp + 1):
                        for k in range(3):
                            last = mm(b[:, 256 * (h % 2):256 * (h % 2) + 256], uq[:, k, 192 * h:192 * h + 128],
                                      cqT[:, k, :], k == 0, k == 2)
                    last.then_inc(filled, 1)
                for g in range(2):
                    b = tile(l, ("qpe", g))
                    for k in range(3):
                        w = uq[:, k, :].rearrange("p (h n) -> p h n", h=HEADS)[:, :, NOPE:NOPE + ROPE]
                        last = mm(b[:, 0:256], cqT[:, k, 128 * g:128 * g + 128], w, k == 0, k == 2)
                    last.then_inc(filled, 1)
                i += 1
                for g in range(2):
                    b = tile(l, ("qpeT", g))
                    pe.wait_ge(qpe_ready, l * 2 + (g + 1))
                    for h in range(HEADS):
                        last = turn_narrow(b[0:64, 128 * h:128 * h + 128], qpe[:, g, 64 * h:64 * h + 64], ident)
                    last.then_inc(filled, 1)
                ukv = v3(piece(i)[:, 0:2048], 2)
                need(l, ("ckvT", 2))
                for h in range(HEADS):
                    b = tile(l, ("kT", h))
                    for k in range(2):
                        last = mm(b[:, 0:384], ukv[:, k, 256 * h:256 * h + 128], ckvT[:, k, :], k == 0, k == 1)
                    last.then_inc(filled, 1)
                for blk in range(3):
                    b = tile(l, ("v", blk))
                    for k in range(2):
                        w = ukv[:, k, :].rearrange("p (h n) -> p h n", h=HEADS)[:, :, NOPE:NOPE + VDIM]
                        last = mm(b, ckvT[:, k, 128 * blk:128 * blk + 128], w, k == 0, k == 1)
                    last.then_inc(filled, 1)
                i += 1
                need(l, ("qpeT", 1))
                need(l, ("v", 2))
                need(l, ("kT", 3))
                for g in range(2):
                    k0, nk = (0, 1) if g == 0 else (1, 2)
                    keys = slice(128 * k0, 128 * (k0 + nk))
                    for h in range(HEADS):
                        b = tile(l, ("score", g, h))
                        mm(b[:, 0:128 * nk], qT[:, h, g, :], kT[:, h, keys], True, False)
                        mm(b[:, 0:128 * nk], qpeT[:, g, h, :], kpeT[:, keys], False, True).then_inc(filled, 1)
                        b = tile(l, ("pT", g, h))
                        pe.wait_ge(prob_ready, l * 8 + (4 * g + h + 1))
                        for q in range(nk):
                            last = pe.transpose(b[:, 128 * q:128 * q + 128], prob[h % 2][:, 128 * q:128 * q + 128], ident)
                        last.then_inc(filled, 1)
                        b = tile(l, ("mla", g, h))
                        need(l, ("pT", g, h))
                        for q in range(nk):
                            last = mm(b[:, 0:128], pT[h % 2][:, q, :], vv[:, k0 + q, 128 * h:128 * h + 128],
                                      q == 0, q == nk - 1)
                        last.then_inc(filled, 1)

                for pi, p in enumerate(PAIRS):
                    kind, g = p
                    if kind == "gdn":
                        for s in range(2):
                            b = tile(l, ("qkT", g, s))
                            for h in range(HEADS):
                                c0 = Z_G + 256 * s + 64 * h
                                if s == 0 and h == 0:
                                    pe.wait_ge(fin_v, l * 6 + (g + 1))
                                last = turn_narrow(b[0:64, 128 * h:128 * h + 128], z[:, g, c0:c0 + 64], ident)
                            last.then_inc(filled, 1)
                        for d in range(2):
                            b = tile(l, ("row", g, d))
                            if d == 0:
                                pe.wait_ge(gtri_ready, l * 2 + (g + 1))
                            mm(b, cst("ones"), gtri[:, d, :, :].rearrange("p h n -> p (h n)"), True, True
                               ).then_inc(filled, 1)
                        b = tile(l, ("kk", g))
                        need(l, ("qkT", g, 1))
                        for h in range(HEADS):
                            last = mm(b[:, 128 * h:128 * h + 128], qkT[:, 1, h, :], qkT[:, 1, h, :], True, True)
                        last.then_inc(filled, 1)
                        b = tile(l, ("qk", g))
                        for h in range(HEADS):
                            last = mm(b[:, 128 * h:128 * h + 128], qkT[:, 1, h, :], qkT[:, 0, h, :], True, True)
                        last.then_inc(filled, 1)
                        if g:
                            pe.wait_ge(state_in, l * 32 + 16)
                            for name, s in (("kS", 1), ("qS", 0)):
                                b = tile(l, (name, g))
                                for d in range(2):
                                    for h in range(HEADS):
                                        c0 = 64 * (4 * d + h)
                                        last = mm(b[:, c0:c0 + 64], qkT[:, s, h, :], S0g[:, d, h, :], True, True)
                                last.then_inc(filled, 1)
                    else:
                        b = tile(l, ("wdT", g))
                        for q in range(4):
                            c0 = Z_WD + 64 * q
                            last = turn_narrow(b[0:64, 128 * q:128 * q + 128], z[:, g, c0:c0 + 64], ident)
                        last.then_inc(filled, 1)
                        b = tile(l, ("gdT", g))
                        pe.transpose(b[:, 0:128], z[:, g, Z_GD:Z_GD + 128], ident).then_inc(filled, 1)
                        need(l, ("gdT", g))
                        pe.wait_ge(lora_in, l * 96 + 48 * (g + 1))
                        for q, (name, w) in enumerate((("wpre", w2), ("apre", a2))):
                            b = tile(l, (name, g))
                            for d in range(2):
                                last = mm(b[:, 256 * d:256 * d + 256], wdT[:, 2 * q + d, :], w[:, d, :], True, True)
                            last.then_inc(filled, 1)
                        b = tile(l, ("rgate", g))
                        mm(b[:, 0:256], nat["gdT"], nat["g2"], True, True).then_inc(filled, 1)
                        b = tile(l, ("cum", g))
                        pe.wait_ge(rwp, l * 4 + (2 * g + 1))
                        for d in range(2):
                            last = mm(b[:, 256 * d:256 * d + 256], cst(f"cen{d}"), lw[:, d, :], True, True)
                        last.then_inc(filled, 1)
                        if g == 0:
                            b = tile(l, ("suf", g))
                            for d in range(2):
                                last = mm(b[:, 256 * d:256 * d + 256], cst(f"strict{1 - d}"), lw[:, d, :], True, True)
                            last.then_inc(filled, 1)
                        pe.wait_ge(rwp, l * 4 + (2 * g + 2))
                        for d in range(2):
                            for name, src in (("KTt", Ktl), ("RT", Rt), ("BT", Bh), ("KhT", Kh)):
                                b = tile(l, (name, g, d))
                                for h in range(HEADS):
                                    last = turn_narrow(b[0:64, 128 * h:128 * h + 128], src[:, d, 64 * h:64 * h + 64],
                                                        ident)
                                last.then_inc(filled, 1)
                        need(l, ("KhT", g, 1))
                        for d in range(2):
                            for hp in range(2):
                                for name, src in (("PB", BT), ("PK", KTh)):
                                    b = tile(l, (name, g, d, hp))
                                    for h in (2 * hp, 2 * hp + 1):
                                        last = mm(b[:, 256 * (h % 2):256 * (h % 2) + 256], src[:, d, h, :],
                                                  KRT[:, d, h, :, :].rearrange("p s t -> p (s t)"), True, True)
                                    last.then_inc(filled, 1)
                        if g:
                            b = tile(l, ("cc", g))
                            for d in range(2):
                                for h in range(HEADS):
                                    q = 4 * d + h
                                    last = mm(b[0:64, q:q + 1], lw[:, d, 64 * h:64 * h + 64], cst(f"half{d}"),
                                              True, True)
                            last.then_inc(filled, 1)
                            b = tile(l, ("S0T", g))
                            pe.wait_ge(state_in, l * 32 + 32)
                            for d in range(2):
                                for h in range(HEADS):
                                    c0 = 64 * (4 * d + h)
                                    last = turn_narrow(b[0:64, c0:c0 + 64], S0nat[:, d, h, :],
                                                        cst("ident", 64)[:, 0:64])
                            last.then_inc(filled, 1)
                            b = tile(l, ("RS", g))
                            need(l, ("S0T", g))
                            for h in range(HEADS):
                                for d in range(2):
                                    last = mm(b[:, 64 * h:64 * h + 64], KRT[:, d, h, 1, :], S0T[:, d, h, :],
                                              d == 0, d == 1)
                            last.then_inc(filled, 1)
                        b = tile(l, ("R", g))
                        need(l, ("PK", g, 1, 1))
                        for d in range(2):
                            for h in range(HEADS):
                                c0 = 64 * (4 * d + h)
                                v_h = z[:, g, Z_V + 64 * h:Z_V + 64 * h + 64]
                                if g:
                                    mm(b[:, c0:c0 + 64], KRT[:, d, h, 0, :], S0T[:, d, h, :], True, False)
                                last = mm(b[:, c0:c0 + 64], MT[:, d, h, :], v_h, not g, True)
                        last.then_inc(filled, 1)

                    for d in range(2):
                        b = tile(l, ("T1", p, d))
                        if d == 0:
                            pe.wait_ge(tt_ready, l * 4 + (pi + 1))
                        for h in range(HEADS):
                            last = pe.transpose(b[:, 128 * h:128 * h + 128], TT[:, d, h, :], ident)
                        last.then_inc(filled, 1)
                    for k in range(1, LEVELS):
                        final = k == LEVELS - 1
                        for d in range(2):
                            b = tile(l, ("X", p, k, d))
                            if d == 0:
                                pe.wait_ge(lm_ready, l * 4 * LEVELS + (pi * LEVELS + k + 1))
                            need(l, ("T1", p, d) if k == 1 else ("Y", p, k - 1, d))
                            for h in range(HEADS):
                                last = mm(b[:, 128 * h:128 * h + 128], Lm[k % 2][:, d, h, :], Tm[:, d, h, :], True, True)
                            last.then_inc(filled, 1)
                        for d in range(2):
                            if not final:
                                b = tile(l, ("Y", p, k, d))
                                need(l, ("X", p, k, d))
                                if k > 1:
                                    need(l, ("YT", p, k - 1, d))
                                for h in range(HEADS):
                                    last = mm(b[:, 128 * h:128 * h + 128], TT[:, d, h, :], XX[:, d, h, :], True, True)
                                last.then_inc(filled, 1)
                            b = tile(l, ("YT", p, k, d))
                            if final:
                                need(l, ("X", p, k, d))
                                need(l, ("YT", p, k - 1, d))
                            for h in range(HEADS):
                                last = mm(b[:, 128 * h:128 * h + 128], XX[:, d, h, :], TT[:, d, h, :], True, True)
                            last.then_inc(filled, 1)

                    b = tile(l, ("W", p))
                    need(l, ("YT", p, LEVELS - 1, 1))
                    if kind == "gdn":
                        pe.wait_ge(rhs_ready, l * 2 + (g + 1))
                    else:
                        need(l, ("R", g))
                    for d in range(2):
                        for h in range(HEADS):
                            c0 = 64 * (4 * d + h)
                            last = mm(b[:, c0:c0 + 64], TT[:, d, h, :], R[:, d, h, :], True, True)
                    last.then_inc(filled, 1)
                    b = tile(l, ("O", p))
                    need(l, ("W", p))
                    for h in range(HEADS):
                        out = b[:, 64 * h:64 * h + 64]
                        if kind == "gdn":
                            for d in range(2):
                                last = mm(out, PK[:, d, h, :], SA[:, d, h, :], d == 0, d == 1)
                        else:
                            v_h = z[:, g, Z_V + 64 * h:Z_V + 64 * h + 64]
                            for d in range(2):
                                mm(out, PB[:, d, h, :], SA[:, d, h, :], d == 0, False)
                                last = mm(out, PK[:, d, h, :], v_h, False, d == 1)
                    last.then_inc(filled, 1)
                    if g == 0:
                        b = tile(l, ("S", p))
                        if kind == "gdn":
                            pe.wait_ge(kdec_ready, l * 1 + 1)
                        for d in range(2):
                            for h in range(HEADS):
                                c0 = 64 * (4 * d + h)
                                if kind == "gdn":
                                    last = mm(b[0:64, c0:c0 + 64], kdec[:, d, h, :], SA[:, d, h, :], True, True)
                                else:
                                    hs = slice(64 * h, 64 * h + 64)
                                    mm(b[0:64, c0:c0 + 64], SA[:, d, h, :], Bf[:, d, hs], True, False)
                                    last = mm(b[0:64, c0:c0 + 64], z[:, g, Z_V + 64 * h:Z_V + 64 * h + 64],
                                              Kf[:, d, hs], False, True)
                        last.then_inc(filled, 1)

                pe.wait_ge(mixed, l * 2 + 2)
                for g in range(2):
                    for n in range(2):
                        b = tile(l, ("mixT", g, n))
                        for k in range(4):
                            c0 = [(0, 128, 256, 384), (Z_G, Z_G + 128, Z_R, Z_R + 128)][n][k]
                            last = pe.transpose(b[:, 128 * k:128 * k + 128], z[:, g, c0:c0 + 128], ident)
                        last.then_inc(filled, 1)
                need(l, ("mixT", 1, 1))
                for n in range(2):
                    w = v3(piece(i)[:, :], KD)
                    for g in range(2):
                        b = tile(l, ("out", n, g))
                        for k in range(KD):
                            last = mm(b, hT[:, k, 128 * g:128 * g + 128], w[:, k, :], k == 0, k == KD - 1)
                        last.then_inc(filled, 1)
                    i += 1

                to_columns("h2", 3)
                need(l, ("h2", 1, 1))
                w = v3(piece(i)[:, 0:KD * EXPERTS], KD)
                for g in range(2):
                    b = tile(l, ("route", g))
                    for k in range(KD):
                        last = mm(b[:, 0:EXPERTS], hT[:, k, 128 * g:128 * g + 128], w[:, k, :], k == 0, k == KD - 1)
                    last.then_inc(filled, 1)
                i += 1
                for g in range(2):
                    for n in range(2):
                        bk = tile(l, ("rows", g, n))
                        for k in range(4):
                            last = pe.transpose(bk[:, 128 * k:128 * k + 128],
                                                hT[:, 4 * n + k, 128 * g:128 * g + 128], ident)
                        last.then_inc(filled, 1)
                bk = tile(l, ("pos",))
                need(l, ("route", 1))
                need(l, ("rows", 1, 1))
                w = v3(piece(i)[:, :], KD)
                sh_banks = [n for n in range(8) if n != tiles.index[("pos",)] % 8]
                gub, tb = sh_banks[4:6], sh_banks[6]
                for g in range(2):
                    for k in range(KD):
                        last = mm(P[:, gub[g], :], hT[:, k, 128 * g:128 * g + 128], w[:, k, :], k == 0, k == KD - 1)
                    last.then_inc(sh_full, 1)
                pe.wait_ge(chosen_ready, l + 1)
                mm(bk[:, 0:64], cst("strict0"), chosen[:, 0, :], True, True)
                mm(bk[:, 64:128], cst("ones"), chosen[:, 0, :], True, False)
                mm(bk[:, 64:128], cst("strict0"), chosen[:, 1, :], False, True)
                mm(bk[:, 128:192], cst("ones"), chosen[:, 0, :], True, False)
                mm(bk[:, 128:192], cst("ones"), chosen[:, 1, :], False, True).then_inc(filled, 1)
                assert order[0] == tiles.total
                pe.wait_ge(down_in[3], l * (16 + PASSES * DOWN_PASS) + 16)
                for g in range(2):
                    pe.wait_ge(sh_act, l * 2 + (g + 1))
                    if g:
                        pe.wait_ge(sh_ready, l * 2 + 1)
                    for f in range(2):
                        last = pe.transpose(P[:, tb, 128 * f:128 * f + 128], act_[g][:, 128 * f:128 * f + 128], ident)
                    last.then_inc(sh_turn, 1)
                    pe.wait_ge(sh_ready, l * 2 + (g + 1))
                    for n in range(2):
                        for f in range(2):
                            last = mm(P[:, sh_banks[2 * g + n], :], actT[g][:, f, :],
                                      down[3][:, f, 512 * n:512 * n + 512], f == 0, f == 1)
                last.then_inc(sh_y, 1)
                need(l, ("pos",))
                pe.wait_ge(x_shared, l + 1)

                pe.wait_ge(most_ready, l + 1)
                pe.nop().then_inc(own_step, 1)
                most_here = pe.value_load(most[0:1, 0:1], min_val=0, max_val=2 * T)
                ran = pe.value_load(most[0:1, 1:2], min_val=0, max_val=LAYERS * PASSES)
                with pe.Fori(0, PASSES) as b:
                    with pe.If(b * CAP < most_here):
                        q = l * PASSES + b
                        base = q * EXPERTS
                        for n in range(16):
                            eb, g = divmod(n, 2)
                            pe.wait_ge(sel_ready, q * 16 + (n + 1))
                            for j in range(8):
                                e = 8 * eb + j
                                last = pe.matmul(P[0:CAP, 6, 2 * e:2 * e + 2], onehot[n % 2][:, j, :], token[:, g, :],
                                                 start=n == 0 and j == 0, stop=n == 15 and j == 7,
                                                 skip_group_check=True)
                            last.then_inc(sel_used, 1)

                        def turn_x(e, s):
                            pe.wait_ge(gx_in[s % 2], (ran + b) * (8 * EXPERTS) + (e + (2 - s % 2)) * 8)
                            pe.nop().then_inc(narrow_turns, 1)
                            for k in range(KD):
                                last = pe.transpose(P[:, k // 4, 128 * (k % 4):128 * (k % 4) + CAP],
                                                    xg[s % 2][0:CAP, 128 * k:128 * k + 128], ident[0:CAP, 0:CAP])
                            last.then_inc(xT_full, 1)

                        def turn_act(e, s):
                            pe.wait_ge(act_done, base + e + (1 + A0))
                            pe.nop().then_inc(narrow_turns, 1)
                            for f in range(2):
                                last = pe.transpose(P[:, 6 + s % 2, 128 * f:128 * f + CAP],
                                                    act_[s % 2][0:CAP, 128 * f:128 * f + 128], ident[0:CAP, 0:CAP])
                            last.then_inc(t_full, 1)

                        def down_proj(e, s):
                            pe.wait_ge(down_in[s], (l * PASSES + b) * DOWN_PASS + (e + (4 - s)) * 4
                                       + (l * 16 + 16 if s == 3 else 0))
                            pe.wait_ge(t_ready, base + e + 1)
                            for eng in "AV":
                                pe.wait_ge(y_out_e[eng], base + e + Y0)
                            for n in range(2):
                                for f in range(2):
                                    last = mm(P[0:CAP, 2 + n, :], aeT[s % 2][:, f, :],
                                              down[s][:, f, 512 * n:512 * n + 512], f == 0, f == 1)
                            last.then_inc(y_full, 1)

                        def block(eb, first=False, final=False):
                            for s in range(SLOTS):
                                e = eb * SLOTS + s
                                pe.wait_ge(ring_in[s], l * RING_LAYER + b * (16 * EXPERTS // SLOTS) + (e + (4 - s)) * 4
                                           + 16 * len(PIECES) // SLOTS)
                                for eng in "AV":
                                    pe.wait_ge(xT[eng], base + e + 1)
                                pe.wait_ge(act_done, base + e + 1)
                                w = v3(ring[s][:, :], KD)

                                def gate_up(k0, k1):
                                    for k in range(k0, k1):
                                        last = pe.matmul(P[0:CAP, 4 + s % 2, :], xeT[s % 2][:, k, :], w[:, k, :],
                                                         start=k == 0, stop=k == KD - 1, skip_group_check=True)
                                    return last

                                gate_up(0, 4)
                                before = not (first and s == 0)
                                if before:
                                    turn_act(e - 1, (s + 3) % SLOTS)
                                if not (final and s == SLOTS - 1):
                                    turn_x(e + 1, (s + 1) % SLOTS)
                                gate_up(4, KD).then_inc(g_full, 1)
                                if before:
                                    down_proj(e - 1, (s + 3) % SLOTS)

                        turn_x(0, 0)
                        block(0, first=True)
                        with pe.Fori(1, EXPERTS // SLOTS - 1) as eb:
                            block(eb)
                        block(EXPERTS // SLOTS - 1, final=True)
                        turn_act(EXPERTS - 1, 3)
                        down_proj(EXPERTS - 1, 3)
                        for eng in "AV":
                            pe.wait_ge(y_out_e[eng], base + EXPERTS + Y0)
                            pe.nop().then_inc(own_step, 1)
                    with pe.Else():
                        pe.nop().then_inc(sel_used, 16)
                        for sm_ in (xT_full, g_full, t_full, y_full):
                            pe.nop().then_inc(sm_, EXPERTS)

        @block.scalar
        def _(act):
            def row(ap, l):
                return ap[bass.ds(l, 1), :].partition_broadcast(128)

            def f(l, name):
                act.wait_ge(filled, tiles.filled(l, name))
                return P[:, tiles.index[name] % 8, :]

            def done(ins, name):
                i = tiles.index[name]
                assert tiles.who[name] == "A" and tiles.rank[name] == cnt[0] + 1, name
                cnt[0] += 1
                ins.then_inc(empty["A"], 1)

            cnt = [0]
            act.nop().then_inc(y_out_e["A"], Y0)
            act.dma_start(crow[0:1, :], a["c_ctx"].rearrange("(a n) -> a n", a=1)).then_inc(c_in, 16)
            act.dma_start(crow[1:2, :], a["c"]).then_inc(c_in, 16)
            act.wait_ge(c_in, 32)
            act.activation(crow, crow, ACT.Silu).then_inc(cT_ready, 1)
            act.wait_ge(cT_ready, 2)
            act.activation(sm["cT"], P[:, 0, 0:16], ACT.Copy).then_inc(cT_ready, 1)

            with act.Fori(0, LAYERS) as l:
                cnt[0] = 0
                act.wait_ge(x_done, l + 1)
                act.wait_ge(cT_ready, 3)
                act.dma_start(ada_b, a["ada_b"][bass.ds(l, 1), :].partition_broadcast(2)).then_inc(adab_in, 16)
                for w, name in enumerate(("norm1", "norm2")):
                    act.dma_start(nrows[:, w, :], a[name][bass.ds(l, 1), :].rearrange("a (k n) -> (a k) n", k=8)
                                  ).then_inc(adab_in, 16)
                for name in small:
                    act.dma_start(small[name], row(small_src[name], l)).then_inc(small_in, 16)
                conv = a["gdn_conv"]
                for j, (tap, mu) in enumerate(((0, "rwkv_mu_prev"), (2, "rwkv_mu_next"))):
                    act.dma_start(mix3[:, j, 0:768], conv[bass.ds(l, 1), tap, :].partition_broadcast(128)
                                  ).then_inc(mix_in, 16)
                    act.dma_start(mix3[:, j, 768:1920], row(a[mu], l)).then_inc(mix_in, 16)
                act.dma_start(mix3[:, 2, 0:768], conv[bass.ds(l, 1), 1, :].partition_broadcast(128)
                              ).then_inc(mix_in, 16)

                def norm(which, n):
                    for g in range(2):
                        ins = act.activation(W1[:, 6144:7168] if which == 0 else PR[:, 0:D], x[:, g, :], ACT.Square,
                                             accum_out=sm["ss"][:, g:g + 1])
                        act.drain()
                        act.nop().then_inc(ss_ready, 1)
                    act.wait_ge(ss_eps, n)
                    act.activation(sm["rs"][:, 0:2], sm["ss"][:, 2:4], ACT.Ln)
                    act.drain()
                    act.activation(sm["rs"][:, 2:4], sm["rs"][:, 0:2], ACT.Exp, scale=-0.5).then_inc(rs_ready, 1)

                norm(0, l * 2 + 1)
                for w in range(2):
                    for g in range(2):
                        for n in range(2):
                            name = ("gate", w, g, n)
                            done(act.activation(gateB[:, w, g, 512 * n:512 * n + 512], f(l, name), ACT.Copy), name)
                for c in range(ZC):
                    for g in range(2):
                        name = ("z", c, g)
                        done(act.activation(z[:, g, 512 * c:512 * c + ZW[c]], f(l, name)[:, 0:ZW[c]], ACT.Copy), name)
                act.dma_start(ckvn[:, 1, :], a["cache_mla_ckv"][0, bass.ds(l, 1), :, :].rearrange("a t c -> (a t) c")
                              ).then_inc(ctx_in, 16)
                act.dma_start(kpe[:, 1, :], a["cache_mla_kpe"][0, bass.ds(l, 1), :, :].rearrange("a t c -> (a t) c")
                              ).then_inc(ctx_in, 16)
                for g in range(2):
                    act.activation(cqn[:, g, :], z[:, g, 0:QL], ACT.Square, accum_out=sm["ss"][:, 4 * g:4 * g + 1])
                    act.drain()
                    act.activation(ckvn[:, 2 * g, :], z[:, g, QL:QL + KVL], ACT.Square,
                                   accum_out=sm["ss"][:, 4 * g + 1:4 * g + 2])
                    act.drain()
                act.nop().then_inc(gates_a, 1)
                for g in range(2):
                    for c in range(5):
                        act.wait_ge(conv_done, l * 10 + (5 * g + c + 1))
                        c0 = SHIFTED[c]
                        if c < 2:
                            act.activation(z[:, g, c0:c0 + CONV], z[:, g, c0:c0 + CONV], ACT.Silu)
                        if c == 4:
                            act.activation(z[:, g, Z_WD:Z_WD + 128], z[:, g, Z_WD:Z_WD + 128], ACT.Tanh)
                            act.activation(z[:, g, Z_GD:Z_GD + 128], z[:, g, Z_GD:Z_GD + 128], ACT.Sigmoid)
                    act.activation(z[:, g, Z_GATE:Z_GATE + 256], z[:, g, Z_GATE:Z_GATE + 256], ACT.Silu
                                   ).then_inc(silu_done, 1)
                act.wait_ge(gates_v, l * 4 + 1)
                act.activation(beta, z[:, :, Z_AB + 8:Z_AB + 16].rearrange("p g (d h) -> p d g h", d=2), ACT.Sigmoid)
                act.activation(sm["nalog"], small["a_log"], ACT.Exp)
                act.activation(sm["t16"], sm["t16"], ACT.Exp)
                act.drain()
                act.activation(sm["t16"], sm["t16"], ACT.Ln, bias=1.0).then_inc(gates_a, 1)
                act.wait_ge(gates_v, l * 4 + 2)
                act.activation(sm["rs"][:, 0:4], sm["st8"][:, 0:4], ACT.Ln)
                act.activation(sm["nqk"], sm["nqk"], ACT.Ln)
                act.drain()
                act.activation(sm["rs"][:, 0:4], sm["rs"][:, 0:4], ACT.Exp, scale=-0.5)
                act.activation(sm["nqk"], sm["nqk"], ACT.Exp, scale=-0.5).then_inc(gates_a, 1)

                act.wait_ge(ckv_ready, l * 3 + 3)
                act.dma_start(new_ckv[0, bass.ds(l, 1), :, :].rearrange("a t c -> (a t) c"), ckvn[:, 0, :]
                              ).then_inc(ckv_out, 16)
                act.dma_start(new_kpe[0, bass.ds(l, 1), :, :].rearrange("a t c -> (a t) c"), kpe[:, 0, :]
                              ).then_inc(ckv_out, 16)
                for g in range(2):
                    name = ("cqT", g)
                    done(act.activation(cqT[:, :, 128 * g:128 * g + 128], v3(f(l, name)[:, 0:384], 3), ACT.Copy), name)
                for blk in range(3):
                    name = ("ckvT", blk)
                    b = f(l, name)
                    act.activation(ckvT[:, :, 128 * blk:128 * blk + 128], v3(b[:, 0:256], 2), ACT.Copy)
                    done(act.activation(kpeT[:, 128 * blk:128 * blk + 128], b[0:64, 256:384], ACT.Copy), name)
                for hp in range(2):
                    name = ("qT", hp)
                    done(act.activation(qT[:, 2 * hp:2 * hp + 2, :, :].rearrange("p h g t -> p (h g t)"), f(l, name),
                                        ACT.Copy), name)
                for g in range(2):
                    name = ("qpeT", g)
                    done(act.activation(qpeT[:, g, :, :].rearrange("p h t -> p (h t)"), f(l, name)[0:64, :],
                                        ACT.Copy), name)
                for h in range(HEADS):
                    name = ("kT", h)
                    done(act.activation(kT[:, h, :], f(l, name)[:, 0:384], ACT.Copy), name)
                act.wait_ge(ckv_out, l * 32 + 32)
                for g in range(2):
                    nk = 1 + g
                    for h in range(HEADS):
                        name = ("score", g, h)
                        act.wait_ge(nmax, l * 8 + (4 * g + h + 1))
                        ins = act.activation(prob[h % 2][:, 0:128 * nk], f(l, name)[:, 0:128 * nk], ACT.Exp,
                                             bias=sm["mx"][:, h:h + 1], scale=MLA_SCALE,
                                             accum_out=sm["sum"][:, h:h + 1])
                        done(ins, name)
                        act.drain()
                        act.nop().then_inc(prob_ready, 1)

                def ainv(pi, p):
                    for d in range(2):
                        name = ("T1", p, d)
                        done(act.activation(Tm[:, d, :, :].rearrange("p h n -> p (h n)"), f(l, name), ACT.Copy), name)
                    for k in range(1, LEVELS):
                        for d in range(2):
                            name = ("X", p, k, d)
                            done(act.activation(XX[:, d, :, :].rearrange("p h n -> p (h n)"), f(l, name), ACT.Copy),
                                 name)

                for pi, p in enumerate(PAIRS):
                    kind, g = p
                    if kind == "gdn":
                        for s in range(2):
                            name = ("qkT", g, s)
                            done(act.activation(qkT[:, s, :, :].rearrange("p h t -> p (h t)"), f(l, name)[0:64, :],
                                                ACT.Copy), name)
                        if g == 0:
                            act.wait_ge(gates_v, l * 4 + 4)
                            act.wait_ge(empty["V"], tiles.emptied(l, ("decay",)))
                            act.activation(sm["egs"], sm["gcs"], ACT.Exp)
                            act.drain()
                            act.nop().then_inc(dec_a, 1)
                        for d in range(2):
                            act.wait_ge(dec_v, l * 4 + (2 * g + d + 1))
                            act.activation(PB[:, d, :, :], PB[:, d, :, :], ACT.Exp, scale=-1.0).then_inc(dec_a, 1)
                        ainv(pi, p)
                        act.wait_ge(fin_v, l * 6 + (3 + g))
                        act.activation(sm["nqk"][:, 0:4], sm["nqk"][:, 0:4], ACT.Ln)
                        act.drain()
                        act.activation(sm["nqk"][:, 0:4], sm["nqk"][:, 0:4], ACT.Exp, scale=-0.5).then_inc(fin_a, 1)
                        if g == 0:
                            act.wait_ge(state_ready, l * 2 + 1)
                            act.dma_start(new_gdn[0, bass.ds(l, 1), :, :, :, :].rearrange("a d h k v -> k (a d h) v"),
                                          v3(sout, 8)).then_inc(state_out, 16)
                            act.dma_start(v3(nat["w2"][0:64, :], 8),
                                          a["state_gdn"][0, bass.ds(l, 1), :, :, :, :].rearrange("a d h k v -> k (a d h) v")
                                          ).then_inc(state_in, 16)
                    else:
                        act.wait_ge(pair_done, l * 4 + pi)
                        if g == 1:
                            act.wait_ge(state_ready, l * 2 + 2)
                            act.dma_start(new_rwkv[0, bass.ds(l, 1), :, :, :, :].rearrange("a d h k v -> k (a d h) v"),
                                          v3(sout, 8)).then_inc(state_out, 16)
                            act.wait_ge(state_out, l * 32 + 32)
                            act.dma_start(v3(nat["Bf"][0:64, :], 8),
                                          a["state_rwkv"][0, bass.ds(l, 1), :, :, :, :].rearrange("a d h k v -> k (a d h) v")
                                          ).then_inc(state_in, 16)
                        else:
                            act.wait_ge(state_out, l * 32 + 16)
                        act.dma_start(w2, a["rwkv_w2"][bass.ds(l, 1), :, :, :].rearrange("a d r c -> r (a d) c")
                                      ).then_inc(lora_in, 16)
                        act.dma_start(a2, a["rwkv_a2"][bass.ds(l, 1), :, :, :].rearrange("a d r c -> r (a d) c")
                                      ).then_inc(lora_in, 16)
                        act.dma_start(nat["g2"], a["rwkv_g2"][bass.ds(l, 1), :, :].rearrange("a r c -> (a r) c")
                                      ).then_inc(lora_in, 16)
                        name = ("wdT", g)
                        done(act.activation(nat["wdT"][0:64, :], f(l, name)[0:64, :], ACT.Copy), name)
                        name = ("gdT", g)
                        done(act.activation(nat["gdT"], f(l, name)[:, 0:128], ACT.Copy), name)
                        act.wait_ge(rw_v, l * 6 + (3 * g + 1))
                        act.activation(nat["lw"], nat["lw"], ACT.Sigmoid)
                        act.activation(nat["a"], nat["a"], ACT.Sigmoid).then_inc(rw_a, 1)
                        name = ("rgate", g)
                        done(act.activation(nat["gate"], f(l, name)[:, 0:256], ACT.Copy), name)
                        act.wait_ge(rw_v, l * 6 + (3 * g + 2))
                        act.activation(sm["nqk"][:, 0:4], sm["nqk"][:, 0:4], ACT.Ln)
                        act.drain()
                        act.activation(sm["nqk"][:, 0:4], sm["nqk"][:, 0:4], ACT.Exp, scale=-0.5)
                        name = ("cum", g)
                        b = f(l, name)
                        act.wait_ge(rw_v, l * 6 + (3 * g + 3))
                        act.activation(E[:, :, :].rearrange("p d n -> p (d n)"), b, ACT.Exp)
                        act.activation(Ex[:, :, :].rearrange("p d n -> p (d n)"),
                                       Ex[:, :, :].rearrange("p d n -> p (d n)"), ACT.Exp)
                        done(act.activation(Ei[:, :, :].rearrange("p d n -> p (d n)"), b, ACT.Exp, scale=-1.0), name)
                        if g == 0:
                            name = ("suf", g)
                            done(act.activation(Fs[:, :, :].rearrange("p d n -> p (d n)"), f(l, name), ACT.Exp), name)
                        act.drain()
                        act.nop().then_inc(rw_a, 1)
                        for d in range(2):
                            for s in ("KTt", "RT", "BT", "KhT"):
                                name = (s, g, d)
                                b = v3(f(l, name)[0:64, :], HEADS)
                                dst = {"KTt": KRT[:, d, :, 0, :], "RT": KRT[:, d, :, 1, :], "BT": BT[:, d, :, :],
                                       "KhT": KTh[:, d, :, :]}[s]
                                done(act.activation(dst, b, ACT.Copy), name)
                        if g:
                            name = ("cc", g)
                            done(act.activation(sm["ecc"][0:64, :], f(l, name)[0:64, 0:8], ACT.Exp), name)
                            name = ("RS", g)
                            done(act.activation(oacc, f(l, name)[:, 0:256], ACT.Copy), name)
                        name = ("R", g)
                        done(act.activation(nat["R"], f(l, name), ACT.Copy, scale=-1.0), name)
                        ainv(pi, p)
                        act.wait_ge(fin_v, l * 6 + (5 + g))
                        act.activation(sm["nqk"][:, 0:4], sm["nqk"][:, 0:4], ACT.Ln)
                        act.drain()
                        act.activation(sm["nqk"][:, 0:4], sm["nqk"][:, 0:4], ACT.Exp, scale=-0.5).then_inc(fin_a, 1)

                for g in range(2):
                    for n in range(2):
                        name = ("mixT", g, n)
                        done(act.activation(hT[:, 4 * n:4 * n + 4, 128 * g:128 * g + 128], v3(f(l, name), 4), ACT.Copy),
                             name)
                act.wait_ge(empty["V"], tiles.emptied(l, ("out", 1, 1)))
                norm(1, l * 2 + 2)
                for g in range(2):
                    act.wait_ge(logit_v, l * 4 + (2 * g + 1))
                    act.activation(sm["scores"], sm["scores"], ACT.Sigmoid).then_inc(logit_a, 1)
                for g in range(2):
                    for n in range(2):
                        name = ("rows", g, n)
                        done(act.activation(rows[:, g, 512 * n:512 * n + 512], f(l, name), ACT.Copy), name)
                act.wait_ge(empty["A"], tiles.emptied(l, ("rows", 1, 1)))
                for g in range(2):
                    act.dma_start(h_rows[T * g:T * g + T, :], rows[:, g, :]).then_inc(rows_out, 16)
                assert cnt[0] == tiles.per["A"]
                sh_banks = [n for n in range(8) if n != tiles.index[("pos",)] % 8]
                gub, tb = sh_banks[4:6], sh_banks[6]
                for g in range(2):
                    act.wait_ge(sh_full, l * 2 + (g + 1))
                    act.activation(sg[g], P[:, gub[g], 0:FF], ACT.Silu).then_inc(sh_silu, 1)
                for g in range(2):
                    act.wait_ge(sh_turn, l * 2 + (g + 1))
                    act.activation(actT[g][:, :, :].rearrange("p f t -> p (f t)"), P[:, tb, 0:256], ACT.Copy
                                   ).then_inc(sh_ready, 1)

                act.wait_ge(most_ready, l + 1)
                act.nop().then_inc(own_step, 1)
                most_here = act.value_load(most[0:1, 0:1], min_val=0, max_val=2 * T)
                ran = act.value_load(most[0:1, 1:2], min_val=0, max_val=LAYERS * PASSES)
                with act.Fori(0, PASSES) as b:
                    with act.If(b * CAP < most_here):
                        q = l * PASSES + b
                        base = q * EXPERTS

                        def x_half(e, s):
                            act.wait_ge(xT_full, base + e + 1)
                            act.activation(xeT[s % 2][:, 0:4, :], v3(P[:, 0, :], 4)[:, :, 0:CAP], ACT.Copy
                                           ).then_inc(xT["A"], 1)

                        def turned(e, s):
                            act.wait_ge(t_full, base + e + 1)
                            act.activation(aeT[s % 2][:, :, :], v3(P[:, 6 + s % 2, 0:256], 2)[:, :, 0:CAP],
                                           ACT.Copy).then_inc(t_ready, 1)

                        def y_half(e, s, start=False):
                            if not start:
                                act.wait_ge(stored[s % 2], (ran + b) * (8 * EXPERTS) + (e - s % 2) * 8)
                            act.wait_ge(y_full, base + e + (1 + G0))
                            act.activation(yo[s % 2][0:CAP, 0:512], P[0:CAP, 2, :], ACT.Copy).then_inc(y_out_e["A"], 1)
                            for eng in "AV":
                                act.wait_ge(y_out_e[eng], base + e + (1 + Y0))
                                act.nop().then_inc(own_step, 1)
                            act.dma_start(y_rows[bass.ds(e * CAP, CAP), :], yo[s % 2][0:CAP, :]
                                          ).then_inc(stored[s % 2], 16)

                        def block(eb, first=False, final=False):
                            for s in range(SLOTS):
                                e = eb * SLOTS + s
                                before = not (first and s == 0)
                                if before:
                                    turned(e - 1, (s + 3) % SLOTS)
                                if not (final and s == SLOTS - 1):
                                    x_half(e + 1, (s + 1) % SLOTS)
                                act.wait_ge(g_full, base + e + (1 + G0))
                                act.activation(sg[s % 2][0:CAP, :], P[0:CAP, 4 + s % 2, 0:FF], ACT.Silu).then_inc(silu_e, 1)
                                if before:
                                    y_half(e - 1, (s + 3) % SLOTS, start=first and s <= 2)

                        x_half(0, 0)
                        block(0, first=True)
                        with act.Fori(1, EXPERTS // SLOTS - 1) as eb:
                            block(eb)
                        block(EXPERTS // SLOTS - 1, final=True)
                        turned(EXPERTS - 1, 3)
                        y_half(EXPERTS - 1, 3)
                    with act.Else():
                        act.drain()
                        for sm_ in (xT["A"], silu_e, t_ready, y_out_e["A"]):
                            act.nop().then_inc(sm_, EXPERTS)

            act.wait_ge(x_done, LAYERS + 1)
            for g in range(2):
                act.activation(PR[:, 0:D], x[:, g, :], ACT.Square, accum_out=sm["ss"][:, g:g + 1])
                act.drain()
                act.nop().then_inc(ss_ready, 1)
            act.wait_ge(ss_eps, 2 * LAYERS + 1)
            act.activation(sm["rs"][:, 0:2], sm["ss"][:, 2:4], ACT.Ln)
            act.drain()
            act.activation(sm["rs"][:, 2:4], sm["rs"][:, 0:2], ACT.Exp, scale=-0.5).then_inc(rs_ready, 1)

        @block.vector
        def _(dve):
            def f(l, name):
                dve.wait_ge(filled, tiles.filled(l, name))
                return P[:, tiles.index[name] % 8, :]

            def done(ins, name):
                i = tiles.index[name]
                assert tiles.who[name] == "V" and tiles.rank[name] == cnt[0] + 1, name
                cnt[0] += 1
                ins.then_inc(empty["V"], 1)

            def tt(out, p, q, op):
                return dve.tensor_tensor(out, p, q, op)

            cnt = [0]
            dve.memset(sm["ran"], 0.0)
            dve.nop().then_inc(sum_used, 1)
            dve.wait_ge(x_in, 32)
            dve.wait_ge(const_in, 16)
            dve.tensor_copy(token[:, :, :].rearrange("p g c -> p (g c)"), cst("token"))
            dve.nop().then_inc(x_done, 1)
            dve.nop().then_inc(act_done, A0)
            dve.nop().then_inc(y_out_e["V"], Y0)

            def norm(n):
                dve.wait_ge(ss_ready, n * 2 + 2)
                dve.tensor_scalar(sm["ss"][:, 2:4], sm["ss"][:, 0:2], 1.0 / D, EPS, ALU.mult, ALU.add
                                  ).then_inc(ss_eps, 1)
                dve.wait_ge(rs_ready, n + 1)

            with dve.Fori(0, LAYERS) as l:
                cnt[0] = 0

                def normalise(n, which):
                    norm(n)
                    for g in range(2):
                        dve.tensor_scalar((xs, xs1)[which == 0][:, g, :], x[:, g, :], sm["rs"][:, 2 + g:3 + g], None,
                                          ALU.mult).then_inc(xn_ready, 1)
                    for g in range(2):
                        for h in range(2):
                            name = (f"h{which + 1}", g, h)
                            b = f(l, name)
                            for k in range(4):
                                kk = 4 * h + k
                                last = dve.tensor_scalar(hT[:, kk, 128 * g:128 * g + 128], b[:, 128 * k:128 * k + 128],
                                                         modT[:, 2 * which + 1, kk, g:g + 1],
                                                         modT[:, 2 * which, kk, g:g + 1], ALU.mult, ALU.add)
                            done(last, name)

                dve.wait_ge(adab_in, l * 48 + 48)
                for n in range(12):
                    name = ("mods", n)
                    c0 = 512 * n
                    done(tt(mods[:, c0:c0 + 512], f(l, name)[0:2, :], ada_b[:, c0:c0 + 512], ALU.add), name)
                name = ("modT",)
                b = f(l, name)
                dve.tensor_copy(sm["modT"], b[:, 0:64])
                done(dve.tensor_copy(sm["nT"], b[:, 64:80]), name)
                dve.drain()
                for w in range(2):
                    s = modT[:, 2 * w + 1, :, :]
                    n3 = wide(sm["nT"][:, 8 * w:8 * w + 8], 2)
                    dve.tensor_scalar(s, s, 1.0, None, ALU.add)
                    dve.drain()
                    tt(s, s, n3, ALU.mult)
                    dve.drain()
                dve.wait_ge(mix_in, l * 80 + 80)
                c0 = mix3[:, 2, 768:1920]
                tt(c0, mix3[:, 0, 768:1920], mix3[:, 1, 768:1920], ALU.add)
                dve.drain()
                dve.tensor_scalar(c0, c0, -1.0, 1.0, ALU.mult, ALU.add).then_inc(mix_c, 1)
                normalise(l * 2, 0)

                for g in range(2):
                    for c, c0 in enumerate(SHIFTED):
                        m0 = CONV * c
                        bp, bn = f(l, ("zp", g, c)), f(l, ("zn", g, c))
                        done(tt(conv_t[0], bp[:, 0:CONV], mix3[:, 0, m0:m0 + CONV], ALU.mult), ("zp", g, c))
                        done(tt(conv_t[1], bn[:, 0:CONV], mix3[:, 1, m0:m0 + CONV], ALU.mult), ("zn", g, c))
                        dve.drain()
                        tt(conv_t[0], conv_t[0], conv_t[1], ALU.add)
                        dve.drain()
                        dve.wait_ge(z_mid, l * 10 + (5 * g + c + 1))
                        tt(z[:, g, c0:c0 + CONV], z[:, g, c0:c0 + CONV], conv_t[0], ALU.add).then_inc(conv_done, 1)
                        dve.drain()

                dve.wait_ge(small_in, l * (16 * 13) + 16 * 13)
                dve.wait_ge(gates_a, l * 3 + 1)
                dtb = small["dt"].rearrange("p (d a h) -> p d a h", d=2, a=1).to_broadcast([128, 2, 2, 4])
                tt(gg, z[:, :, Z_AB:Z_AB + 8].rearrange("p g (d h) -> p d g h", d=2), dtb, ALU.add)
                dve.drain()
                dve.scalar_tensor_tensor(out=sm["t16"], in0=sm["gg"], scalar=-1.0, in1=sm["gg"], op0=ALU.mult,
                                         op1=ALU.min).then_inc(gates_v, 1)
                for g in range(2):
                    dve.tensor_scalar(sm["st8"][:, 2 * g:2 * g + 1], sm["ss"][:, 4 * g:4 * g + 1], 1.0 / QL, EPS,
                                      ALU.mult, ALU.add)
                    dve.tensor_scalar(sm["st8"][:, 2 * g + 1:2 * g + 2], sm["ss"][:, 4 * g + 1:4 * g + 2], 1.0 / KVL,
                                      EPS, ALU.mult, ALU.add)
                dve.wait_ge(silu_done, l * 2 + 2)
                for g in range(2):
                    qk = z[:, g, Z_G:Z_G + 512]
                    tt(sq, qk, qk, ALU.mult)
                    dve.drain()
                    dve.tensor_reduce(sm["nqk"][:, 8 * g:8 * g + 8], v3(sq, 8), AX, ALU.add)
                    dve.drain()
                dve.tensor_scalar(sm["nqk"], sm["nqk"], EPS, None, ALU.add).then_inc(gates_v, 1)
                dve.wait_ge(gates_a, l * 3 + 2)
                dve.scalar_tensor_tensor(out=sm["gg"], in0=sm["gg"], scalar=0.0, in1=sm["t16"], op0=ALU.max,
                                         op1=ALU.add)
                dve.tensor_scalar(sm["nalog"], sm["nalog"], -1.0, None, ALU.mult)
                dve.drain()
                nal = sm["nalog"].rearrange("p (d a h) -> p d a h", d=2, a=1).to_broadcast([128, 2, 2, 4])
                tt(gg, gg, nal, ALU.mult).then_inc(gates_v, 1)
                dve.wait_ge(gates_a, l * 3 + 3)
                for g in range(2):
                    dve.scalar_tensor_tensor(out=cqn[:, g, :], in0=z[:, g, 0:QL], scalar=sm["rs"][:, 2 * g:2 * g + 1],
                                             in1=small["q_norm"], op0=ALU.mult, op1=ALU.mult).then_inc(cq_ready, 1)
                for blk, g in ((0, 0), (1, None), (2, 1)):
                    if g is None:
                        dve.wait_ge(ctx_in, l * 32 + 32)
                        dve.nop().then_inc(ckv_ready, 1)
                        continue
                    kp = z[:, g, QL + KVL:P_MLA]
                    if g == 0:
                        dve.tensor_copy(kpe[:, 0, :], kp)
                    else:
                        q4 = kp.rearrange("p (a s n) -> p a s n", a=2, s=2)
                        r4 = rt[:, 0, 0:64].rearrange("p (a s n) -> p a s n", a=2, s=2)
                        s4 = cst("sin").rearrange("p (a s n) -> p a s n", a=2, s=2)
                        for s in range(2):
                            tt(r4[:, :, s, :], q4[:, :, 1 - s, :], s4[:, :, s, :], ALU.mult)
                        tt(kpe[:, 2, :], kp, cst("cos"), ALU.mult)
                        dve.drain()
                        tt(kpe[:, 2, :], kpe[:, 2, :], rt[:, 0, 0:64], ALU.add)
                    dve.scalar_tensor_tensor(out=ckvn[:, blk, :], in0=z[:, g, QL:QL + KVL],
                                             scalar=sm["rs"][:, 2 * g + 1:2 * g + 2], in1=small["kv_norm"],
                                             op0=ALU.mult, op1=ALU.mult).then_inc(ckv_ready, 1)
                for g in range(2):
                    dve.tensor_scalar(sm["nqk"][:, 8 * g:8 * g + 4], sm["nqk"][:, 8 * g:8 * g + 4], N ** -0.5, None,
                                      ALU.mult)
                dve.drain()
                for g in range(2):
                    qk = v3(z[:, g, Z_G:Z_G + 512], 8)
                    tt(qk, qk, wide(sm["nqk"][:, 8 * g:8 * g + 8], 64), ALU.mult).then_inc(fin_v, 1)
                dve.nop().then_inc(gates_v, 1)
                name = ("decay",)
                done(dve.tensor_copy(sm["gcs"], f(l, name)[:, 0:32]), name)

                for g in range(2):
                    name = ("qpe", g)
                    b = f(l, name)
                    if g == 0:
                        ins = dve.tensor_copy(qpe[:, 0, :], b[:, 0:256])
                        done(ins, name)
                        dve.drain()
                        dve.nop().then_inc(qpe_ready, 1)
                    else:
                        dve.tensor_copy(rt[:, 1, 0:256], b[:, 0:256])
                        dve.drain()
                        src = rt[:, 1, 0:256].rearrange("p (h a s n) -> p (h a) s n", h=4, a=2, s=2)
                        dst = rt[:, 0, 0:256].rearrange("p (h a s n) -> p (h a) s n", h=4, a=2, s=2)
                        s4 = cst("sin").rearrange("p (x a s n) -> p x a s n", x=1, a=2, s=2)
                        for h in range(HEADS):
                            for s in range(2):
                                tt(dst[:, 2 * h:2 * h + 2, s, :], src[:, 2 * h:2 * h + 2, 1 - s, :],
                                   cst("sin").rearrange("p (a s n) -> p a s n", a=2, s=2)[:, :, s, :], ALU.mult)
                        tt(v3(qpe[:, 1, :], 4), v3(rt[:, 1, 0:256], 4), many(cst("cos"), 4), ALU.mult)
                        dve.drain()
                        tt(qpe[:, 1, :], qpe[:, 1, :], rt[:, 0, 0:256], ALU.add).then_inc(qpe_ready, 1)
                        done(dve.nop(), name)
                for blk in range(3):
                    name = ("v", blk)
                    done(dve.tensor_copy(vv[:, blk, :], f(l, name)), name)
                for g in range(2):
                    nk = 1 + g
                    for h in range(HEADS):
                        b = f(l, ("score", g, h))
                        dve.tensor_reduce(sm["st8"][:, h:h + 1], b[:, 0:128 * nk], AX, ALU.max)
                        dve.drain()
                        dve.tensor_scalar(sm["mx"][:, h:h + 1], sm["st8"][:, h:h + 1], -MLA_SCALE, None, ALU.mult
                                          ).then_inc(nmax, 1)
                        name = ("pT", g, h)
                        done(dve.tensor_copy(pT[h % 2][:, 0:nk, :].rearrange("p k t -> p (k t)"),
                                             f(l, name)[:, 0:128 * nk]), name)
                        dve.wait_ge(prob_ready, l * 8 + (4 * g + h + 1))
                        dve.reciprocal(sm["st8"][:, 4:5], sm["sum"][:, h:h + 1])
                        dve.drain()
                        name = ("mla", g, h)
                        done(dve.tensor_scalar(z[:, g, 128 * h:128 * h + 128], f(l, name)[:, 0:128], sm["st8"][:, 4:5],
                                               None, ALU.mult), name)
                        dve.drain()

                def solve(pi, p):
                    dve.wait_ge(lm_ready, l * 4 * LEVELS + (pi * LEVELS + 1))
                    for d in range(2):
                        last = tt(TT[:, d, :, :], many(ident, HEADS), Lm[0][:, d, :, :], ALU.subtract)
                    last.then_inc(tt_ready, 1)
                    for k in range(1, LEVELS):
                        for d in range(2):
                            if k < LEVELS - 1:
                                name = ("Y", p, k, d)
                                if d == 0:
                                    dve.drain()
                                b = v3(f(l, name), HEADS)
                                done(tt(Tm[:, d, :, :], Tm[:, d, :, :], b, ALU.subtract), name)
                            elif d == 0:
                                dve.drain()
                            name = ("YT", p, k, d)
                            b = v3(f(l, name), HEADS)
                            done(tt(TT[:, d, :, :], TT[:, d, :, :], b, ALU.subtract), name)

                for pi, p in enumerate(PAIRS):
                    kind, g = p
                    if kind == "gdn":
                        if g == 0:
                            dve.wait_ge(filled, tiles.filled(l, ("mla", 1, 3)))
                        for d in range(2):
                            for h in range(HEADS):
                                last = dve.tensor_scalar(gtri[:, d, h, :], cst(f"tri{d}"), gg[:, d, g, h:h + 1], None,
                                                         ALU.mult)
                        last.then_inc(gtri_ready, 1)
                        for d in range(2):
                            name = ("row", g, d)
                            b = f(l, name)
                            for h in range(HEADS):
                                last = dve.tensor_scalar(PB[:, d, h, :], b[:, 128 * h:128 * h + 128],
                                                         gc[:, d, g, h:h + 1], -1.0, ALU.subtract, ALU.mult)
                            done(last, name)
                            dve.drain()
                            dve.tensor_scalar(PB[:, d, :, :], PB[:, d, :, :], 0.0, None, ALU.max).then_inc(dec_v, 1)
                        for d in range(2):
                            dve.wait_ge(dec_a, l * 5 + (2 + 2 * g + d))
                            tt(PB[:, d, :, :], PB[:, d, :, :], many(cst(f"tri{d}"), HEADS), ALU.mult)
                        dve.drain()
                        b = f(l, ("kk", g))
                        for d in range(2):
                            for h in range(HEADS):
                                last = dve.scalar_tensor_tensor(out=AT[:, d, h, :], in0=b[:, 128 * h:128 * h + 128],
                                                                scalar=beta[:, d, g, h:h + 1], in1=PB[:, d, h, :],
                                                                op0=ALU.mult, op1=ALU.mult)
                        done(last, ("kk", g))
                        b = v3(f(l, ("qk", g)), HEADS)
                        for d in range(2):
                            last = tt(PK[:, d, :, :], b, PB[:, d, :, :], ALU.mult)
                        done(last, ("qk", g))
                        dve.drain()
                        dve.nop().then_inc(at_ready, 1)
                        vg = v3(z[:, g, Z_G + 512:Z_G + 768], HEADS)
                        if g == 0:
                            for d in range(2):
                                last = dve.tensor_copy(R[:, d, :, :], vg)
                            last.then_inc(rhs_ready, 1)
                            kg = v3(z[:, g, Z_G + 256:Z_G + 512], HEADS)
                            for d in range(2):
                                last = tt(kdec[:, d, :, :], kg, wide(egs[:, d, g, :], 64), ALU.mult)
                            last.then_inc(kdec_ready, 1)
                        else:
                            b = u4(f(l, ("kS", g)))
                            for d in range(2):
                                last = tt(R[:, d, :, :], b[:, d, :, :], wide(egc[:, d, g, :], 64), ALU.mult)
                            done(last, ("kS", g))
                            dve.drain()
                            for d in range(2):
                                last = tt(R[:, d, :, :], vg, R[:, d, :, :], ALU.subtract)
                            last.then_inc(rhs_ready, 1)
                            b = u4(f(l, ("qS", g)))
                            tt(v3(oacc, HEADS), b[:, 0, :, :], wide(egc[:, 0, g, :], 64), ALU.mult)
                            done(tt(v3(sq[:, 0:256], HEADS), b[:, 1, :, :], wide(egc[:, 1, g, :], 64), ALU.mult),
                                 ("qS", g))
                            dve.drain()
                            tt(oacc, oacc, sq[:, 0:256], ALU.add)
                            dve.drain()
                        solve(pi, p)
                        b = u4(f(l, ("W", p)))
                        for d in range(2):
                            last = tt(SA[:, d, :, :], b[:, d, :, :], wide(beta[:, d, g, :], 64), ALU.mult)
                        done(last, ("W", p))
                        b = f(l, ("O", p))
                        if g:
                            ins = tt(oacc, b[:, 0:256], oacc, ALU.add)
                        else:
                            ins = dve.tensor_copy(oacc, b[:, 0:256])
                        done(ins, ("O", p))
                        dve.drain()
                        tt(sq[:, 0:256], oacc, oacc, ALU.mult)
                        dve.drain()
                        dve.tensor_reduce(sm["st8"][:, 0:4], v3(sq[:, 0:256], HEADS), AX, ALU.add)
                        dve.drain()
                        dve.tensor_scalar(sm["nqk"][:, 0:4], sm["st8"][:, 0:4], 1.0 / N, EPS, ALU.mult, ALU.add
                                          ).then_inc(fin_v, 1)
                        tt(v3(sq[:, 0:256], HEADS), v3(z[:, g, Z_GATE:Z_GATE + 256], HEADS),
                           many(small["gdn_norm"], HEADS), ALU.mult)
                        dve.drain()
                        tt(oacc, oacc, sq[:, 0:256], ALU.mult)
                        dve.drain()
                        dve.wait_ge(fin_a, l * 4 + (pi + 1))
                        tt(v3(z[:, g, Z_G:Z_G + 256], HEADS), v3(oacc, HEADS), wide(sm["nqk"][:, 0:4], 64), ALU.mult)
                        if g == 0:
                            name = ("S", p)
                            done(dve.tensor_copy(sout, f(l, name)[0:64, :]), name)
                            dve.drain()
                            dve.nop().then_inc(state_ready, 1)
                        dve.drain()
                        dve.nop().then_inc(pair_done, 1)
                        continue

                    r, k_, v_ = (z[:, g, c0:c0 + 256] for c0 in (Z_R, Z_K, Z_V))

                    name = ("wpre", g)
                    done(tt(nat["lw"], f(l, name), small["w0"], ALU.add), name)
                    name = ("apre", g)
                    done(tt(nat["a"], f(l, name), small["a0"], ALU.add), name)
                    dve.drain()
                    dve.nop().then_inc(rw_v, 1)
                    kk = nat["kk"]
                    tt(kk, k_, small["k_k"], ALU.mult)
                    dve.drain()
                    tt(sq[:, 0:256], kk, kk, ALU.mult)
                    dve.drain()
                    dve.tensor_reduce(sm["st8"][:, 0:4], v3(sq[:, 0:256], HEADS), AX, ALU.add)
                    dve.drain()
                    dve.tensor_scalar(sm["nqk"][:, 0:4], sm["st8"][:, 0:4], EPS, None, ALU.add).then_inc(rw_v, 1)
                    dve.wait_ge(rw_a, l * 4 + (2 * g + 1))
                    dve.tensor_scalar(nat["lw"], nat["lw"], -float(np.exp(-0.5)), None, ALU.mult).then_inc(rwp, 1)
                    ka = many(small["k_a"], 2)
                    dve.scalar_tensor_tensor(out=kd, in0=aa, scalar=-1.0, in1=ka, op0=ALU.add, op1=ALU.mult)
                    dve.drain()
                    tt(kd, kd, many(k_, 2), ALU.mult)
                    dve.drain()
                    tt(kd, kd, many(k_, 2), ALU.add)
                    b = v3(f(l, ("cum", g)), 2)
                    tt(Ex, b, lw, ALU.subtract)
                    dve.drain()
                    dve.nop().then_inc(rw_v, 1)
                    dve.wait_ge(rw_a, l * 4 + (2 * g + 2))
                    tt(v3(kk, HEADS), v3(kk, HEADS), wide(sm["nqk"][:, 0:4], 64), ALU.mult)
                    dve.drain()
                    tt(aa, aa, many(kk, 2), ALU.mult)
                    dve.drain()
                    tt(Rt, many(r, 2), E, ALU.mult)
                    tt(Ktl, many(kk, 2), Ex, ALU.mult)
                    tt(Bh, aa, Ei, ALU.mult)
                    tt(Kh, kd, Ei, ALU.mult).then_inc(rwp, 1)
                    if g == 0:
                        tt(Bf, aa, Fs, ALU.mult)
                        tt(Kf, kd, Fs, ALU.mult)
                    tt(sq[:, 256:512], r, small["r_k"], ALU.mult)
                    tt(sq[:, 0:256], kd[:, 0, :], kd[:, 1, :], ALU.add)
                    dve.drain()
                    tt(sq[:, 0:256], sq[:, 0:256], sq[:, 256:512], ALU.mult)
                    dve.drain()
                    dve.tensor_reduce(sm["st8"][:, 8:12], v3(sq[:, 0:256], HEADS), AX, ALU.add)
                    dve.drain()
                    for d in range(2):
                        for hp in range(2):
                            for s, (low, high) in (("PB", (AT, PB)), ("PK", (MT, PK))):
                                name = (s, g, d, hp)
                                b = f(l, name).rearrange("p (h s t) -> p h s t", h=2, s=2)
                                hs = slice(2 * hp, 2 * hp + 2)
                                tt(low[:, d, hs, :], b[:, :, 0, :], many(cst(f"strict{d}"), 2), ALU.mult)
                                done(tt(high[:, d, hs, :], b[:, :, 1, :], many(cst(f"tri{d}"), 2), ALU.mult), name)
                    dve.drain()
                    dve.nop().then_inc(at_ready, 1)
                    if g:
                        name = ("S0T", g)
                        b = f(l, name)
                        dve.wait_ge(empty["A"], tiles.emptied(l, ("cc", g)))
                        done(tt(v3(nat["Kf"][0:64, :], 8), v3(b[0:64, :], 8), wide(sm["ecc"][0:64, :], 64), ALU.mult),
                             name)
                    solve(pi, p)
                    name = ("W", p)
                    done(dve.tensor_copy(nat["SA"], f(l, name)), name)
                    b = f(l, ("O", p))
                    if g:
                        ins = tt(oacc, b[:, 0:256], oacc, ALU.add)
                    else:
                        ins = dve.tensor_copy(oacc, b[:, 0:256])
                    done(ins, ("O", p))
                    dve.drain()
                    o4 = v3(oacc, HEADS)
                    dve.tensor_reduce(sm["st8"][:, 0:4], o4, AX, ALU.add)
                    dve.drain()
                    dve.tensor_scalar(sm["st8"][:, 0:4], sm["st8"][:, 0:4], 1.0 / N, None, ALU.mult)
                    dve.drain()
                    tt(o4, o4, wide(sm["st8"][:, 0:4], 64), ALU.subtract)
                    dve.drain()
                    tt(sq[:, 0:256], oacc, oacc, ALU.mult)
                    dve.drain()
                    dve.tensor_reduce(sm["st8"][:, 4:8], v3(sq[:, 0:256], HEADS), AX, ALU.add)
                    dve.drain()
                    dve.tensor_scalar(sm["nqk"][:, 0:4], sm["st8"][:, 4:8], 1.0 / N, GN_EPS, ALU.mult, ALU.add
                                      ).then_inc(fin_v, 1)
                    tt(v3(sq[:, 0:256], HEADS), v3(v_, HEADS), wide(sm["st8"][:, 8:12], 64), ALU.mult)
                    dve.drain()
                    tt(sq[:, 0:256], sq[:, 0:256], small["gn_b"], ALU.add)
                    tt(oacc, oacc, small["gn_w"], ALU.mult)
                    dve.drain()
                    dve.wait_ge(fin_a, l * 4 + (pi + 1))
                    tt(o4, o4, wide(sm["nqk"][:, 0:4], 64), ALU.mult)
                    dve.drain()
                    tt(oacc, oacc, sq[:, 0:256], ALU.add)
                    dve.drain()
                    ins = tt(r, oacc, nat["gate"], ALU.mult)
                    if g == 0:
                        name = ("S", p)
                        done(dve.tensor_copy(sout, f(l, name)[0:64, :]), name)
                        dve.drain()
                        dve.nop().then_inc(state_ready, 1)
                    dve.drain()
                    dve.nop().then_inc(mixed, 1)
                    dve.nop().then_inc(pair_done, 1)

                for n in range(2):
                    for g in range(2):
                        name = ("out", n, g)
                        cols = slice(512 * n, 512 * n + 512)
                        tt(xs[:, g, cols], f(l, name), gateB[:, 0, g, cols], ALU.mult)
                        dve.drain()
                        done(tt(x[:, g, cols], x[:, g, cols], xs[:, g, cols], ALU.add), name)
                        dve.drain()
                normalise(l * 2 + 1, 1)

                for g in range(2):
                    name = ("route", g)
                    done(dve.tensor_copy(sm["scores"], f(l, name)[:, 0:EXPERTS]), name)
                    dve.drain()
                    dve.nop().then_inc(logit_v, 1)
                    dve.wait_ge(logit_a, l * 2 + (g + 1))
                    sel, w64, st = sm["sel"], sm["w64"], sm["st8"]
                    tt(sel, sm["scores"], small["bias"], ALU.add)
                    dve.drain()
                    for q in range(8):
                        dve.max(w64[:, 8 * q:8 * q + 8], sel[:, 8 * q:8 * q + 8])
                    dve.drain()
                    top = v3(w64, 8)
                    grp = st[:, 0:8]
                    tt(grp.rearrange("p (k a) -> p k a", a=1), top[:, :, 0:1], top[:, :, 1:2], ALU.add)
                    dve.drain()
                    tt(v3(w64, 8), many(grp, 8), wide(grp, 8), ALU.is_equal)
                    tt(v3(PR[:, 0:64], 8), many(grp, 8), wide(grp, 8), ALU.is_gt)
                    dve.drain()
                    tt(w64, w64, cst("before"), ALU.mult)
                    dve.drain()
                    tt(w64, w64, PR[:, 0:64], ALU.add)
                    dve.drain()
                    dve.tensor_reduce(st[:, 8:16], v3(w64, 8), AX, ALU.add)
                    dve.drain()
                    dve.tensor_scalar(st[:, 8:16], st[:, 8:16], 4.0, -BIG, ALU.is_ge, ALU.mult)
                    dve.drain()
                    tt(v3(sel, 8), v3(sel, 8), wide(st[:, 8:16], 8), ALU.add)
                    dve.drain()
                    dve.max(st[:, 16:24], sel)
                    dve.drain()
                    dve.match_replace(out=w64, in_to_replace=st[:, 16:24], in_values=sel, imm_value=-3 * BIG)
                    dve.drain()
                    tt(chosen[:, g, :], w64, sel, ALU.not_equal)
                    dve.drain()
                    tt(w64, chosen[:, g, :], sm["scores"], ALU.mult)
                    dve.drain()
                    dve.tensor_reduce(st[:, 0:1], w64, AX, ALU.add)
                    dve.drain()
                    dve.reciprocal(st[:, 1:2], st[:, 0:1])
                    dve.drain()
                    dve.tensor_scalar(comb[:, g, :], w64, st[:, 1:2], ROUTE_SCALE, ALU.mult, ALU.mult
                                      ).then_inc(logit_v, 1)
                    dve.drain()

                dve.nop().then_inc(chosen_ready, 1)
                sh_banks = [n for n in range(8) if n != tiles.index[("pos",)] % 8]
                for g in range(2):
                    dve.wait_ge(sh_silu, l * 2 + (g + 1))
                    tt(act_[g], P[:, sh_banks[4 + g], FF:2 * FF], sg[g], ALU.mult).then_inc(sh_act, 1)
                name = ("pos",)
                bk = f(l, name)
                dve.tensor_copy(moe["pos"], bk[:, 0:128])
                done(dve.tensor_reduce(sm["st8"][:, 0:1], bk[:, 128:192], AX, ALU.max), name)
                assert cnt[0] == tiles.per["V"]
                dve.drain()
                dve.tensor_copy(most[:, 0:1], sm["st8"][:, 0:1])
                dve.tensor_copy(most[:, 1:2], sm["ran"])
                dve.drain()
                for b in range(PASSES):
                    dve.scalar_tensor_tensor(out=sm["ran"], in0=sm["st8"][:, 0:1], scalar=float(b * CAP), in1=sm["ran"],
                                             op0=ALU.is_gt, op1=ALU.add)
                    dve.drain()
                dve.nop().then_inc(most_ready, 1)
                dve.scalar_tensor_tensor(out=moe["pos"], in0=moe["pos"], scalar=1.0, in1=moe["chosen"], op0=ALU.add,
                                         op1=ALU.mult)
                dve.drain()
                dve.tensor_scalar(moe["pos"], moe["pos"], float(CAP - 1), None, ALU.add)
                src, dst = chosen, v3(moe["ra"], 2)
                spare, spare2 = v3(moe["rb"], 2), v3(moe["in"], 2)
                rix, rw = (moe[n].rearrange("p (r g) -> p r g", g=2) for n in ("rix", "rw"))
                for k in range(6):
                    step = 1 << k
                    tt(dst[:, :, step:], src[:, :, step:], src[:, :, 0:EXPERTS - step], ALU.add)
                    dve.tensor_copy(dst[:, :, 0:step], src[:, :, 0:step])
                    dve.drain()
                    src, dst = dst, (spare if k == 0 else src)
                tt(dst, src, chosen, ALU.mult)
                dve.drain()
                dve.wait_ge(sh_y, l + 1)
                for g in range(2):
                    for n in range(2):
                        cols = slice(512 * n, 512 * n + 512)
                        tt(xs[:, g, cols], P[:, sh_banks[2 * g + n], :], gateB[:, 1, g, cols], ALU.mult)
                dve.drain()
                tt(x[:, :, :], x[:, :, :], xs, ALU.add).then_inc(x_shared, 1)
                dve.drain()

                most_here = dve.value_load(most[0:1, 0:1], min_val=0, max_val=2 * T)
                ran = dve.value_load(most[0:1, 1:2], min_val=0, max_val=LAYERS * PASSES)
                with dve.Fori(0, PASSES) as b:
                    with dve.If(b * CAP < most_here):
                        q = l * PASSES + b
                        base = q * EXPERTS
                        dve.wait_ge(pass_stored, ran + b + 1)
                        dve.tensor_scalar(moe["pos"], moe["pos"], -float(CAP), None, ALU.add)
                        dve.drain()
                        for n in range(16):
                            eb, g = divmod(n, 2)
                            dve.wait_ge(sel_used, q * 16 + (n + 1))
                            tt(onehot[n % 2], many(cst("iota")[:, 0:CAP], 8), wide(pos[:, g, 8 * eb:8 * eb + 8], CAP),
                               ALU.is_equal).then_inc(sel_ready, 1)
                        dve.wait_ge(sel_used, q * 16 + 18)
                        dve.tensor_copy(moe["iw"][0:CAP, :], P[0:CAP, 6, 0:2 * EXPERTS])
                        dve.drain()
                        col = iw[0:CAP, :, 0:1]
                        tt(col, col, iw[0:CAP, :, 1:2], ALU.add)
                        dve.drain()
                        t64 = moe["cnt"].rearrange("p (e a) -> p e a", a=1)[0:CAP, :, :]
                        dve.tensor_scalar(t64, col, 0.0, NOWHERE, ALU.is_equal, ALU.mult)
                        dve.drain()
                        dve.scalar_tensor_tensor(out=idt[0:CAP, :, 0:1], in0=t64, scalar=-1.0, in1=col, op0=ALU.add,
                                                 op1=ALU.add)
                        dve.drain()
                        for i in range(2):
                            dve.tensor_copy(gidx[i][0:CAP, :], IDT[0:CAP, i:i + 1])
                        dve.drain()
                        dve.nop().then_inc(idx_ready, 1)
                        tt(v3(moe["row"], 2), pos, many(cst("first_row"), 2), ALU.add)
                        dve.tensor_scalar(moe["in"], moe["pos"], float(CAP), None, ALU.is_lt)
                        dve.drain()
                        dve.scalar_tensor_tensor(out=moe["in"], in0=moe["pos"], scalar=0.0, in1=moe["in"],
                                                 op0=ALU.is_ge, op1=ALU.mult)
                        dve.drain()
                        tt(moe["row"], moe["row"], moe["in"], ALU.mult)
                        tt(moe["cw"], sm["comb"], moe["in"], ALU.mult)
                        dve.drain()
                        for r in range(TOP_K):
                            for table, found, by_rank in ((moe["row"], spare, rix), (moe["cw"], spare2, rw)):
                                dve.scalar_tensor_tensor(out=found, in0=dst, scalar=float(r + 1), in1=v3(table, 2),
                                                         op0=ALU.is_equal, op1=ALU.mult)
                            dve.drain()
                            dve.tensor_reduce(rix[:, r, :], spare, AX, ALU.add)
                            dve.tensor_reduce(rw[:, r, :], spare2, AX, ALU.add)
                            dve.drain()
                        dve.tensor_scalar(moe["none"], moe["rix"], 0.0, NOWHERE, ALU.is_equal, ALU.mult)
                        dve.drain()
                        dve.scalar_tensor_tensor(out=RIX[:, :], in0=moe["none"], scalar=-1.0, in1=moe["rix"],
                                                 op0=ALU.add, op1=ALU.add).then_inc(rix_ready, 1)
                        dve.drain()

                        def x_half(e, s, more=True):
                            dve.wait_ge(xT_full, base + e + 1)
                            if more:
                                dve.tensor_copy(gidx[s % 2][0:CAP, :],
                                                idt[0:CAP, bass.ds(e + 2, 1), 0:1].rearrange("p e c -> p (e c)"))
                            dve.tensor_copy(xeT[s % 2][:, 4:8, :], v3(P[:, 1, :], 4)[:, :, 0:CAP]
                                            ).then_inc(xT["V"], 1)

                        def y_half(e, s, start=False):
                            if not start:
                                dve.wait_ge(stored[s % 2], (ran + b) * (8 * EXPERTS) + (e - s % 2) * 8)
                            dve.wait_ge(y_full, base + e + (1 + G0))
                            dve.tensor_copy(yo[s % 2][0:CAP, 512:1024], P[0:CAP, 3, :]).then_inc(y_out_e["V"], 1)

                        def block(eb, first=False, final=False):
                            for s in range(SLOTS):
                                e = eb * SLOTS + s
                                if not (final and s == SLOTS - 1):
                                    x_half(e + 1, (s + 1) % SLOTS, more=not (final and s > 0))
                                dve.wait_ge(silu_e, base + e + 1)
                                tt(act_[s % 2][0:CAP, :], P[0:CAP, 4 + s % 2, FF:2 * FF], sg[s % 2][0:CAP, :], ALU.mult
                                   ).then_inc(act_done, 1)
                                if not (first and s == 0):
                                    y_half(e - 1, (s + 3) % SLOTS, start=first and s <= 2)

                        x_half(0, 0)
                        block(0, first=True)
                        with dve.Fori(1, EXPERTS // SLOTS - 1) as eb:
                            block(eb)
                        block(EXPERTS // SLOTS - 1, final=True)
                        y_half(EXPERTS - 1, 3)
                        for r in range(TOP_K):
                            part = v3(W1[:, 2048 * (r % 4):2048 * (r % 4) + 2048], 2)
                            dve.wait_ge(sum_in[r % 4], (ran + b) * 64 + 32 * (r // 4 + 1))
                            for g in range(2):
                                if r == 0:
                                    last = dve.tensor_scalar(v3(acc, 2)[:, g, :], part[:, g, :], rw[:, r, g:g + 1], None,
                                                             ALU.mult)
                                else:
                                    last = dve.scalar_tensor_tensor(out=v3(acc, 2)[:, g, :], in0=part[:, g, :],
                                                                    scalar=rw[:, r, g:g + 1], in1=v3(acc, 2)[:, g, :],
                                                                    op0=ALU.mult, op1=ALU.add)
                            last.then_inc(sum_used, 1)
                            dve.drain()
                        for g in range(2):
                            tt(xs[:, g, :], v3(acc, 2)[:, g, :], gateB[:, 1, g, :], ALU.mult)
                        dve.drain()
                        tt(x[:, :, :], x[:, :, :], xs, ALU.add)
                    with dve.Else():
                        dve.drain()
                        dve.nop().then_inc(rix_ready, 1)
                        dve.nop().then_inc(sel_ready, 16)
                        dve.nop().then_inc(idx_ready, 1)
                        for sm_ in (xT["V"], act_done, y_out_e["V"]):
                            dve.nop().then_inc(sm_, EXPERTS)
                dve.drain()
                dve.nop().then_inc(x_done, 1)

            norm(2 * LAYERS)
            dve.wait_ge(normf_in, 16)
            for g in range(2):
                dve.scalar_tensor_tensor(out=xo[:, g, :], in0=x[:, g, :], scalar=sm["rs"][:, 2 + g:3 + g], in1=normf,
                                         op0=ALU.mult, op1=ALU.mult).then_inc(y_ready, 1)

        @block.gpsimd
        def _(pool):
            pool.wait_ge(const_in, 16)
            pool.nop().then_inc(pass_stored, 1)
            with pool.Fori(0, LAYERS) as l:
                pool.wait_ge(mix_c, l + 1)
                for g in range(2):
                    for c, c0 in enumerate(SHIFTED):
                        pool.wait_ge(filled, tiles.filled(l, ("zn", g, c)))
                        zc = z[:, g, c0:c0 + CONV]
                        pool.tensor_tensor(zc, zc, mix3[:, 2, CONV * c:CONV * c + CONV], ALU.mult).then_inc(z_mid, 1)
                for pi, p in enumerate(PAIRS):
                    for k in range(LEVELS):
                        if k == 0:
                            pool.wait_ge(at_ready, l * 4 + (pi + 1))
                            pool.wait_ge(filled, tiles.filled(l, ("kk", p[1]) if p[0] == "gdn" else ("R", p[1])))
                        elif k == 1:
                            pass
                        elif k == 2:
                            pool.wait_ge(tt_ready, l * 4 + (pi + 1))
                        else:
                            pool.wait_ge(filled, tiles.filled(l, ("X", p, k - 2, 1)))
                        for d in range(2):
                            last = pool.tensor_tensor(Lm[k % 2][:, d, :, :], AT[:, d, :, :],
                                                      many(cst(f"level{k}_{d}"), HEADS), ALU.mult)
                        last.then_inc(lm_ready, 1)

                pool.wait_ge(most_ready, l + 1)
                pool.nop().then_inc(own_step, 1)
                most_here = pool.value_load(most[0:1, 0:1], min_val=0, max_val=2 * T)
                ran = pool.value_load(most[0:1, 1:2], min_val=0, max_val=LAYERS * PASSES)
                pool.wait_ge(rows_out, l * 32 + 32)
                pool.nop().then_inc(own_step, 1)
                for i in range(2):
                    pool.memset(xg[i], 0.0)
                pool.drain()
                with pool.Fori(0, PASSES) as b:
                    with pool.If(b * CAP < most_here):
                        q = l * PASSES + b
                        base = q * EXPERTS

                        def gather(e, s):
                            pool.indirect_dma_start(xg[s % 2][0:CAP, :], None, h_rows,
                                                    bass.IndirectOffsetOnAxis(ap=gidx[s % 2][0:CAP, 0:1], axis=0),
                                                    bounds_check=2 * T - 1, oob_is_err=False).then_inc(gx_in[s % 2], 16)

                        def block(eb, first=False, final=False):
                            for s in range(SLOTS):
                                e = eb * SLOTS + s
                                if not (final and s >= 2):
                                    pool.wait_ge(xT["V"], base + e + 1)
                                    pool.nop().then_inc(own_step, 1)
                                    gather(e + 2, (s + 2) % SLOTS)

                        pool.wait_ge(idx_ready, q + 1)
                        pool.nop().then_inc(own_step, 1)
                        gather(0, 0)
                        gather(1, 1)
                        block(0, first=True)
                        with pool.Fori(1, EXPERTS // SLOTS - 1) as eb:
                            block(eb)
                        block(EXPERTS // SLOTS - 1, final=True)
                        for i in range(2):
                            pool.wait_ge(stored[i], (ran + b + 1) * (8 * EXPERTS))
                            pool.nop().then_inc(own_step, 1)
                        pool.wait_ge(rix_ready, q + 1)
                        pool.nop().then_inc(own_step, 1)
                        for r in range(TOP_K):
                            if r >= 4:
                                pool.wait_ge(sum_used, (ran + b) * TOP_K + (r - 3) + 1)
                                pool.nop().then_inc(own_step, 1)
                            for g in range(2):
                                c0 = 2048 * (r % 4) + 1024 * g
                                pool.indirect_dma_start(W1[:, c0:c0 + D], None, y_rows,
                                                        bass.IndirectOffsetOnAxis(
                                                            ap=RIX[:, 2 * r + g:2 * r + g + 1], axis=0),
                                                        bounds_check=EXPERTS * CAP - 1, oob_is_err=False
                                                        ).then_inc(sum_in[r % 4], 16)
                        pool.nop().then_inc(pass_stored, 1)


_INS = ["x_prompt", "x_sample", "cache_mla_ckv", "cache_mla_kpe", "state_gdn", "state_rwkv", "c", "c_ctx", "ada_w",
        "ada_b", "norm1", "w_in", "mla_q_norm", "mla_w_uq", "mla_kv_norm", "mla_w_ukv", "gdn_conv", "gdn_a_log",
        "gdn_dt_bias", "gdn_norm", "rwkv_mu_prev", "rwkv_mu_next", "rwkv_w0", "rwkv_w2", "rwkv_a0", "rwkv_a2",
        "rwkv_g2", "rwkv_k_k", "rwkv_k_a", "rwkv_r_k", "rwkv_gn_w", "rwkv_gn_b", "w_out", "norm2", "moe_router",
        "moe_bias", "moe_w_gu", "moe_w_down", "shared_w_gu", "shared_w_down", "norm_f"]
_OUTS = [(1, T, D), (1, T, D), (1, LAYERS, T, KVL), (1, LAYERS, T, ROPE), (1, LAYERS, 2, HEADS, N, N),
         (1, LAYERS, 2, HEADS, N, N)]


def kernel(**inputs):
    import concourse.bacc as _bacc
    from concourse.bass_utils import run_bass_kernel_spmd as _run

    nc = _bacc.Bacc("TRN2", target_bir_lowering=False, num_devices=1, dynamic_dma_scratch_size=8192)
    arrays, args = {}, {}
    for name in _INS:
        arr = np.ascontiguousarray(inputs[name])
        arrays[f"in_{name}"] = arr
        args[name] = nc.dram_tensor(f"in_{name}", arr.shape, mybir.dt.from_np(arr.dtype), kind="ExternalInput").ap()
    table = constants()
    arrays["shape_constants"] = table
    consts = nc.dram_tensor("shape_constants", table.shape, F32, kind="ExternalInput").ap()
    outs = [nc.dram_tensor(f"out_{i}", s, F32, kind="ExternalOutput").ap() for i, s in enumerate(_OUTS)]
    build(nc, args, consts, outs)
    r = _run(nc, [arrays], core_ids=[0])
    return tuple(r.results[0][f"out_{i}"] for i in range(len(_OUTS)))
```
